# Optimizing a Trainium2 kernel written in Bass

```python
import math
import jax, jax.numpy as jnp
from jax import lax
import numpy as np

D_MODEL = 1024
BATCH = 1
SEQ = 2048
DEPTH = 1
DEC_BATCH = 1
DEC_SEQ = 256
PAST_LEN = 128

D_MIX = D_MODEL
D_HYENA = D_MIX // 2
HYENA_GROUPS = 8
HYENA_ORDER = 2
SHORT_CONV = 3
FILTER_BANDS = 16
FILTER_EMB = 1 + 2 * FILTER_BANDS
FILTER_HIDDEN = 64
N_DIR = 2
DECAY_MIN = -math.log(1e-2) / 1.5
DECAY_MAX = -math.log(1e-2) / 0.3
DECAY_SHIFT = 0.05
N_HEADS = 8
QK_NOPE = 64
QK_ROPE = 32
QK_HEAD = QK_NOPE + QK_ROPE
V_HEAD = 64
D_ATTN = N_HEADS * V_HEAD
Q_LORA = 256
KV_LORA = 128
ROPE_THETA = 10000.0
Q_BLOCK = 128
N_EXPERTS = 16
EC_CAPACITY = 2
D_EXPERT = 512
EPS = 1e-6
COL_HYENA = (HYENA_ORDER + 1) * D_HYENA
COL_Q = COL_HYENA + Q_LORA
COL_KV = COL_Q + KV_LORA
D_IN = COL_KV + QK_ROPE

kernel_name = "hymba_hyena_mla_ec_encoder"

def rms_norm(x, g):
    xf = x.astype(jnp.float32)
    y = xf * lax.rsqrt(jnp.mean(xf * xf, axis=-1, keepdims=True) + EPS)
    return (y * g.astype(jnp.float32)).astype(x.dtype)

def short_conv(u, w, b):
    L = u.shape[1]
    up = jnp.pad(u, ((0, 0), (1, 1), (0, 0)))
    return up[:, :L] * w[0] + up[:, 1:L + 1] * w[1] + up[:, 2:] * w[2] + b

def hyena_filters(L, w1, b1, w2, b2, w3, freq, decay):
    f32 = jnp.float32
    t_idx = jnp.arange(L, dtype=f32)[:, None]
    t = t_idx / (L - 1)
    bands = jnp.linspace(1e-4, FILTER_BANDS - 1, FILTER_BANDS, dtype=f32)
    ang = 2.0 * math.pi * bands * t_idx / L
    feats = jnp.concatenate([t, jnp.cos(ang), -jnp.sin(ang)], axis=-1)
    fr = freq.astype(f32)
    h = jnp.sin(fr * (feats @ w1.astype(f32) + b1.astype(f32)))
    h = jnp.sin(fr * (h @ w2.astype(f32) + b2.astype(f32)))
    h = (h @ w3.astype(f32)).reshape(L, N_DIR, HYENA_ORDER, D_HYENA)
    window = jnp.exp(-t[:, :, None, None] * decay.astype(f32)) + DECAY_SHIFT
    h = h * window
    k = jnp.concatenate([h[:, 0],
                         jnp.zeros((1, HYENA_ORDER, D_HYENA), f32),
                         h[:0:-1, 1]], axis=0)
    k = k / jnp.sum(jnp.abs(k), axis=0, keepdims=True)
    return jnp.fft.rfft(k, axis=0)

def fft_conv(z, kf, bias):
    L = z.shape[1]
    zf32 = z.astype(jnp.float32)
    zf = jnp.fft.rfft(zf32, n=2 * L, axis=1)
    y = jnp.fft.irfft(zf * kf, n=2 * L, axis=1)[:, :L]
    return y + zf32 * bias.astype(jnp.float32)

def hyena_mixer(u, conv_w, conv_b, w1, b1, w2, b2, w3, freq, decay, bias):
    L = u.shape[1]
    uc = short_conv(u, conv_w, conv_b)
    v, x1, x2 = jnp.split(uc, HYENA_ORDER + 1, axis=-1)
    kf = hyena_filters(L, w1, b1, w2, b2, w3, freq, decay)
    z = x1.astype(jnp.float32) * fft_conv(v, kf[:, 0], bias[0])
    z = x2.astype(jnp.float32) * fft_conv(z, kf[:, 1], bias[1])
    return z.astype(u.dtype)

def rope(x, cos, sin):
    x1, x2 = jnp.split(x, 2, axis=-1)
    return x * cos + jnp.concatenate([-x2, x1], axis=-1) * sin

def mla_mixer(cq, ckv, krope, q_a_norm, w_uq, kv_a_norm, w_ukv, q_norm, k_norm):
    f32 = jnp.float32
    B, L, _ = cq.shape
    q = (rms_norm(cq, q_a_norm) @ w_uq).reshape(B, L, N_HEADS, QK_HEAD)
    kv = (rms_norm(ckv, kv_a_norm) @ w_ukv).reshape(B, L, N_HEADS, QK_NOPE + V_HEAD)
    k_nope, v = kv[..., :QK_NOPE], kv[..., QK_NOPE:]
    k = jnp.concatenate([k_nope, jnp.broadcast_to(krope[:, :, None, :], (B, L, N_HEADS, QK_ROPE))], axis=-1)
    q = rms_norm(q, q_norm).astype(f32)
    k = rms_norm(k, k_norm).astype(f32)
    pos = jnp.arange(L, dtype=f32)
    inv_freq = ROPE_THETA ** (-jnp.arange(0, QK_ROPE, 2, dtype=f32) / QK_ROPE)
    ang = pos[:, None] * inv_freq
    ang = jnp.concatenate([ang, ang], axis=-1)[:, None, :]
    cos, sin = jnp.cos(ang), jnp.sin(ang)
    q = jnp.concatenate([q[..., :QK_NOPE], rope(q[..., QK_NOPE:], cos, sin)], axis=-1) * (QK_HEAD ** -0.5)
    k = jnp.concatenate([k[..., :QK_NOPE], rope(k[..., QK_NOPE:], cos, sin)], axis=-1)
    v = v.astype(f32)
    qb = q.reshape(B, L // Q_BLOCK, Q_BLOCK, N_HEADS, QK_HEAD).transpose(1, 0, 2, 3, 4)

    def attend(q_blk):
        s = jnp.einsum('bqhd,bkhd->bhqk', q_blk, k)
        p = jax.nn.softmax(s, axis=-1)
        return jnp.einsum('bhqk,bkhd->bqhd', p, v)

    o = lax.map(attend, qb)
    return o.transpose(1, 0, 2, 3, 4).reshape(B, L, D_ATTN).astype(cq.dtype)

def ec_moe(x, w_router, w_gate, w_up, w_down):
    B, L, D = x.shape
    N = B * L
    cap = max(1, EC_CAPACITY * N // N_EXPERTS)
    xt = x.reshape(N, D)
    aff = jax.nn.softmax((xt @ w_router).astype(jnp.float32), axis=-1)
    gates, idx = lax.top_k(aff.T, cap)
    xs = xt[idx]
    h = jax.nn.silu(jnp.einsum('ecd,edf->ecf', xs, w_gate)) * jnp.einsum('ecd,edf->ecf', xs, w_up)
    y = jnp.einsum('ecf,efd->ecd', h, w_down) * gates[..., None].astype(x.dtype)
    out = jnp.zeros((N, D), x.dtype).at[idx.reshape(-1)].add(y.reshape(-1, D).astype(x.dtype))
    return out.reshape(B, L, D)

def setup_inputs(seed: int = 0) -> dict:
    key = jax.random.key(seed)
    ks = jax.random.split(key, 32)
    f32 = jnp.float32

    def nrm(k, shape, scale):
        return jax.random.normal(k, shape, f32) * scale

    def gain(k, shape):
        return 1.0 + 0.05 * jax.random.normal(k, shape, f32)

    return {
        "x_prompt": nrm(ks[0], (BATCH, SEQ, D_MODEL), 1.0),
        "x_sample": nrm(ks[1], (DEC_BATCH, DEC_SEQ, D_MODEL), 1.0),
        "attn_norm": gain(ks[2], (DEPTH, D_MODEL)),
        "w_in": nrm(ks[3], (DEPTH, D_MODEL, D_IN), D_MODEL ** -0.5),
        "conv_w": nrm(ks[4], (DEPTH, SHORT_CONV, COL_HYENA), SHORT_CONV ** -0.5),
        "conv_b": nrm(ks[5], (DEPTH, COL_HYENA), 0.02),
        "filt_w1": nrm(ks[6], (DEPTH, FILTER_EMB, FILTER_HIDDEN), FILTER_EMB ** -0.5),
        "filt_b1": nrm(ks[7], (DEPTH, FILTER_HIDDEN), 0.02),
        "filt_w2": nrm(ks[8], (DEPTH, FILTER_HIDDEN, FILTER_HIDDEN), FILTER_HIDDEN ** -0.5),
        "filt_b2": nrm(ks[9], (DEPTH, FILTER_HIDDEN), 0.02),
        "filt_w3": nrm(ks[10], (DEPTH, FILTER_HIDDEN, N_DIR * HYENA_ORDER * D_HYENA), FILTER_HIDDEN ** -0.5),
        "filt_freq": gain(ks[11], (DEPTH, FILTER_HIDDEN)),
        "filt_decay": jax.random.uniform(ks[12], (DEPTH, N_DIR, HYENA_ORDER, D_HYENA), f32, DECAY_MIN, DECAY_MAX),
        "hyena_bias": nrm(ks[13], (DEPTH, HYENA_ORDER, D_HYENA), 1.0),
        "q_a_norm": gain(ks[14], (DEPTH, Q_LORA)),
        "w_uq": nrm(ks[15], (DEPTH, Q_LORA, N_HEADS * QK_HEAD), Q_LORA ** -0.5),
        "kv_a_norm": gain(ks[16], (DEPTH, KV_LORA)),
        "w_ukv": nrm(ks[17], (DEPTH, KV_LORA, N_HEADS * (QK_NOPE + V_HEAD)), KV_LORA ** -0.5),
        "q_norm": gain(ks[18], (DEPTH, QK_HEAD)),
        "k_norm": gain(ks[19], (DEPTH, QK_HEAD)),
        "out_norm": gain(ks[20], (DEPTH, D_MIX)),
        "w_out": nrm(ks[21], (DEPTH, D_MIX, D_MODEL), D_MIX ** -0.5),
        "mlp_norm": gain(ks[22], (DEPTH, D_MODEL)),
        "w_router": nrm(ks[23], (DEPTH, D_MODEL, N_EXPERTS), D_MODEL ** -0.5),
        "w_gate": nrm(ks[24], (DEPTH, N_EXPERTS, D_MODEL, D_EXPERT), D_MODEL ** -0.5),
        "w_up": nrm(ks[25], (DEPTH, N_EXPERTS, D_MODEL, D_EXPERT), D_MODEL ** -0.5),
        "w_down": nrm(ks[26], (DEPTH, N_EXPERTS, D_EXPERT, D_MODEL), D_EXPERT ** -0.5),
    }

def reference(x_prompt, x_sample, attn_norm, w_in, conv_w, conv_b, filt_w1, filt_b1, filt_w2, filt_b2,
              filt_w3, filt_freq, filt_decay, hyena_bias, q_a_norm, w_uq, kv_a_norm, w_ukv, q_norm, k_norm,
              out_norm, w_out, mlp_norm, w_router, w_gate, w_up, w_down):

    def trunk(x):
        B, L, _ = x.shape
        for l in range(DEPTH):
            u = rms_norm(x, attn_norm[l]) @ w_in[l]
            y_h = hyena_mixer(u[..., :COL_HYENA], conv_w[l], conv_b[l], filt_w1[l], filt_b1[l],
                              filt_w2[l], filt_b2[l], filt_w3[l], filt_freq[l], filt_decay[l], hyena_bias[l])
            y_a = mla_mixer(u[..., COL_HYENA:COL_Q], u[..., COL_Q:COL_KV], u[..., COL_KV:],
                            q_a_norm[l], w_uq[l], kv_a_norm[l], w_ukv[l], q_norm[l], k_norm[l])
            y = jnp.concatenate([y_h, y_a], axis=-1).reshape(B, L, 2, D_MIX // 2)
            y = rms_norm(y, out_norm[l].reshape(2, D_MIX // 2)).reshape(B, L, D_MIX)
            x = x + y @ w_out[l]
            x = x + ec_moe(rms_norm(x, mlp_norm[l]), w_router[l], w_gate[l], w_up[l], w_down[l])
        return x

    y_prompt = trunk(x_prompt)
    y_sample = trunk(x_sample)
    return (y_prompt, y_sample)


_drawn_inputs = setup_inputs


def setup_inputs(seed=0):
    import zlib

    import numpy as np

    out = dict(_drawn_inputs(seed))
    spreads = {}
    factors = {'filt_b1': 8.0, 'filt_b2': 8.0, 'filt_freq': 8.0, 'filt_decay': 28.685, 'mlp_norm': 2.821}
    for name, (base, spread) in spreads.items():
        noise = np.random.default_rng([zlib.crc32(name.encode()), seed]).standard_normal(out[name].shape)
        drawn = base * np.exp(spread * noise) if base else spread * noise
        out[name] = __import__('jax').numpy.asarray(drawn.astype(out[name].dtype))
    for name, factor in factors.items():
        out[name] = (out[name] * factor).astype(out[name].dtype)
    return out
```

```python
import math
from contextlib import ExitStack

import numpy as np
import concourse.bass as bass
from concourse import mybir

F32, BF16, I32, U32 = mybir.dt.float32, mybir.dt.bfloat16, mybir.dt.int32, mybir.dt.uint32
ALU = mybir.AluOpType
ACT = mybir.ActivationFunctionType
AX = mybir.AxisListType

P = 128
D = 1024
KD = D // P
GROUPS = (2048, 256)
T = sum(GROUPS)
NT = T // P
NTP = GROUPS[0] // P
DH = 512
CH = 3 * DH
QL, KVL, RD = 256, 128, 32
CM = QL + KVL + RD
NH, ND, QH, VH = 8, 64, 96, 64
E_N, FE = 16, 512
FEAT, FH = 33, 64
N2 = 64
EPS = 1e-6
U_OFF = (1, GROUPS[0] + 3)
U_ROWS = T + 4
CAPS = tuple(2 * n // E_N for n in GROUPS)


def dft_tables(L):
    N = 2 * L
    N1, T1 = N // N2, L // N2
    J = P // T1
    q = np.arange(N1)
    k1 = np.where(q == 1, N1 // 2, q // 2)
    imag = (q > 1) & (q % 2 == 1)
    t1 = np.arange(T1)
    ang = 2 * np.pi * np.outer(t1, k1) / N1
    fwd = np.where(imag, -np.sin(ang), np.cos(ang))
    inv = fwd.T * np.where(q > 1, 2.0, 1.0)[:, None] / N
    first = np.zeros((2, J, T1, J // 2, N1))
    last = np.zeros((2, J // 2, N1, J, T1))
    for h in range(2):
        for jj in range(J // 2):
            first[h, h * (J // 2) + jj, :, jj, :] = fwd
            last[h, jj, :, h * (J // 2) + jj, :] = inv
    nb = N1 // 2 + 1
    t2 = np.arange(N2)[:, None]
    spec = np.zeros((5, nb, P, P))
    for b in range(nb):
        k = b + N1 * np.arange(N2)[None, :]
        th = 2 * np.pi * ((t2 * k) % N) / N
        c, s = np.cos(th), np.sin(th)
        re = np.concatenate([c, s], 0)
        im = np.concatenate([-s, c], 0)
        gre = np.concatenate([c.T, -s.T], 0)
        gim = np.concatenate([s.T, c.T], 0)
        if b == 0:
            re[N2:] = im[N2:] = 0
            gim[:] = 0
        if b == nb - 1:
            re[N2:], im[N2:] = re[:N2].copy(), im[:N2].copy()
            re[:N2] = im[:N2] = 0
            gim, gre = gre.copy(), np.zeros_like(gre)
        inv1 = np.concatenate([gre, gim], 1)
        spec[0, b] = np.concatenate([re, im], 1)
        spec[1, b] = inv1
        spec[2, b] = np.concatenate([inv1[N2:], inv1[:N2]], 0)
        spec[3, b] = np.concatenate([re, re], 1)
        spec[4, b] = np.concatenate([im, -im], 1)
    return (first.reshape(2, P, P).transpose(1, 0, 2), last.reshape(2, P, P).transpose(1, 0, 2), spec)


def token_order(L):
    T1 = L // N2
    J = P // T1
    i, j, t1 = np.meshgrid(np.arange(N2 // J), np.arange(J), np.arange(T1), indexing="ij")
    return (64 * t1 + i * J + j).reshape(-1)


def feature_tables(L):
    f = np.float32
    t_idx = np.arange(L, dtype=f)[:, None]
    t = t_idx / f(L - 1)
    bands = np.linspace(1e-4, 15, 16, dtype=f)
    ang = f(2.0 * math.pi) * bands * t_idx / f(L)
    feats = np.concatenate([t, np.cos(ang), -np.sin(ang)], axis=-1).astype(f)
    order = token_order(L)
    return feats[order].T, -t[order, 0].reshape(-1, P).T, (order != 0).astype(f)


def tables():
    out = {}
    pos = np.concatenate([np.arange(L, dtype=np.float32) for L in GROUPS])
    inv = np.float32(10000.0) ** (-np.arange(0, RD, 2, dtype=np.float32) / np.float32(RD))
    ang = (pos[:, None] * inv).astype(np.float32)
    out["rope"] = np.concatenate([np.cos(ang), np.cos(ang), -np.sin(ang), np.sin(ang)], 1)
    out["eye"] = np.eye(P)
    for g, L in enumerate(GROUPS):
        out[f"first{g}"], out[f"last{g}"], out[f"spec{g}"] = dft_tables(L)
        out[f"feats{g}"], out[f"negt{g}"], mask = feature_tables(L)
        out[f"mask{g}"] = np.broadcast_to(mask, (FH, L))
    return {"tab_" + k: np.ascontiguousarray(v, dtype=np.float32) for k, v in out.items()}


def in_pairs(eng, n, step):
    step(0, 0)
    step(1, 1)
    if n > 2:
        with eng.Fori(1, n // 2) as i:
            step(2 * i, 0)
            step(2 * i + 1, 1)


def early(t):
    return isinstance(t, int) and t < 2


def rows(t, n=P):
    return bass.ds(t * n, n)


def semaphores(nc, ctx, prefix):
    taken = []
    ctx.callback(nc.all_engine_barrier)
    ctx.callback(lambda: nc.clear_and_free_semaphores(taken))

    def sem(name):
        taken.append(nc.alloc_semaphore(prefix + name))
        return taken[-1]
    return sem


def project(nc, io):
    with ExitStack() as ctx:
        def sb(name, shape, dt=F32):
            return ctx.enter_context(nc.sbuf_tensor(name, shape, dt))

        sem = semaphores(nc, ctx, "")

        w = sb("pj_w", [P, KD, CH + CM])
        gain = sb("pj_gain", [P, KD])
        eye = sb("pj_eye", [P, P])
        zero = sb("pj_zero", [4, CH])
        x = sb("pj_x", [P, 2, D])
        sq = sb("pj_sq", [P, D])
        ms = sb("pj_ms", [P, 2])
        mse = sb("pj_mse", [P, 2])
        mhalf = sb("pj_mhalf", [P, 1])
        eps = sb("pj_eps", [P, 1])
        rstd = sb("pj_rstd", [P, 2])
        xn = sb("pj_xn", [P, 2, D])
        xT = [sb(f"pj_xT{b}", [P, KD, P]) for b in range(2)]
        u = sb("pj_u", [P, 2, CH + CM])
        pT = ctx.enter_context(nc.psum_tensor("pj_pT", [P, KD, P], F32))
        pU = [ctx.enter_context(nc.psum_tensor(f"pj_pU{c}", [P, 512], F32)) for c in range(4)]
        widths = [DH, DH, DH, CM]

        wts = sem("pj_wts")
        scaled = sem("pj_scaled")
        x_in = [sem(f"pj_x_in{b}") for b in range(2)]
        squared = sem("pj_squared")
        with_eps = sem("pj_with_eps")
        have_rstd = sem("pj_have_rstd")
        normed = sem("pj_normed")
        turned = sem("pj_turned")
        xT_ready = sem("pj_xT_ready")
        u_done = sem("pj_u_done")
        u_moved = sem("pj_u_moved")
        zeroed = sem("pj_zeroed")
        u_out = [sem(f"pj_u_out{b}") for b in range(2)]
        pads = sem("pj_pads")

        block = ctx.enter_context(nc.Block())

        @block.sync
        def _(sp):
            sp.dma_start(eye[:, :], io["tab_eye"]).then_inc(wts, 16)
            sp.dma_start(gain[:, :], io["attn_norm"]).then_inc(wts, 16)
            for k in range(KD):
                sp.dma_start(w[:, k, :], io["w_in"][0, k * P:(k + 1) * P, :]).then_inc(wts, 16)

            def load(t, b, src, again=False):
                if again:
                    sp.wait_ge(normed, t - 1)
                sp.dma_start(x[:, b, :], src).then_inc(x_in[b], 16)
            def store(t, b, row):
                sp.wait_ge(u_moved, 4 * t + 4)
                sp.dma_start(io["U"][bass.ds(row, P), :], u[:, b, 0:CH]).then_inc(u_out[b], 16)
                sp.dma_start(io["C"][rows(t), :], u[:, b, CH:]).then_inc(u_out[b], 16)

            for t in range(2):
                load(t, t, io["x_prompt"][0, rows(t), :])
            with sp.Fori(0, NTP // 2 - 1) as i:
                for b in range(2):
                    load(2 * i + b + 2, b, io["x_prompt"][0, rows(2 * i + b + 2), :], True)
                    store(2 * i + b, b, (2 * i + b) * P + U_OFF[0])
            for t in range(NTP - 2, NT):
                if t + 2 < NT:
                    load(t + 2, t % 2, io["x_sample"][0, rows(t + 2 - NTP), :], True)
                store(t, t % 2, t * P + U_OFF[0] if t < NTP else (t - NTP) * P + U_OFF[1])
            for b in range(2):
                sp.wait_ge(u_out[b], 16 * NT)

        @block.gpsimd
        def _(pool):
            pool.memset(zero[:, :], 0.0).then_inc(zeroed, 1)
            pool.memset(mhalf[:, :], -0.5).then_inc(zeroed, 1)
            pool.memset(eps[:, :], EPS).then_inc(zeroed, 1)
            pool.wait_ge(zeroed, 3)
            edges = [r for g, L in enumerate(GROUPS) for r in (U_OFF[g] - 1, U_OFF[g] + L)]
            for n, r in enumerate(edges):
                pool.dma_start(io["U"][r:r + 1, :], zero[n:n + 1, :]).then_inc(pads, 16)

            def root(t, b):
                pool.wait_ge(squared, t + 1)
                if not early(t):
                    pool.wait_ge(normed, t - 1)
                pool.tensor_tensor(mse[:, b:b + 1], ms[:, b:b + 1], eps[:, 0:1], ALU.add).then_inc(with_eps, 1)
                pool.wait_ge(with_eps, t + 1)
                pool.tensor_tensor(rstd[:, b:b + 1], mse[:, b:b + 1], mhalf[:, 0:1], ALU.pow).then_inc(have_rstd, 1)

            root(0, 0)
            root(1, 1)
            with pool.Fori(1, NT // 2) as i:
                root(2 * i, 0)
                root(2 * i + 1, 1)
            pool.wait_ge(pads, 64)

        @block.scalar
        def _(act):
            def step(t, b):
                act.wait_ge(x_in[b], 8 * t - 8 * b + 16)
                if not (isinstance(t, int) and t == 0):
                    act.wait_ge(squared, t)
                if not early(t):
                    act.wait_ge(have_rstd, t - 1)
                act.activation(sq[:, :], x[:, b, :], ACT.Square, scale=D ** -0.5,
                               accum_out=ms[:, b:b + 1]).then_inc(squared, 1)
                act.wait_ge(turned, t + 1)
                if not early(t):
                    act.wait_ge(u_done, 4 * t - 4)
                for h in range(2):
                    act.activation(xT[b][:, 4 * h:4 * h + 4, :], pT[:, 4 * h:4 * h + 4, :],
                                   ACT.Copy).then_inc(xT_ready, 1)
            in_pairs(act, NT, step)

        @block.tensor
        def _(pe):
            def turn(t, b):
                pe.wait_ge(normed, t + 1)
                if not (isinstance(t, int) and t == 0):
                    pe.wait_ge(xT_ready, 2 * t)
                for k in range(KD):
                    last = pe.transpose(pT[:, k, :], xn[:, b, k * P:(k + 1) * P], eye[:, :])
                last.then_inc(turned, 1)

            def products(t, b):
                pe.wait_ge(xT_ready, 2 * t + 2)
                for c in range(4):
                    if not (isinstance(t, int) and t == 0):
                        pe.wait_ge(u_moved, 4 * t - 3 + c)
                    for k in range(KD):
                        last = pe.matmul(pU[c][:, 0:widths[c]], xT[b][:, k, :],
                                         w[:, k, c * DH:c * DH + widths[c]], start=(k == 0), stop=(k == KD - 1))
                    last.then_inc(u_done, 1)

            pe.wait_ge(wts, 16 * (KD + 2))
            pe.wait_ge(scaled, KD)
            turn(0, 0)

            def step(t, b):
                turn(t + 1, 1 - b)
                products(t, b)
            step(0, 0)
            step(1, 1)
            with pe.Fori(1, NT // 2 - 1) as i:
                step(2 * i, 0)
                step(2 * i + 1, 1)
            step(NT - 2, 0)
            products(NT - 1, 1)

        @block.vector
        def _(dve):
            def norm(t, b):
                dve.wait_ge(have_rstd, t + 1)
                if not early(t):
                    dve.wait_ge(turned, t - 1)
                dve.tensor_scalar(xn[:, b, :], x[:, b, :], rstd[:, b:b + 1], None, ALU.mult).then_inc(normed, 1)

            def move(t, b):
                if not early(t):
                    dve.wait_ge(u_out[b], 16 * t - 16 * b)
                for c in range(4):
                    dve.wait_ge(u_done, 4 * t + c + 1)
                    dve.tensor_copy(u[:, b, c * DH:c * DH + widths[c]], pU[c][:, 0:widths[c]]).then_inc(u_moved, 1)

            norm(0, 0)
            dve.wait_ge(wts, 16 * (KD + 2))
            for k in range(KD):
                dve.tensor_scalar(w[:, k, :], w[:, k, :], gain[:, k:k + 1], None, ALU.mult).then_inc(scaled, 1)

            def step(t, b):
                norm(t + 1, 1 - b)
                move(t, b)
            step(0, 0)
            step(1, 1)
            with dve.Fori(1, NT // 2 - 1) as i:
                step(2 * i, 0)
                step(2 * i + 1, 1)
            step(NT - 2, 0)
            move(NT - 1, 1)


def latent(nc, io):
    H2 = 2 * NH
    with ExitStack() as ctx:
        def sb(name, shape, dt=F32):
            return ctx.enter_context(nc.sbuf_tensor(name, shape, dt))

        sem = semaphores(nc, ctx, "lt_")

        wq = sb("lt_wq", [P, 2, NH * QH])
        wkv = sb("lt_wkv", [P, NH * (ND + VH)])
        qan = sb("lt_qan", [P, 2])
        kvan = sb("lt_kvan", [P, 1])
        eye = sb("lt_eye", [P, P])
        gain = sb("lt_gain", [P, 2, QH])
        eps = sb("lt_eps", [P, H2])
        mhalf = sb("lt_mhalf", [P, H2])
        c = sb("lt_c", [P, 2, CM])
        rope = sb("lt_rope", [P, 2, 2 * RD])
        junk = sb("lt_junk", [P, QL])
        ms = sb("lt_ms", [P, 2, 2])
        mse = sb("lt_mse", [P, 2, 2])
        rc = sb("lt_rc", [P, 2, 2])
        cn = sb("lt_cn", [P, 2, QL + KVL])
        cT = [sb(f"lt_cT{b}", [P, 3, P]) for b in range(2)]
        qk = sb("lt_qk", [P, 2, H2, QH])
        sq = sb("lt_sq", [P, H2, QH])
        ss = sb("lt_ss", [P, H2])
        sse = sb("lt_sse", [P, H2])
        rh = sb("lt_rh", [P, H2])
        ra = sb("lt_ra", [P, H2, RD])
        rb = sb("lt_rb", [P, H2, RD])
        v = sb("lt_v", [P, 2, NH, VH])
        hT = sb("lt_hT", [QH, 2, H2, P])
        pT = ctx.enter_context(nc.psum_tensor("lt_pT", [P, 512], F32))
        pQ = ctx.enter_context(nc.psum_tensor("lt_pQ", [P, 1024], F32))
        pK = ctx.enter_context(nc.psum_tensor("lt_pK", [P, NH, ND + VH], F32))
        pH = [ctx.enter_context(nc.psum_tensor(f"lt_pH{b}", [P, 4, P], F32)) for b in range(2)]

        wts, scaled, consts = sem("wts"), sem("scaled"), sem("consts")
        c_in = [sem(f"c_in{b}") for b in range(2)]
        squared, with_eps, have_rc, c_normed = sem("squared"), sem("with_eps"), sem("have_rc"), sem("c_normed")
        turned, cT_ready, made = sem("turned"), sem("cT_ready"), sem("made")
        q_moved, k_moved, rope_moved, heads_sq = sem("q_moved"), sem("k_moved"), sem("rope_moved"), sem("heads_sq")
        summed, with_eps2, have_rh = sem("summed"), sem("with_eps2"), sem("have_rh")
        chain, roped = sem("chain"), sem("roped")
        heads_turned, hT_ready = sem("heads_turned"), sem("hT_ready")
        out_done = [sem(f"out_done{b}") for b in range(2)]
        WTS = 16 * 8

        block = ctx.enter_context(nc.Block())

        @block.sync
        def _(sp):
            sp.dma_start(eye[:, :], io["tab_eye"]).then_inc(wts, 16)
            sp.dma_start(qan[:, :], io["q_a_norm"]).then_inc(wts, 16)
            sp.dma_start(kvan[:, :], io["kv_a_norm"]).then_inc(wts, 16)
            sp.dma_start(gain[:, 0, :], io["q_norm"].to_broadcast([P, QH])).then_inc(wts, 16)
            sp.dma_start(gain[:, 1, :], io["k_norm"].to_broadcast([P, QH])).then_inc(wts, 16)
            sp.dma_start(wkv[:, :], io["w_ukv"][0]).then_inc(wts, 16)
            for k in range(2):
                sp.dma_start(wq[:, k, :], io["w_uq"][0, k * P:(k + 1) * P, :]).then_inc(wts, 16)

            for t in range(2):
                sp.dma_start(c[:, t, :], io["C"][rows(t), :]).then_inc(c_in[t], 16)
                sp.dma_start(rope[:, t, :], io["tab_rope"][rows(t), :]).then_inc(c_in[t], 16)

        def pipelined(eng, front, back):
            front(0, 0)
            front(1, 1)
            back(0, 0)
            with eng.Fori(1, NT // 2 - 1) as i:
                front(2 * i, 0)
                back(2 * i - 1, 1)
                front(2 * i + 1, 1)
                back(2 * i, 0)
            front(NT - 2, 0)
            back(NT - 3, 1)
            front(NT - 1, 1)
            back(NT - 2, 0)
            back(NT - 1, 1)

        @block.gpsimd
        def _(pool):
            pool.memset(eps[:, :], EPS).then_inc(consts, 1)
            pool.memset(mhalf[:, :], -0.5).then_inc(consts, 1)
            pool.wait_ge(consts, 2)

            def front(t, b):
                pool.wait_ge(squared, 2 * t + 2)
                if not early(t):
                    pool.wait_ge(c_normed, 2 * t - 2)
                pool.tensor_tensor(mse[:, b, :], ms[:, b, :], eps[:, 0:2], ALU.add).then_inc(with_eps, 1)
                pool.wait_ge(with_eps, t + 1)
                pool.tensor_tensor(rc[:, b, :], mse[:, b, :], mhalf[:, 0:2], ALU.pow).then_inc(have_rc, 1)

            def back(t, b):
                pool.wait_ge(summed, t + 1)
                pool.tensor_tensor(sse[:, :], ss[:, :], eps[:, :], ALU.add).then_inc(with_eps2, 1)
                pool.wait_ge(with_eps2, t + 1)
                if not (isinstance(t, int) and t == 0):
                    pool.wait_ge(chain, 6 * t - 5)
                pool.tensor_tensor(rh[:, :], sse[:, :], mhalf[:, :], ALU.pow).then_inc(have_rh, 1)

            pipelined(pool, front, back)

        @block.scalar
        def _(act):
            def front(t, b):
                act.wait_ge(c_in[b], 16 * t - 16 * b + 32)
                if not early(t):
                    act.wait_ge(have_rc, t - 1)
                if not (isinstance(t, int) and t == 0):
                    act.wait_ge(squared, 2 * t)
                act.activation(junk[:, :], c[:, b, 0:QL], ACT.Square, scale=QL ** -0.5,
                               accum_out=ms[:, b, 0:1]).then_inc(squared, 1)
                act.wait_ge(squared, 2 * t + 1)
                act.activation(junk[:, 0:KVL], c[:, b, QL:QL + KVL], ACT.Square, scale=KVL ** -0.5,
                               accum_out=ms[:, b, 1:2]).then_inc(squared, 1)
                act.wait_ge(turned, t + 1)
                if not early(t):
                    act.wait_ge(made, 2 * t - 2)
                act.activation(cT[b][:, :, :], pT[:, 0:3 * P].rearrange("p (k t) -> p k t", k=3),
                               ACT.Copy).then_inc(cT_ready, 1)
                act.wait_ge(made, 2 * t + 1)
                if not early(t):
                    act.wait_ge(heads_turned, 4 * t - 4)
                    act.wait_ge(out_done[b], 16 * t - 16 * b)
                act.activation(qk[:, b, 0:NH, :], pQ[:, 0:NH * QH].rearrange("p (h d) -> p h d", h=NH),
                               ACT.Copy).then_inc(q_moved, 1)
                act.wait_ge(made, 2 * t + 2)
                act.activation(qk[:, b, NH:, 0:ND], pK[:, :, 0:ND], ACT.Copy).then_inc(k_moved, 1)
                act.activation(v[:, b, :, :], pK[:, :, ND:], ACT.Copy).then_inc(k_moved, 1)
                act.wait_ge(q_moved, t + 1)
                act.wait_ge(k_moved, 2 * t + 2)
                act.wait_ge(rope_moved, t + 1)
                if not (isinstance(t, int) and t == 0):
                    act.wait_ge(summed, t)
                act.activation(sq[:, :, :], qk[:, b, :, :], ACT.Square, scale=QH ** -0.5).then_inc(heads_sq, 1)

            def back(t, b):
                if not (isinstance(t, int) and t >= NT - 2):
                    act.wait_ge(roped, t + 1)
                    ahead = bass.ds(t * P + 2 * P, P)
                    act.dma_start(c[:, b, :], io["C"][ahead, :]).then_inc(c_in[b], 16)
                    act.dma_start(rope[:, b, :], io["tab_rope"][ahead, :]).then_inc(c_in[b], 16)
                if not early(t):
                    act.wait_ge(out_done[b], 16 * t - 16 * b)
                for n in range(4):
                    act.wait_ge(heads_turned, 4 * t + n + 1)
                    act.activation(hT[:, b, 4 * n:4 * n + 4, :], pH[n % 2][0:QH, :, :], ACT.Copy).then_inc(hT_ready, 1)
                act.wait_ge(hT_ready, 4 * t + 4)
                act.dma_start(io["QK"][:, :, rows(t)].rearrange("h d t -> d h t"), hT[:, b, :, :]).then_inc(out_done[b], 16)
                act.dma_start(io["V"][rows(t), :, :], v[:, b, :, :]).then_inc(out_done[b], 16)

            pipelined(act, front, back)
            for b in range(2):
                act.wait_ge(out_done[b], 16 * NT)

        @block.tensor
        def _(pe):
            pe.wait_ge(wts, WTS)
            pe.wait_ge(scaled, 3)

            def front(t, b):
                pe.wait_ge(c_normed, 2 * t + 2)
                if not (isinstance(t, int) and t == 0):
                    pe.wait_ge(cT_ready, t)
                for k in range(3):
                    last = pe.transpose(pT[:, k * P:(k + 1) * P], cn[:, b, k * P:(k + 1) * P], eye[:, :])
                last.then_inc(turned, 1)
                pe.wait_ge(cT_ready, t + 1)
                if not (isinstance(t, int) and t == 0):
                    pe.wait_ge(q_moved, t)
                for n0, n1 in ((0, 512), (512, NH * QH)):
                    for k in range(2):
                        last = pe.matmul(pQ[:, n0:n1], cT[b][:, k, :], wq[:, k, n0:n1], start=(k == 0), stop=(k == 1))
                last.then_inc(made, 1)
                if not (isinstance(t, int) and t == 0):
                    pe.wait_ge(k_moved, 2 * t)
                for n in range(2):
                    last = pe.matmul(pK[:, 4 * n:4 * n + 4, :].rearrange("p h d -> p (h d)"), cT[b][:, 2, :],
                                     wkv[:, n * 512:(n + 1) * 512], start=True, stop=True)
                last.then_inc(made, 1)

            def back(t, b):
                pe.wait_ge(roped, t + 1)
                for n in range(4):
                    if not (isinstance(t, int) and t == 0 and n < 2):
                        pe.wait_ge(hT_ready, 4 * t + n - 1)
                    for m in range(4):
                        last = pe.transpose(pH[n % 2][0:QH, m, :], qk[:, b, 4 * n + m, :], eye[:, :])
                    last.then_inc(heads_turned, 1)

            pipelined(pe, front, back)

        @block.vector
        def _(dve):
            dve.wait_ge(wts, WTS)
            for k in range(2):
                dve.tensor_scalar(wq[:, k, :], wq[:, k, :], qan[:, k:k + 1], None, ALU.mult).then_inc(scaled, 1)
            dve.tensor_scalar(wkv[:, :], wkv[:, :], kvan[:, 0:1], None, ALU.mult).then_inc(scaled, 1)

            def front(t, b):
                dve.wait_ge(have_rc, t + 1)
                if not early(t):
                    dve.wait_ge(turned, t - 1)
                dve.tensor_scalar(cn[:, b, 0:QL], c[:, b, 0:QL], rc[:, b, 0:1], None, ALU.mult).then_inc(c_normed, 1)
                dve.tensor_scalar(cn[:, b, QL:], c[:, b, QL:QL + KVL], rc[:, b, 1:2], None, ALU.mult).then_inc(c_normed, 1)

                if not early(t):
                    dve.wait_ge(heads_turned, 4 * t - 4)
                dve.tensor_copy(qk[:, b, NH:, ND:], c[:, b, QL + KVL:].unsqueeze(1).to_broadcast([P, NH, RD])
                                ).then_inc(rope_moved, 1)

            def back(t, b):
                x = qk[:, b, :, :]
                turn = x[:, :, ND:]
                half = RD // 2
                dve.wait_ge(heads_sq, t + 1)
                if not (isinstance(t, int) and t == 0):
                    dve.wait_ge(with_eps2, t)
                dve.tensor_reduce(ss[:, :], sq[:, :, :], AX.X, ALU.add).then_inc(summed, 1)
                dve.wait_ge(have_rh, t + 1)
                dve.tensor_tensor(x, x, rh[:, :].unsqueeze(2).to_broadcast([P, H2, QH]), ALU.mult).then_inc(chain, 1)
                dve.wait_ge(chain, 6 * t + 1)
                for g in range(2):
                    dve.tensor_tensor(x[:, NH * g:NH * g + NH, :], x[:, NH * g:NH * g + NH, :],
                                      gain[:, g, :].unsqueeze(1).to_broadcast([P, NH, QH]), ALU.mult).then_inc(chain, 1)
                dve.wait_ge(chain, 6 * t + 3)
                cos, nsin, sin = (rope[:, b, n0:n1].unsqueeze(1).to_broadcast([P, H2, n1 - n0])
                                  for n0, n1 in ((0, RD), (RD, RD + half), (RD + half, 2 * RD)))
                dve.tensor_tensor(ra[:, :, :], turn, cos, ALU.mult).then_inc(chain, 1)
                dve.tensor_tensor(rb[:, :, 0:half], turn[:, :, half:], nsin, ALU.mult).then_inc(chain, 1)
                dve.tensor_tensor(rb[:, :, half:], turn[:, :, 0:half], sin, ALU.mult).then_inc(chain, 1)
                dve.wait_ge(chain, 6 * t + 6)
                dve.tensor_tensor(turn, ra[:, :, :], rb[:, :, :], ALU.add).then_inc(roped, 1)

            pipelined(dve, front, back)


def attend(nc, io):
    for g in range(2):
        attend_group(nc, io, g)


def attend_group(nc, io, g):
    L = GROUPS[g]
    g0 = sum(GROUPS[:g])
    QB = min(512, L)
    NQ, KT, QT = L // QB, L // P, L // P
    NS = NQ * KT
    MC = min(1024, L)
    MS = L // MC
    SLOTS = QT * MS
    TQ = QB // P
    slot_at = [12 + j * 3 // 2 if NS > SLOTS else 0 for j in range(SLOTS)]
    turn_at = NS - 3 if NS > SLOTS else 0
    scale = QH ** -0.5
    VW = P
    with ExitStack() as ctx:
        def sb(name, shape, dt=F32):
            return ctx.enter_context(nc.sbuf_tensor(f"at{g}_{name}", shape, dt))

        def ps(name, shape):
            return ctx.enter_context(nc.psum_tensor(f"at{g}_{name}", shape, F32))

        sem = semaphores(nc, ctx, f"at{g}_")

        eye = sb("eye", [P, P])
        q = [sb(f"q{b}", [QH + 1, L]) for b in range(2)]
        k = [sb(f"k{b}", [QH + 1, L]) for b in range(2)]
        v = [sb(f"v{b}", [P, KT, VW]) for b in range(2)]
        qh = sb("qh", [QH, L], BF16)
        kh = sb("kh", [QH, L], BF16)
        mxs = sb("mxs", [P, QT, MS])
        mx = sb("mx", [P, QT])
        nmx = sb("nmx", [QT, P])
        prob = [sb(f"prob{r}", [P, QB]) for r in range(4)]
        rec = sb("rec", [P, 2, TQ])
        o = sb("o", [P, 2, QT, VH])
        pM = [ps(f"pM{r}", [P, MC]) for r in range(2)]
        pS = [ps(f"pS{r}", [P, 512]) for r in range(2)]
        pO = [ps(f"pO{r}", [P, 512]) for r in range(2)]

        consts, ready = sem("consts"), sem("ready")
        head_in = [sem(f"head_in{b}") for b in range(2)]
        cast, slot_made, slot_max = sem("cast"), sem("slot_made"), sem("slot_max")
        max_ready, max_turned, max_moved, max_in = sem("max_ready"), sem("max_turned"), sem("max_moved"), sem("max_in")
        p_free, pS_free, o_free = sem("p_free"), sem("pS_free"), sem("o_free")
        s_made, inverted = sem("s_made"), sem("inverted")
        pM_free, o_stored = sem("pM_free"), [sem(f"o_stored{b}") for b in range(2)]

        block = ctx.enter_context(nc.Block())

        def over_heads(eng, head, peel=False):
            if peel:
                head(0, 0, True)
                head(1, 1, True)
            with eng.Fori(int(peel), NH // 2 - 1) as i:
                head(2 * i, 0, True)
                head(2 * i + 1, 1, True)
            head(NH - 2, 0, True)
            head(NH - 1, 1, False)

        def load(eng, h, b):
            eng.dma_start(q[b][0:QH, :], io["QK"][h, :, g0:g0 + L]).then_inc(head_in[b], 16)
            eng.dma_start(k[b][0:QH, :], io["QK"][h + NH, :, g0:g0 + L]).then_inc(head_in[b], 16)
            eng.dma_start(v[b][:, :, 0:VH], io["V"][g0:g0 + L, h, :].rearrange("(k p) d -> p k d", p=P)).then_inc(head_in[b], 16)

        @block.sync
        def _(sp):
            sp.dma_start(eye[:, :], io["tab_eye"]).then_inc(consts, 16)
            load(sp, 0, 0)

            def put_max(h, b):
                sp.wait_ge(max_moved, h + 1)
                sp.dma_start(q[b][QH:QH + 1, :], nmx[:, :]).then_inc(max_in, 16)
            with sp.Fori(0, NH // 2) as i:
                put_max(2 * i, 0)
                put_max(2 * i + 1, 1)
            sp.wait_ge(max_in, 16 * NH)

        @block.gpsimd
        def _(pool):
            for b in range(2):
                pool.memset(k[b][QH:QH + 1, :], 1.0).then_inc(ready, 1)
                pool.wait_ge(ready, 3 * b + 1)
                pool.memset(v[b][:, :, VH:VH + 1], 1.0).then_inc(ready, 1)
                pool.wait_ge(ready, 3 * b + 2)
                pool.memset(v[b][:, :, VH + 1:], 0.0).then_inc(ready, 1)
                pool.wait_ge(ready, 3 * b + 3)

            def store(h, b):
                pool.wait_ge(o_free, NQ * h + NQ + 2)
                pool.dma_start(io["YA"][g0:g0 + L, bass.ds(h * VH, VH)].rearrange("(k p) d -> p k d", p=P),
                               o[:, b, :, :]).then_inc(o_stored[b], 16)
            with pool.Fori(0, NH // 2) as i:
                store(2 * i, 0)
                store(2 * i + 1, 1)
            for b in range(2):
                pool.wait_ge(o_stored[b], 16 * NH // 2)

        @block.scalar
        def _(act):
            act.sem_inc(pS_free, 2)

            def head(h, b, more):
                for n in range(NS):
                    r = b * NS + n
                    act.wait_ge(s_made, NS * h + n + 1)
                    act.wait_ge(p_free, NS * h + n + 1)
                    act.activation(prob[r % 4][:, :], pS[r % 2][:, 0:QB], ACT.Exp, scale=scale).then_inc(pS_free, 1)
                    if n == min(3, NS - 1) and more:
                        act.wait_ge(p_free, NS * h + 4)
                        load(act, h + 1, 1 - b)

            over_heads(act, head)

        @block.tensor
        def _(pe):
            pe.sem_inc(p_free, 4)
            pe.wait_ge(consts, 16)
            pe.wait_ge(ready, 6)

            def slot(h, j):
                if j == 0:
                    pe.wait_ge(cast, 2 * h + 2)
                    if not (isinstance(h, int) and h == 0):
                        pe.wait_ge(max_moved, h)
                pe.wait_ge(pM_free, SLOTS * h + j + 1)
                for c in range(0, MC, 512):
                    n = min(512, MC)
                    at = (j % MS) * MC + c
                    last = pe.matmul(pM[j % 2][:, c:c + n], qh[:, (j // MS) * P:(j // MS + 1) * P], kh[:, at:at + n],
                                     start=True, stop=True)
                last.then_inc(slot_made, 1)

            def turn_max(h):
                pe.wait_ge(max_ready, h + 1)
                pe.transpose(pM[0][0:QT, 0:P], mx[:, :], eye[:, :]).then_inc(max_turned, 1)

            def scores(h, b, n):
                r = b * NS + n
                qb, kt = n // KT, n % KT
                if n == 0:
                    pe.wait_ge(head_in[b], 24 * h - 24 * b + 48)
                    pe.wait_ge(max_in, 16 * h + 16)
                pe.wait_ge(pS_free, NS * h + n + 1)
                pe.matmul(pS[r % 2][:, 0:QB], k[b][:, kt * P:(kt + 1) * P], q[b][:, qb * QB:(qb + 1) * QB],
                          start=True, stop=True).then_inc(s_made, 1)

            def values(h, b, n):
                r = b * NS + n
                qb, kt = n // KT, n % KT
                o_at = (b * NQ + qb) % 2
                pe.wait_ge(pS_free, NS * h + n + 3)
                if kt == 0:
                    pe.wait_ge(o_free, NQ * h + qb + 1)
                for t in range(TQ):
                    last = pe.matmul(pO[o_at][:, t * VW:(t + 1) * VW], prob[r % 4][:, t * P:(t + 1) * P],
                                     v[b][:, kt, :], start=(kt == 0 and t == 0), stop=(kt == KT - 1),
                                     skip_group_check=True)
                last.then_inc(p_free, 1)

            def head(h, b, more):
                for n in range(NS):
                    if n + 1 < NS:
                        scores(h, b, n + 1)
                    elif more:
                        scores(h + 1, 1 - b, 0)
                    values(h, b, n)
                    if more:
                        for j in range(SLOTS):
                            if slot_at[j] == n:
                                slot(h + 1, j)
                        if n == turn_at:
                            turn_max(h + 1)

            for j in range(SLOTS):
                slot(0, j)
            turn_max(0)
            scores(0, 0, 0)
            over_heads(pe, head)

        @block.vector
        def _(dve):
            dve.sem_inc(pM_free, 2)
            dve.sem_inc(o_free, 2)

            def casts(h, b):
                dve.wait_ge(head_in[b], 24 * h - 24 * b + 48)
                dve.tensor_copy(qh[:, :], q[b][0:QH, :]).then_inc(cast, 1)
                dve.tensor_copy(kh[:, :], k[b][0:QH, :]).then_inc(cast, 1)

            def slot(h, j):
                dve.wait_ge(slot_made, SLOTS * h + j + 1)
                ins = dve.tensor_reduce(mxs[:, j // MS, j % MS:j % MS + 1], pM[j % 2][:, :], AX.X, ALU.max)
                ins.then_inc(pM_free, 1)

            def join(h):
                dve.wait_ge(pM_free, SLOTS * h + SLOTS + 2)
                if not (isinstance(h, int) and h == 0):
                    dve.wait_ge(max_turned, h)
                dve.tensor_reduce(mx[:, :], mxs[:, :, :], AX.X, ALU.max).then_inc(max_ready, 1)
                dve.wait_ge(max_turned, h + 1)
                if not (isinstance(h, int) and h == 0):
                    dve.wait_ge(max_in, 16 * h)
                dve.tensor_scalar(nmx[:, :], pM[0][0:QT, 0:P], -1.0, None, ALU.mult).then_inc(max_moved, 1)

            def normalise(h, b, qb):
                o_at = (b * NQ + qb) % 2
                dve.wait_ge(p_free, NS * h + KT * (qb + 1) + 4)
                if qb == 0 and not early(h):
                    dve.wait_ge(o_stored[b], 8 * h - 8 * b)
                both = pO[o_at][:, 0:TQ * VW].rearrange("p (t d) -> p t d", t=TQ)
                dve.reciprocal(rec[:, o_at, :], both[:, :, VH]).then_inc(inverted, 1)
                dve.wait_ge(inverted, NQ * h + qb + 1)
                dve.tensor_tensor(o[:, b, qb * TQ:(qb + 1) * TQ, :], both[:, :, 0:VH],
                                  rec[:, o_at, :].unsqueeze(2).to_broadcast([P, TQ, VH]), ALU.mult).then_inc(o_free, 1)

            def head(h, b, more):
                if more:
                    casts(h + 1, 1 - b)
                for n in range(NS):
                    if more:
                        for j in range(SLOTS):
                            if slot_at[j] == n:
                                slot(h + 1, j)
                        if n == turn_at:
                            join(h + 1)
                    if n % KT == KT - 1:
                        normalise(h, b, n // KT)

            casts(0, 0)
            for j in range(SLOTS):
                slot(0, j)
            join(0)
            over_heads(dve, head, peel=True)


TWO_PI = (6.28125, 0.0019340515136718750, 2 * math.pi - 6.28125 - 0.0019340515136718750)
ROUND = 1.5 * 2.0 ** 23
PI_BELOW = 3.1415925


def hyena(nc, io):
    for g in range(2):
        hyena_group(nc, io, g)


def hyena_group(nc, io, g):
    L = GROUPS[g]
    T1 = L // N2
    J = P // T1
    NI = N2 // J
    N1 = 2 * T1
    with ExitStack() as ctx:
        def sb(name, shape, dt=F32):
            return ctx.enter_context(nc.sbuf_tensor(f"hy{g}_{name}", shape, dt))

        s = {"g": g, "PARTS": J if J < 16 else 1, "L": L, "T1": T1, "J": J, "NI": NI, "N1": N1,
             "h2T": sb("h2T", [FH, L]), "h2M": sb("h2M", [FH, L]),
             "acc": sb("acc", [P, 2, DH]), "rn": sb("rn", [P, DH]),
             "z": sb("z", [P, 3 * NI, DH]),
             "first": sb("first", [P, 2, P]), "last": sb("last", [P, 2, P]), "ones": sb("ones", [P, P])}
        filter_features(nc, io, s)
        short_convolution(nc, io, s)
        for order in range(2):
            filter_first_stage(nc, io, s, order)
            signal_first_stage(nc, io, s, order)
            spectrum_products(nc, io, s, order)
            last_stage(nc, io, s, order)


def stage_rows(x, N1):
    return x[0:N2 * N1, :].rearrange("(t b r) c -> b r t c", b=N1 // 2, r=2)


def token_rows(x, s):
    return x.rearrange("(t i j) c -> i j t c", i=s["NI"], j=s["J"])


def copy_parts(eng, s, tile, dram, sem, store=False):
    a, b = dram.shape[0], dram.shape[1]
    n = 1 if a >= 16 else a
    for m in range(n):
        part, whole = (tile, dram) if n == 1 else (tile[m * b:(m + 1) * b, :], dram[m])
        eng.dma_start(*((whole, part) if store else (part, whole))).then_inc(sem, 16)


def filter_features(nc, io, s):
    g, L = s["g"], s["L"]
    C = min(512, L)
    with ExitStack() as ctx:
        def sb(name, shape):
            return ctx.enter_context(nc.sbuf_tensor(f"ff{g}_{name}", shape, F32))

        sem = semaphores(nc, ctx, f"ff{g}_")

        feats = sb("feats", [FEAT, L])
        mask = sb("mask", [FH, L])
        w1, w2 = sb("w1", [FEAT, FH]), sb("w2", [FH, FH])
        b1, b2, fr = sb("b1", [FH, 1]), sb("b2", [FH, 1]), sb("fr", [FH, 1])
        arg, turns, h1 = sb("arg", [FH, L]), sb("turns", [FH, L]), sb("h1", [FH, L])
        pA = ctx.enter_context(nc.psum_tensor(f"ff{g}_pA", [FH, L], F32))
        loaded, made, chain, sines, masked = sem("loaded"), sem("made"), sem("chain"), sem("sines"), sem("masked")
        layers = ((w1, feats, b1, h1), (w2, h1, b2, s["h2T"]))
        STEPS = 7
        block = ctx.enter_context(nc.Block())

        @block.sync
        def _(sp):
            for dst, src in ((feats, io[f"tab_feats{g}"]), (mask, io[f"tab_mask{g}"]), (w1, io["filt_w1"][0]),
                             (w2, io["filt_w2"][0]), (b1, io["filt_b1"]), (b2, io["filt_b2"]), (fr, io["filt_freq"]),
                             (s["first"], io[f"tab_first{g}"]), (s["last"], io[f"tab_last{g}"])):
                sp.dma_start(dst[:], src).then_inc(loaded, 16)
            sp.wait_ge(loaded, 144)

        @block.tensor
        def _(pe):
            pe.wait_ge(loaded, 144)
            for n, (w, x, _, _) in enumerate(layers):
                if n:
                    pe.wait_ge(sines, n)
                for c in range(0, L, C):
                    last = pe.matmul(pA[:, c:c + C], w[:, :], x[:, c:c + C], start=True, stop=True)
                last.then_inc(made, 1)

        @block.vector
        def _(dve):
            dve.memset(s["ones"][:, :], 1.0)
            for n, (_, _, b, out) in enumerate(layers):
                dve.wait_ge(made, n + 1)
                if n:
                    dve.wait_ge(sines, n)
                dve.tensor_scalar(arg[:, :], pA[:, :], b[:, 0:1], fr[:, 0:1], ALU.add, ALU.mult).then_inc(chain, 1)
                dve.wait_ge(chain, STEPS * n + 1)
                dve.tensor_scalar(turns[:, :], arg[:, :], 1 / (2 * math.pi), ROUND, ALU.mult, ALU.add).then_inc(chain, 1)
                dve.wait_ge(chain, STEPS * n + 2)
                dve.tensor_scalar(turns[:, :], turns[:, :], ROUND, None, ALU.subtract).then_inc(chain, 1)
                for m, part in enumerate(TWO_PI):
                    dve.wait_ge(chain, STEPS * n + 3 + m)
                    dve.scalar_tensor_tensor(arg[:, :], turns[:, :], -part, arg[:, :], ALU.mult, ALU.add).then_inc(chain, 1)
                dve.wait_ge(chain, STEPS * n + 6)
                dve.tensor_scalar(arg[:, :], arg[:, :], PI_BELOW, -PI_BELOW, ALU.min, ALU.max).then_inc(chain, 1)
            dve.wait_ge(sines, 2)
            dve.tensor_tensor(s["h2M"][:, :], s["h2T"][:, :], mask[:, :], ALU.mult).then_inc(masked, 1)
            dve.wait_ge(masked, 1)

        @block.scalar
        def _(act):
            for n, (_, _, _, out) in enumerate(layers):
                act.wait_ge(chain, STEPS * (n + 1))
                act.activation(out[:, :], arg[:, :], ACT.Sin).then_inc(sines, 1)


def short_convolution(nc, io, s):
    g, L, NI, J = s["g"], s["L"], s["NI"], s["J"]
    with ExitStack() as ctx:
        def sb(name, shape):
            return ctx.enter_context(nc.sbuf_tensor(f"sc{g}_{name}", shape, F32))

        sem = semaphores(nc, ctx, f"sc{g}_")

        PARTS = s["PARTS"]
        u = sb("u", [P, 2, 3, CH])
        taps = sb("taps", [P, 4, CH])
        wts, u_in = sem("wts"), [sem(f"u_in{b}") for b in range(2)]
        scaled, scaled_pool, summed = sem("scaled"), sem("scaled_pool"), sem("summed")
        shifted = [token_rows(io["U"][U_OFF[g] + d:U_OFF[g] + d + L, :], s) for d in (-1, 0, 1)]
        z = s["z"][:, :, :].rearrange("p (n i) c -> p i n c", n=3)
        block = ctx.enter_context(nc.Block())

        @block.sync
        def _(sp):
            for m in range(3):
                sp.dma_start(taps[:, m, :], io["conv_w"][0, m:m + 1, :].to_broadcast([P, CH])).then_inc(wts, 16)
            sp.dma_start(taps[:, 3, :], io["conv_b"].to_broadcast([P, CH])).then_inc(wts, 16)

        def load(eng, i, b):
            for m in range(3):
                copy_parts(eng, s, u[:, b, m, :], shifted[m][i], u_in[b])

        def in_tiles(eng, step):
            if NI > 2:
                with eng.Fori(0, NI // 2 - 1) as i:
                    step(2 * i, 0, True)
                    step(2 * i + 1, 1, True)
            step(NI - 2, 0, False)
            step(NI - 1, 1, False)

        @block.scalar
        def _(act):
            load(act, 0, 0)
            load(act, 1, 1)

            def step(i, b, more):
                if more:
                    act.wait_ge(summed, 4 * i + 4)
                    load(act, i + 2, b)
            in_tiles(act, step)

        @block.gpsimd
        def _(pool):
            pool.wait_ge(wts, 64)

            def step(i, b, more):
                pool.wait_ge(u_in[b], PARTS * (24 * i - 24 * b + 48))
                pool.tensor_tensor(u[:, b, 0, :], u[:, b, 0, :], taps[:, 0, :], ALU.mult).then_inc(scaled_pool, 1)
            in_tiles(pool, step)

        @block.vector
        def _(dve):
            dve.wait_ge(wts, 64)

            def step(i, b, more):
                dve.wait_ge(u_in[b], PARTS * (24 * i - 24 * b + 48))
                for m in (1, 2):
                    dve.tensor_tensor(u[:, b, m, :], u[:, b, m, :], taps[:, m, :], ALU.mult).then_inc(scaled, 1)
                dve.wait_ge(scaled, 2 * i + 2)
                dve.tensor_tensor(u[:, b, 1, :], u[:, b, 1, :], taps[:, 3, :], ALU.add).then_inc(summed, 1)
                dve.wait_ge(summed, 4 * i + 1)
                dve.tensor_tensor(u[:, b, 1, :], u[:, b, 1, :], u[:, b, 2, :], ALU.add).then_inc(summed, 1)
                dve.wait_ge(summed, 4 * i + 2)
                dve.wait_ge(scaled_pool, i + 1)
                dve.tensor_tensor(u[:, b, 1, :], u[:, b, 1, :], u[:, b, 0, :], ALU.add).then_inc(summed, 1)
                dve.wait_ge(summed, 4 * i + 3)
                dve.tensor_copy(z[:, i, :, :] if isinstance(i, int) else s["z"][:, :, :].rearrange(
                    "p (n i) c -> p i n c", n=3)[:, bass.ds(i, 1), :, :].rearrange("p i n c -> p (i n) c"),
                    u[:, b, 1, :].rearrange("p (n c) -> p n c", n=3)).then_inc(summed, 1)
            in_tiles(dve, step)


def filter_first_stage(nc, io, s, order):
    g, L, NI, N1 = s["g"], s["L"], s["NI"], s["N1"]
    with ExitStack() as ctx:
        def sb(name, shape):
            return ctx.enter_context(nc.sbuf_tensor(f"fs{g}{order}_{name}", shape, F32))

        sem = semaphores(nc, ctx, f"fs{g}{order}_")

        w3 = sb("w3", [FH, 2, DH])
        decay = sb("decay", [P, 2, DH])
        negt = sb("negt", [P, NI])
        hs = [[sb(f"hs{b}{d}", [FH, P]) for d in range(2)] for b in range(2)]
        win = sb("win", [P, 2, 2, DH])
        tap = sb("tap", [P, 2, 2, DH])
        size = sb("size", [P, 2, 2, DH])
        sd = sb("sd", [P, 2, 2, DH])
        a = sb("a", [P, 2, 4, DH])
        pH = [ctx.enter_context(nc.psum_tensor(f"fs{g}{order}_pH{d}", [P, DH], F32)) for d in range(2)]
        pA = [ctx.enter_context(nc.psum_tensor(f"fs{g}{order}_pA{m}", [P, DH], F32)) for m in range(4)]
        wts, zeroed, hs_ready, windows = sem("wts"), sem("zeroed"), sem("hs_ready"), sem("windows")
        h_made, tapped, sized, summed, mixed = sem("h_made"), sem("tapped"), sem("sized"), sem("summed"), sem("mixed")
        a_made, a_moved, total = sem("a_made"), sem("a_moved"), sem("total")
        a_out = [sem(f"a_out{b}") for b in range(2)]
        block = ctx.enter_context(nc.Block())

        def pairs(eng, step, lag=None):
            step(0, 0)
            step(1, 1)
            if lag:
                lag(0, 0)
            if NI > 2:
                with eng.Fori(1, NI // 2) as i:
                    step(2 * i, 0)
                    if lag:
                        lag(2 * i - 1, 1)
                    step(2 * i + 1, 1)
                    if lag:
                        lag(2 * i, 0)
            if lag:
                lag(NI - 1, 1)

        @block.sync
        def _(sp):
            for d in range(2):
                at = (2 * d + order) * DH
                sp.dma_start(w3[:, d, :], io["filt_w3"][0, :, at:at + DH]).then_inc(wts, 16)
                sp.dma_start(decay[:, d, :], io["filt_decay"][0, d, order:order + 1, :].to_broadcast([P, DH])).then_inc(wts, 16)
            sp.dma_start(negt[:, :], io[f"tab_negt{g}"]).then_inc(wts, 16)

        @block.gpsimd
        def _(pool):
            def step(i, b):
                pool.wait_ge(tapped, 2 * i + 2)
                if not early(i):
                    pool.wait_ge(a_made, 4 * i - 4)
                pool.tensor_tensor(sd[:, b, 0, :], tap[:, b, 0, :], tap[:, b, 1, :], ALU.add).then_inc(mixed, 1)
                pool.tensor_tensor(sd[:, b, 1, :], tap[:, b, 0, :], tap[:, b, 1, :], ALU.subtract).then_inc(mixed, 1)
            pairs(pool, step)

        @block.scalar
        def _(act):
            act.wait_ge(wts, 80)

            def step(i, b):
                if not early(i):
                    act.wait_ge(h_made, 2 * i - 2)
                    act.wait_ge(tapped, 2 * i - 2)
                for d, src in enumerate((s["h2T"], s["h2M"])):
                    act.activation(hs[b][d][:, :], src[:, rows(i)], ACT.Copy).then_inc(hs_ready, 1)
                for d in range(2):
                    act.activation(win[:, b, d, :], decay[:, d, :], ACT.Exp, scale=negt[:, bass.ds(i, 1)]).then_inc(windows, 1)

            def lag(i, b):
                act.wait_ge(tapped, 2 * i + 2)
                if not early(i):
                    act.wait_ge(summed, i - 1)
                act.activation(size[:, b, :, :], tap[:, b, :, :], ACT.Abs).then_inc(sized, 1)
                if not early(i):
                    act.wait_ge(a_out[b], 16 * i - 16 * b)
                for m in range(4):
                    act.wait_ge(a_made, 4 * i + m + 1)
                    act.activation(a[:, b, m, :], pA[m][:, :], ACT.Copy).then_inc(a_moved, 1)
                act.wait_ge(a_moved, 4 * i + 4)
                for m, dst in enumerate((io["A"], io["B"])):
                    act.dma_start(dst[rows(i, 2 * P), :].rearrange("(h p) c -> p h c", h=2),
                                  a[:, b, 2 * m:2 * m + 2, :]).then_inc(a_out[b], 16)
            pairs(act, step, lag)
            for b in range(2):
                act.wait_ge(a_out[b], 16 * NI)

        @block.tensor
        def _(pe):
            pe.wait_ge(wts, 80)

            def step(i, b):
                for d in range(2):
                    pe.wait_ge(hs_ready, 2 * i + d + 1)
                    if not (isinstance(i, int) and i == 0):
                        pe.wait_ge(tapped, 2 * i + d - 1)
                    pe.matmul(pH[d][:, :], hs[b][d][:, :], w3[:, d, :], start=True, stop=True).then_inc(h_made, 1)

            def lag(i, b):
                for m in range(4):
                    pe.wait_ge(mixed, 2 * i + m // 2 + 1)
                    if not (isinstance(i, int) and i == 0):
                        pe.wait_ge(a_moved, 4 * i + m - 3)
                    pe.matmul(pA[m][:, :], s["first"][:, m % 2, :], sd[:, b, m // 2, :], start=True, stop=True
                              ).then_inc(a_made, 1)
            pairs(pe, step, lag)
            pe.wait_ge(summed, NI)
            pe.wait_ge(a_moved, 4 * NI)
            for d in range(2):
                last = pe.matmul(pA[0][:, :], s["ones"][:, :], s["acc"][:, d, :], start=(d == 0), stop=(d == 1))
            last.then_inc(total, 1)

        @block.vector
        def _(dve):
            dve.memset(s["acc"][:, :], 0.0).then_inc(zeroed, 1)
            dve.wait_ge(zeroed, 1)

            def step(i, b):
                if not early(i):
                    dve.wait_ge(mixed, 2 * i - 2)
                    dve.wait_ge(sized, i - 1)
                for d in range(2):
                    dve.wait_ge(windows, 2 * i + d + 1)
                    dve.wait_ge(h_made, 2 * i + d + 1)
                    dve.scalar_tensor_tensor(tap[:, b, d, :], win[:, b, d, :], 0.05, pH[d][:, :], ALU.add, ALU.mult
                                             ).then_inc(tapped, 1)

            def lag(i, b):
                dve.wait_ge(sized, i + 1)
                dve.wait_ge(summed, i)
                dve.tensor_tensor(s["acc"][:, :, :], s["acc"][:, :, :], size[:, b, :, :], ALU.add).then_inc(summed, 1)
            pairs(dve, step, lag)
            dve.wait_ge(total, 1)
            dve.reciprocal(s["rn"][:, :], pA[0][:, :]).then_inc(total, 1)
            dve.wait_ge(total, 2)


def signal_first_stage(nc, io, s, order):
    g, NI = s["g"], s["NI"]
    with ExitStack() as ctx:
        sem = semaphores(nc, ctx, f"sf{g}{order}_")

        a = ctx.enter_context(nc.sbuf_tensor(f"sf{g}{order}_a", [P, 2, 2, DH], F32))
        pA = [ctx.enter_context(nc.psum_tensor(f"sf{g}{order}_pA{m}", [P, DH], F32)) for m in range(4)]
        a_made, a_moved = sem("a_made"), sem("a_moved")
        a_out = [sem(f"a_out{b}") for b in range(2)]
        block = ctx.enter_context(nc.Block())

        @block.tensor
        def _(pe):
            def step(i, b):
                for h in range(2):
                    if not early(i):
                        pe.wait_ge(a_moved, 2 * i + h - 3)
                    pe.matmul(pA[2 * b + h][:, :], s["first"][:, h, :], s["z"][:, bass.ds(i, 1), :].rearrange(
                        "p i c -> p (i c)"), start=True, stop=True).then_inc(a_made, 1)
            in_pairs(pe, NI, step)

        @block.scalar
        def _(act):
            def step(i, b):
                if not early(i):
                    act.wait_ge(a_out[b], 8 * i - 8 * b)
                for h in range(2):
                    act.wait_ge(a_made, 2 * i + h + 1)
                    act.activation(a[:, b, h, :], pA[2 * b + h][:, :], ACT.Copy).then_inc(a_moved, 1)
                act.wait_ge(a_moved, 2 * i + 2)
                act.dma_start(io["Z"][rows(i, 2 * P), :].rearrange("(h p) c -> p h c", h=2), a[:, b, :, :]
                              ).then_inc(a_out[b], 16)
            in_pairs(act, NI, step)
            for b in range(2):
                act.wait_ge(a_out[b], 8 * NI)


def spectrum_products(nc, io, s, order):
    g, N1 = s["g"], s["N1"]
    NB = N1 // 2
    with ExitStack() as ctx:
        def sb(name, shape):
            return ctx.enter_context(nc.sbuf_tensor(f"sp{g}{order}_{name}", shape, F32))

        def ps(name):
            return ctx.enter_context(nc.psum_tensor(f"sp{g}{order}_{name}", [P, DH], F32))

        sem = semaphores(nc, ctx, f"sp{g}{order}_")

        tab = [sb(f"tab{b}", [P, 5, P]) for b in range(2)]
        rows_in = [sb(f"rows{b}", [P, 3, DH]) for b in range(2)]
        kk = sb("kk", [P, 2, 2, DH])
        pk = sb("pk", [P, 2, 2, DH])
        gg = sb("gg", [P, 2, DH])
        pX = [ps(f"pX{b}") for b in range(2)]
        pK = [[ps(f"pK{b}{m}") for m in range(2)] for b in range(2)]
        pG = [ps(f"pG{b}") for b in range(2)]
        tab_in = [sem(f"tab_in{b}") for b in range(2)]
        rows_ready = [sem(f"rows_in{b}") for b in range(2)]
        spectra, copied, multiplied = sem("spectra"), sem("copied"), sem("multiplied")
        g_made, g_moved = sem("g_made"), sem("g_moved")
        g_out = [sem(f"g_out{b}") for b in range(2)]
        src = [stage_rows(io[n], N1) for n in ("Z", "A", "B")]
        dst = stage_rows(io["G"], N1)
        block = ctx.enter_context(nc.Block())

        def load(eng, n, b):
            k1 = {0: NB, 1: 0}.get(n, n - 1) if isinstance(n, int) else n - 1
            pair = 0 if isinstance(n, int) and n < 2 else n - 1
            eng.dma_start(tab[b][:, :, :], io[f"tab_spec{g}"][:, bass.ds(k1, 1), :, :].rearrange(
                "m b p n -> p m (b n)")).then_inc(tab_in[b], 16)
            for m in range(3):
                copy_parts(eng, s, rows_in[b][:, m, :], src[m][pair], rows_ready[b])

        def over_steps(eng, step, lag):
            step(0, 0)
            step(1, 1)
            lag(0, 0)
            step(2, 0)
            lag(1, 1)
            step(3, 1)
            lag(2, 0)
            if NB > 4:
                with eng.Fori(2, NB // 2) as i:
                    step(2 * i, 0)
                    lag(2 * i - 1, 1)
                    step(2 * i + 1, 1)
                    lag(2 * i, 0)
            step(NB, 0)
            lag(NB - 1, 1)
            lag(NB, 0)

        @block.sync
        def _(sp):
            load(sp, 0, 0)
            load(sp, 1, 1)

        @block.scalar
        def _(act):
            def step(n, b):
                for m in range(2):
                    act.wait_ge(spectra, 3 * n + m + 2)
                    if not early(n):
                        act.wait_ge(multiplied, 2 * n + m - 3)
                    act.activation(kk[:, b, m, :], pK[b][m][:, :], ACT.Copy).then_inc(copied, 1)

            def lag(n, b):
                if not (isinstance(n, int) and n == 0):
                    act.wait_ge(g_made, 2 * n + 2)
                    if not (isinstance(n, int) and n < 3):
                        act.wait_ge(g_out[b], 16 * (n - 2 + b))
                    act.activation(gg[:, b, :], pG[b][:, :], ACT.Copy).then_inc(g_moved, 1)
                    act.wait_ge(g_moved, n)
                    copy_parts(act, s, gg[:, b, :], dst[n - 1], g_out[b], store=True)
                if not (isinstance(n, int) and n + 2 > NB):
                    act.wait_ge(g_made, 2 * n + 2)
                    load(act, n + 2, b)
            over_steps(act, step, lag)
            act.wait_ge(g_out[0], 16 * NB)
            act.wait_ge(g_out[1], 16 * NB)

        @block.tensor
        def _(pe):
            def step(n, b):
                pe.wait_ge(tab_in[b], 8 * n - 8 * b + 16)
                pe.wait_ge(rows_ready[b], 48 * n - 48 * b + 96)
                if not early(n):
                    pe.wait_ge(multiplied, 2 * n - 2)
                pe.matmul(pX[b][:, :], tab[b][:, 0, :], rows_in[b][:, 0, :], start=True, stop=True).then_inc(spectra, 1)
                for m in range(2):
                    pe.matmul(pK[b][m][:, :], tab[b][:, 3 + m, :], rows_in[b][:, 1 + m, :], start=True, stop=True
                              ).then_inc(spectra, 1)

            def lag(n, b):
                shared = isinstance(n, int) and n == 0
                out = pG[1] if shared else pG[b]
                if not (isinstance(n, int) and n < 3):
                    pe.wait_ge(g_moved, n - 2)
                for m in range(2):
                    pe.wait_ge(multiplied, 2 * n + m + 1)
                    pe.matmul(out[:, :], tab[b][:, 1 + m, :], pk[:, b, m, :],
                              start=(m == 0 and not (isinstance(n, int) and n == 1)),
                              stop=(m == 1 and not shared)).then_inc(g_made, 1)
            over_steps(pe, step, lag)

        @block.vector
        def _(dve):
            def step(n, b):
                for m in range(2):
                    dve.wait_ge(copied, 2 * n + m + 1)
                    dve.wait_ge(spectra, 3 * n + 3)
                    if not early(n):
                        dve.wait_ge(g_made, 2 * n + m - 3)
                    dve.tensor_tensor(pk[:, b, m, :], kk[:, b, m, :], pX[b][:, :], ALU.mult).then_inc(multiplied, 1)
            over_steps(dve, step, lambda n, b: None)


def last_stage(nc, io, s, order):
    g, L, NI, J = s["g"], s["L"], s["NI"], s["J"]
    g0 = sum(GROUPS[:g])
    with ExitStack() as ctx:
        def sb(name, shape):
            return ctx.enter_context(nc.sbuf_tensor(f"ls{g}{order}_{name}", shape, F32))

        sem = semaphores(nc, ctx, f"ls{g}{order}_")

        bias = sb("bias", [P, DH])
        gin = sb("gin", [P, 2, 2, DH])
        ynorm = sb("ynorm", [P, 2, DH])
        zb = sb("zb", [P, 2, DH])
        out = sb("out", [P, 2, DH])
        pY = [ctx.enter_context(nc.psum_tensor(f"ls{g}{order}_pY{b}", [P, DH], F32)) for b in range(2)]
        wts, y_made, chain, biased = sem("wts"), sem("y_made"), sem("chain"), sem("biased")
        g_in = [sem(f"g_in{b}") for b in range(2)]
        stored = [sem(f"stored{b}") for b in range(2)]
        dst = token_rows(io["YH"][g0:g0 + L, :], s)
        z = s["z"]
        block = ctx.enter_context(nc.Block())

        def tile_of(n, i):
            return z[:, bass.ds(n * NI + i, 1), :].rearrange("p i c -> p (i c)")

        def load(eng, i, b):
            eng.dma_start(gin[:, b, :, :], io["G"][rows(i, 2 * P), :].rearrange("(h p) c -> p h c", h=2)
                          ).then_inc(g_in[b], 16)

        def in_tiles(eng, step):
            if NI > 2:
                with eng.Fori(0, NI // 2 - 1) as i:
                    step(2 * i, 0, True)
                    step(2 * i + 1, 1, True)
            step(NI - 2, 0, False)
            step(NI - 1, 1, False)

        @block.sync
        def _(sp):
            sp.dma_start(bias[:, :], io["hyena_bias"][0, order:order + 1, :].to_broadcast([P, DH])).then_inc(wts, 16)

        @block.scalar
        def _(act):
            load(act, 0, 0)
            load(act, 1, 1)

            def step(i, b, more):
                if more:
                    act.wait_ge(y_made, i + 1)
                    load(act, i + 2, b)
                if order == 1:
                    act.wait_ge(chain, 3 * i + 3)
                    copy_parts(act, s, out[:, b, :], dst[i], stored[b], store=True)
            in_tiles(act, step)
            if order == 1:
                for b in range(2):
                    act.wait_ge(stored[b], s["PARTS"] * 8 * NI)

        @block.tensor
        def _(pe):
            def step(i, b):
                pe.wait_ge(g_in[b], 8 * i - 8 * b + 16)
                if not early(i):
                    pe.wait_ge(chain, 3 * i - 5)
                for h in range(2):
                    last = pe.matmul(pY[b][:, :], s["last"][:, h, :], gin[:, b, h, :], start=(h == 0), stop=(h == 1))
                last.then_inc(y_made, 1)
            in_pairs(pe, NI, step)

        @block.gpsimd
        def _(pool):
            pool.wait_ge(wts, 16)

            def step(i, b):
                if not early(i):
                    pool.wait_ge(chain, 3 * i - 4)
                pool.tensor_tensor(zb[:, b, :], tile_of(0, i), bias[:, :], ALU.mult).then_inc(biased, 1)
            in_pairs(pool, NI, step)

        @block.vector
        def _(dve):
            def step(i, b):
                dve.wait_ge(y_made, i + 1)
                dve.tensor_tensor(ynorm[:, b, :], s["rn"][:, :], pY[b][:, :], ALU.mult).then_inc(chain, 1)
                dve.wait_ge(chain, 3 * i + 1)
                dve.wait_ge(biased, i + 1)
                dve.tensor_tensor(ynorm[:, b, :], ynorm[:, b, :], zb[:, b, :], ALU.add).then_inc(chain, 1)
                dve.wait_ge(chain, 3 * i + 2)
                if order == 1 and not early(i):
                    dve.wait_ge(stored[b], s["PARTS"] * (8 * i - 8 * b))
                dve.tensor_tensor(out[:, b, :] if order == 1 else tile_of(0, i), ynorm[:, b, :], tile_of(1 + order, i),
                                  ALU.mult).then_inc(chain, 1)
            in_pairs(dve, NI, step)


def merge(nc, io):
    with ExitStack() as ctx:
        def sb(name, shape, dt=F32):
            return ctx.enter_context(nc.sbuf_tensor("mg_" + name, shape, dt))

        def ps(name, shape):
            return ctx.enter_context(nc.psum_tensor("mg_" + name, shape, F32))

        sem = semaphores(nc, ctx, "mg_")
        w = sb("w", [P, KD, D])
        wr = sb("wr", [P, KD, E_N])
        ogain = sb("ogain", [P, KD])
        mgain = sb("mgain", [P, D])
        eye = sb("eye", [P, P])
        eps, mhalf = sb("eps", [P, 2]), sb("mhalf", [P, 2])
        y = sb("y", [P, 2, D])
        x = sb("x", [P, 2, D])
        junk_y, junk_x = sb("junk_y", [P, D]), sb("junk_x", [P, D])
        my, mye, ry = sb("my", [P, 2, 2]), sb("mye", [P, 2, 2]), sb("ry", [P, 2, 2])
        mx, mxe, rx = sb("mx", [P, 2]), sb("mxe", [P, 2]), sb("rx", [P, 2])
        yn = sb("yn", [P, 2, D])
        yT = [sb(f"yT{b}", [P, KD, P]) for b in range(2)]
        x2 = sb("x2", [P, 2, D])
        xn = sb("xn", [P, 2, D])
        xT = sb("xT", [P, KD, P])
        lg = sb("lg", [E_N, 2, P])
        pY, pX = ps("pY", [P, KD, P]), ps("pX", [P, KD, P])
        pU, pL = ps("pU", [P, D]), ps("pL", [E_N, P])

        wts, scaled, consts = sem("wts"), sem("scaled"), sem("consts")
        t_in = [sem(f"t_in{b}") for b in range(2)]
        squared, eps_y, root_y, y_normed = sem("squared"), sem("eps_y"), sem("root_y"), sem("y_normed")
        y_turned, yT_ready, produced, added = sem("y_turned"), sem("yT_ready"), sem("produced"), sem("added")
        x_squared, eps_x, root_x, x_normed = sem("x_squared"), sem("eps_x"), sem("root_x"), sem("x_normed")
        x_turned, xT_ready, routed, lg_ready = sem("x_turned"), sem("xT_ready"), sem("routed"), sem("lg_ready")
        x2_out = [sem(f"x2_out{b}") for b in range(2)]
        xn_out = [sem(f"xn_out{b}") for b in range(2)]
        lg_out = [sem(f"lg_out{b}") for b in range(2)]
        WTS = 16 * (KD + 4)
        block = ctx.enter_context(nc.Block())

        def over_tiles(eng, step):
            step(0, 0)
            step(1, 1)
            with eng.Fori(1, NTP // 2 - 1) as i:
                step(2 * i, 0)
                step(2 * i + 1, 1)
            for t in range(NTP - 2, NT):
                step(t, t % 2)

        def x_rows(t, names):
            name = names[0] if not isinstance(t, int) or t < NTP else names[1]
            return io[name][0, rows(t if name == names[0] else t - NTP), :]

        def load(eng, t, b):
            eng.dma_start(y[:, b, 0:DH], io["YH"][rows(t), :]).then_inc(t_in[b], 16)
            eng.dma_start(y[:, b, DH:], io["YA"][rows(t), :]).then_inc(t_in[b], 16)
            eng.dma_start(x[:, b, :], x_rows(t, ("x_prompt", "x_sample"))).then_inc(t_in[b], 16)

        @block.sync
        def _(sp):
            sp.dma_start(eye[:, :], io["tab_eye"]).then_inc(wts, 16)
            sp.dma_start(ogain[:, :], io["out_norm"]).then_inc(wts, 16)
            sp.dma_start(mgain[:, :], io["mlp_norm"].to_broadcast([P, D])).then_inc(wts, 16)
            sp.dma_start(wr[:, :, :], io["w_router"][0].rearrange("(k p) e -> p k e", p=P)).then_inc(wts, 16)
            for k in range(KD):
                sp.dma_start(w[:, k, :], io["w_out"][0, k * P:(k + 1) * P, :]).then_inc(wts, 16)

        @block.gpsimd
        def _(pool):
            pool.memset(eps[:, :], EPS).then_inc(consts, 1)
            pool.memset(mhalf[:, :], -0.5).then_inc(consts, 1)
            pool.wait_ge(consts, 2)

            def of_y(t, b):
                pool.wait_ge(squared, 2 * t + 2)
                if not early(t):
                    pool.wait_ge(y_normed, 2 * t - 2)
                pool.tensor_tensor(mye[:, b, :], my[:, b, :], eps[:, :], ALU.add).then_inc(eps_y, 1)
                pool.wait_ge(eps_y, t + 1)
                pool.tensor_tensor(ry[:, b, :], mye[:, b, :], mhalf[:, :], ALU.pow).then_inc(root_y, 1)

            def step(t, b):
                if not (isinstance(t, int) and t == NT - 1):
                    of_y(t + 1, 1 - b)
                pool.wait_ge(x_squared, t + 1)
                if not early(t):
                    pool.wait_ge(x_normed, t - 1)
                pool.tensor_tensor(mxe[:, b:b + 1], mx[:, b:b + 1], eps[:, 0:1], ALU.add).then_inc(eps_x, 1)
                pool.wait_ge(eps_x, t + 1)
                pool.tensor_tensor(rx[:, b:b + 1], mxe[:, b:b + 1], mhalf[:, 0:1], ALU.pow).then_inc(root_x, 1)
            of_y(0, 0)
            over_tiles(pool, step)

        @block.scalar
        def _(act):
            load(act, 0, 0)
            load(act, 1, 1)

            def square_y(t, b):
                act.wait_ge(t_in[b], 24 * t - 24 * b + 48)
                act.wait_ge(squared, 2 * t)
                if not early(t):
                    act.wait_ge(root_y, t - 1)
                for h in range(2):
                    act.activation(junk_y[:, h * DH:(h + 1) * DH], y[:, b, h * DH:(h + 1) * DH], ACT.Square,
                                   scale=DH ** -0.5, accum_out=my[:, b, h:h + 1]).then_inc(squared, 1)

            def copy_yT(t, b):
                act.wait_ge(y_turned, t + 1)
                if not early(t):
                    act.wait_ge(produced, t - 1)
                for h in range(2):
                    act.activation(yT[b][:, 4 * h:4 * h + 4, :], pY[:, 4 * h:4 * h + 4, :], ACT.Copy).then_inc(yT_ready, 1)

            def copy_xT(t, b):
                act.wait_ge(x_turned, t + 1)
                if not (isinstance(t, int) and t == 0):
                    act.wait_ge(routed, t)
                for h in range(2):
                    act.activation(xT[:, 4 * h:4 * h + 4, :], pX[:, 4 * h:4 * h + 4, :], ACT.Copy).then_inc(xT_ready, 1)

            def copy_logits(t, b):
                act.wait_ge(routed, t + 1)
                act.wait_ge(lg_out[b], 8 * t - 8 * b)
                act.activation(lg[:, b, :], pL[:, :], ACT.Copy).then_inc(lg_ready, 1)
                act.wait_ge(lg_ready, t + 1)
                act.dma_start(io["LG"][:, rows(t)], lg[:, b, :]).then_inc(lg_out[b], 16)
                act.dma_start(io["XN"][rows(t), :], xn[:, b, :]).then_inc(xn_out[b], 16)

            def step(t, b):
                if not (isinstance(t, int) and t == NT - 1):
                    square_y(t + 1, 1 - b)
                if not (isinstance(t, int) and t == 0):
                    copy_xT(t - 1, 1 - b)
                if not (isinstance(t, int) and t == NT - 1):
                    copy_yT(t + 1, 1 - b)
                if not (isinstance(t, int) and t == 0):
                    copy_logits(t - 1, 1 - b)
                act.wait_ge(added, 2 * t + 2)
                act.wait_ge(x_squared, t)
                if not early(t):
                    act.wait_ge(root_x, t - 1)
                act.activation(junk_x[:, :], x2[:, b, :], ACT.Square, scale=D ** -0.5,
                               accum_out=mx[:, b:b + 1]).then_inc(x_squared, 1)
                act.dma_start(x_rows(t, ("y_prompt", "y_sample")), x2[:, b, :]).then_inc(x2_out[b], 16)
                if not (isinstance(t, int) and t + 2 >= NT):
                    load(act, t + 2, b)

            square_y(0, 0)
            copy_yT(0, 0)
            over_tiles(act, step)
            copy_xT(NT - 1, 1)
            copy_logits(NT - 1, 1)
            for b in range(2):
                for out in (x2_out, xn_out, lg_out):
                    act.wait_ge(out[b], 16 * NT // 2)

        @block.tensor
        def _(pe):
            pe.wait_ge(wts, WTS)
            pe.wait_ge(scaled, KD)

            def turn_y(t, b):
                pe.wait_ge(y_normed, 2 * t + 2)
                if not (isinstance(t, int) and t == 0):
                    pe.wait_ge(yT_ready, 2 * t)
                for k in range(KD):
                    last = pe.transpose(pY[:, k, :], yn[:, b, k * P:(k + 1) * P], eye[:, :])
                last.then_inc(y_turned, 1)

            def turn_x(t, b):
                pe.wait_ge(x_normed, t + 1)
                if not (isinstance(t, int) and t == 0):
                    pe.wait_ge(xT_ready, 2 * t)
                for k in range(KD):
                    last = pe.transpose(pX[:, k, :], xn[:, b, k * P:(k + 1) * P], eye[:, :])
                last.then_inc(x_turned, 1)

            def route(t, b):
                pe.wait_ge(xT_ready, 2 * t + 2)
                if not (isinstance(t, int) and t == 0):
                    pe.wait_ge(lg_ready, t)
                for k in range(KD):
                    last = pe.matmul(pL[:, :], wr[:, k, :], xT[:, k, :], start=(k == 0), stop=(k == KD - 1))
                last.then_inc(routed, 1)

            def step(t, b):
                pe.wait_ge(yT_ready, 2 * t + 2)
                if not (isinstance(t, int) and t == 0):
                    pe.wait_ge(added, 2 * t)
                for h in range(2):
                    for k in range(KD):
                        last = pe.matmul(pU[:, h * 512:(h + 1) * 512], yT[b][:, k, :], w[:, k, h * 512:(h + 1) * 512],
                                         start=(k == 0), stop=(k == KD - 1))
                last.then_inc(produced, 1)
                if not (isinstance(t, int) and t == 0):
                    turn_x(t - 1, 1 - b)
                if not (isinstance(t, int) and t == NT - 1):
                    turn_y(t + 1, 1 - b)
                if not (isinstance(t, int) and t == 0):
                    route(t - 1, 1 - b)
            turn_y(0, 0)
            over_tiles(pe, step)
            turn_x(NT - 1, 1)
            route(NT - 1, 1)

        @block.vector
        def _(dve):
            def norm_y(t, b):
                dve.wait_ge(root_y, t + 1)
                if not early(t):
                    dve.wait_ge(y_turned, t - 1)
                for h in range(2):
                    dve.tensor_scalar(yn[:, b, h * DH:(h + 1) * DH], y[:, b, h * DH:(h + 1) * DH], ry[:, b, h:h + 1],
                                      None, ALU.mult).then_inc(y_normed, 1)

            def step(t, b):
                if not (isinstance(t, int) and t == NT - 1):
                    norm_y(t + 1, 1 - b)
                dve.wait_ge(produced, t + 1)
                dve.wait_ge(x2_out[b], 8 * t - 8 * b)
                for h in range(2):
                    dve.tensor_tensor(x2[:, b, h * 512:(h + 1) * 512], x[:, b, h * 512:(h + 1) * 512],
                                      pU[:, h * 512:(h + 1) * 512], ALU.add).then_inc(added, 1)
                dve.wait_ge(root_x, t + 1)
                if not early(t):
                    dve.wait_ge(x_turned, t - 1)
                    dve.wait_ge(xn_out[b], 8 * t - 8 * b)
                dve.scalar_tensor_tensor(xn[:, b, :], x2[:, b, :], rx[:, b:b + 1], mgain[:, :], ALU.mult, ALU.mult
                                         ).then_inc(x_normed, 1)
            norm_y(0, 0)
            dve.wait_ge(wts, WTS)
            for k in range(KD):
                dve.tensor_scalar(w[:, k, :], w[:, k, :], ogain[:, k:k + 1], None, ALU.mult).then_inc(scaled, 1)
            over_tiles(dve, step)


SLOT_TILES = ((0, 0, P), (0, P, P), (1, 0, CAPS[1]))
NTOK = sum(n for _, _, n in SLOT_TILES)


def moe(nc, io):
    with ExitStack() as ctx:
        def sb(name, dt=F32):
            return ctx.enter_context(nc.sbuf_tensor("mo_" + name, [P, len(SLOT_TILES), E_N], dt))

        chosen = {"gather": sb("gather", I32), "scatter": sb("scatter", I32), "gate": sb("gate")}
        choose(nc, io, chosen)
        experts(nc, io, chosen)


def choose(nc, io, chosen):
    assert CAPS[0] == 2 * P
    with ExitStack() as ctx:
        def sb(name, shape, dt=F32):
            return ctx.enter_context(nc.sbuf_tensor("ch_" + name, shape, dt))

        def ps(name, shape):
            return ctx.enter_context(nc.psum_tensor("ch_" + name, shape, F32))

        sem = semaphores(nc, ctx, "ch_")
        eye = sb("eye", [P, P])
        lg = sb("lg", [E_N, T])
        ex = sb("ex", [P, NT, E_N])
        top, tot, inv = sb("top", [P, NT]), sb("tot", [P, NT]), sb("inv", [P, NT])
        aff = sb("aff", [E_N, T])
        val = sb("val", [E_N, NTOK])
        idx = sb("idx", [E_N, NTOK], U32)
        idf = sb("idf", [E_N, NTOK])
        pT = ps("pT", [P, NT, E_N])
        pA = ps("pA", [E_N, 5 * 512])
        pC = ps("pC", [P, 2, len(SLOT_TILES), E_N])
        loaded, turned, chain, exps, back = sem("loaded"), sem("turned"), sem("chain"), sem("exps"), sem("back")
        aff_ready, picked, columns, placed = sem("aff_ready"), sem("picked"), sem("columns"), sem("placed")
        inverted, eights = sem("summed"), sem("eights")
        block = ctx.enter_context(nc.Block())

        @block.sync
        def _(sp):
            sp.dma_start(eye[:, :], io["tab_eye"]).then_inc(loaded, 16)
            sp.dma_start(lg[:, :], io["LG"]).then_inc(loaded, 16)

        @block.tensor
        def _(pe):
            pe.wait_ge(loaded, 32)
            for t in range(NT):
                last = pe.transpose(pT[:, t, :], lg[:, t * P:(t + 1) * P], eye[0:E_N, 0:E_N])
            last.then_inc(turned, 1)
            pe.wait_ge(chain, 4)
            for t in range(NT):
                last = pe.transpose(pA[:, t * P:(t + 1) * P], ex[:, t, :], eye[:, :])
            last.then_inc(back, 1)
            pe.wait_ge(picked, 2)
            s0 = 0
            for c, (g, a, n) in enumerate(SLOT_TILES):
                for m, src in enumerate((idf, val)):
                    last = pe.transpose(pC[0:n, m, c, :], src[:, s0:s0 + n], eye[0:E_N, 0:E_N])
                s0 += n
            last.then_inc(columns, 1)

        @block.scalar
        def _(act):
            act.wait_ge(chain, 2)
            act.activation(ex[:, :, :], ex[:, :, :], ACT.Exp).then_inc(exps, 1)
            act.wait_ge(back, 1)
            act.activation(aff[:, GROUPS[0]:], pA[:, GROUPS[0]:T], ACT.Copy).then_inc(aff_ready, 1)
            act.activation(aff[:, 0:GROUPS[0]], pA[:, 0:GROUPS[0]], ACT.Copy).then_inc(aff_ready, 1)

        @block.vector
        def _(dve):
            def step(ins, sem, n):
                ins.then_inc(sem, 1)
                dve.wait_ge(sem, n)

            dve.wait_ge(turned, 1)
            step(dve.tensor_reduce(top[:, :], pT[:, :, :], AX.X, ALU.max), chain, 1)
            step(dve.tensor_tensor(ex[:, :, :], pT[:, :, :], top[:, :].unsqueeze(2).to_broadcast([P, NT, E_N]),
                                   ALU.subtract), chain, 2)
            dve.wait_ge(exps, 1)
            dve.tensor_reduce(tot[:, :], ex[:, :, :], AX.X, ALU.add).then_inc(inverted, 1)
            dve.wait_ge(inverted, 1)
            step(dve.reciprocal(inv[:, :], tot[:, :]), chain, 3)
            step(dve.tensor_tensor(ex[:, :, :], ex[:, :, :], inv[:, :].unsqueeze(2).to_broadcast([P, NT, E_N]),
                                   ALU.mult), chain, 4)
            dve.memset(chosen["gather"][:, :, :], 0).then_inc(placed, 1)
            dve.memset(chosen["scatter"][:, :, :], 0).then_inc(placed, 1)
            count = 0
            for g, order in ((1, 1), (0, 2)):
                dve.wait_ge(aff_ready, order)
                rest = aff[:, sum(GROUPS[:g]):sum(GROUPS[:g + 1])]
                s0 = sum(CAPS[:g])
                for r in range(CAPS[g] // 8):
                    v8, i8 = val[:, s0 + 8 * r:s0 + 8 * r + 8], idx[:, s0 + 8 * r:s0 + 8 * r + 8]
                    step(dve.max(v8, rest), eights, count + 1)
                    step(dve.max_index(i8, v8, rest), eights, count + 2)
                    step(dve.match_replace(rest, v8, rest, -1.0), eights, count + 3)
                    count += 3
            step(dve.tensor_copy(idf[:, :], idx[:, :]), picked, 1)
            dve.tensor_copy(val[:, 0:1], val[:, 0:1]).then_inc(picked, 1)
            dve.wait_ge(columns, 1)
            dve.wait_ge(placed, 2)
            for c, (g, a, n) in enumerate(SLOT_TILES):
                dve.tensor_copy(chosen["scatter"][0:n, c, :], pC[0:n, 0, c, :]).then_inc(placed, 1)
                dve.tensor_scalar(chosen["gather"][0:n, c, :], pC[0:n, 0, c, :], float(sum(GROUPS[:g])), None, ALU.add
                                  ).then_inc(placed, 1)
                dve.tensor_copy(chosen["gate"][0:n, c, :], pC[0:n, 1, c, :]).then_inc(placed, 1)
            dve.wait_ge(placed, 2 + 3 * len(SLOT_TILES))


def experts(nc, io, chosen):
    NC = len(SLOT_TILES)
    FT = FE // P
    starts = [sum(n for _, _, n in SLOT_TILES[:c]) for c in range(NC)]
    with ExitStack() as ctx:
        def sb(name, shape, dt=F32):
            return ctx.enter_context(nc.sbuf_tensor("ex_" + name, shape, dt))

        def ps(name, shape):
            return ctx.enter_context(nc.psum_tensor("ex_" + name, shape, F32))

        sem = semaphores(nc, ctx, "ex_")
        eye = sb("eye", [P, P])
        wg = [sb(f"wg{b}", [P, KD, FE]) for b in range(2)]
        wu = [sb(f"wu{b}", [P, KD, FE]) for b in range(2)]
        wd = [sb(f"wd{b}", [P, FT, D]) for b in range(2)]
        now_g = [sb(f"now_g{b}", [P, NC], I32) for b in range(2)]
        now_s = [sb(f"now_s{b}", [P, NC], I32) for b in range(2)]
        now_w = [sb(f"now_w{b}", [P, NC]) for b in range(2)]
        xs = [[sb(f"xs{b}{c}", [P, D]) for c in range(NC)] for b in range(2)]
        xT = sb("xT", [P, KD, NTOK])
        si = sb("si", [P, 2, NTOK])
        hT = sb("hT", [P, FT, NTOK])
        ys = [[sb(f"ys{b}{c}", [P, D]) for c in range(NC)] for b in range(2)]
        pT = ps("pT", [P, 2, 512])
        pG = [ps(f"pG{r}", [P, 512]) for r in range(2)]
        pU = [ps(f"pU{r}", [P, 512]) for r in range(2)]
        pY = ps("pY", [P, D])

        mark = sb("mark", [P, 2])
        wts, ticks = sem("wts"), sem("ticks")
        gu_in = [sem(f"gu_in{b}") for b in range(2)]
        d_in = [sem(f"d_in{b}") for b in range(2)]
        placed = sem("placed")
        gathered = [sem(f"gathered{b}") for b in range(2)]
        x_turned, xT_ready, gate_made, up_made = sem("x_turned"), sem("xT_ready"), sem("gate_made"), sem("up_made")
        silued, h_ready, y_made, y_ready = sem("silued"), sem("h_ready"), sem("y_made"), sem("y_ready")
        scattered = sem("scattered")
        block = ctx.enter_context(nc.Block())

        def over_experts(eng, step):
            step(0, 0, True)
            step(1, 1, True)
            with eng.Fori(1, E_N // 2 - 1) as i:
                step(2 * i, 0, True)
                step(2 * i + 1, 1, True)
            step(E_N - 2, 0, True)
            step(E_N - 1, 1, False)

        def load_gu(eng, e, b):
            for w, name in ((wg, "w_gate"), (wu, "w_up")):
                eng.dma_start(w[b][:, :, :], io[name][0, e, :, :].rearrange("(k p) f -> p k f", p=P)).then_inc(gu_in[b], 16)

        def load_d(eng, e, b):
            eng.dma_start(wd[b][:, :, :], io["w_down"][0, e, :, :].rearrange("(k p) f -> p k f", p=P)).then_inc(d_in[b], 16)

        @block.sync
        def _(sp):
            sp.dma_start(eye[:, :], io["tab_eye"]).then_inc(wts, 16)
            for b in range(2):
                load_gu(sp, b, b)
                load_d(sp, b, b)

            def step(e, b):
                sp.wait_ge(up_made, FT * e + FT)
                load_gu(sp, e + 2, b)
                sp.wait_ge(y_made, NC * e + NC)
                load_d(sp, e + 2, b)
            with sp.Fori(0, E_N // 2 - 1) as i:
                step(2 * i, 0)
                step(2 * i + 1, 1)

        @block.gpsimd
        def _(pool):
            pool.memset(mark[:, :], 0.0).then_inc(ticks, 1)
            pool.wait_ge(ticks, 1)

            def tick(n):
                pool.wait_ge(ticks, n + 1)
                pool.tensor_tensor(mark[:, 1:2], mark[:, 0:1], mark[:, 0:1], ALU.add).then_inc(ticks, 1)

            def gather(e, b):
                pool.wait_ge(placed, 3 * e + 3)
                if not early(e):
                    pool.wait_ge(x_turned, 4 * e - 4)
                tick((NC + 1) * e - NC if not isinstance(e, int) or e else 0)
                for c, (g, _, n) in enumerate(SLOT_TILES):
                    pool.indirect_dma_start(out=xs[b][c][0:n, :], out_offset=None, in_=io["XN"],
                                            in_offset=bass.IndirectOffsetOnAxis(ap=now_g[b][0:n, c:c + 1], axis=0)
                                            ).then_inc(gathered[b], 16)

            def step(e, b, more):
                if more:
                    gather(e + 1, 1 - b)
                if not (isinstance(e, int) and e == 0):
                    pool.wait_ge(scattered, 16 * NC * e)
                for c, (g, _, n) in enumerate(SLOT_TILES):
                    pool.wait_ge(y_ready, NC * e + c + 1)
                    tick((NC + 1) * e + 1 + more + c)
                    out = io[("y_prompt", "y_sample")[g]][0]
                    pool.indirect_dma_start(out=out, out_offset=bass.IndirectOffsetOnAxis(ap=now_s[b][0:n, c:c + 1], axis=0),
                                            in_=ys[b][c][0:n, :], in_offset=None, compute_op=ALU.add).then_inc(scattered, 16)
            gather(0, 0)
            over_experts(pool, step)
            pool.wait_ge(scattered, 16 * NC * E_N)

        @block.scalar
        def _(act):
            def copies(e, b):
                for j in range(KD // 2):
                    act.wait_ge(x_turned, 4 * e + j + 1)
                    if j == 0 and not (isinstance(e, int) and e == 0):
                        act.wait_ge(up_made, FT * e)
                    act.activation(xT[:, 2 * j:2 * j + 2, :], pT[:, :, 0:NTOK], ACT.Copy).then_inc(xT_ready, 1)

            def step(e, b, more):
                for f in range(FT):
                    act.wait_ge(gate_made, FT * e + f + 1)
                    if not (isinstance(e, int) and e == 0 and f < 2):
                        act.wait_ge(h_ready, FT * e + f - 1)
                    act.activation(si[:, f % 2, :], pG[f % 2][:, 0:NTOK], ACT.Silu).then_inc(silued, 1)
                if more:
                    copies(e + 1, 1 - b)
            copies(0, 0)
            over_experts(act, step)

        @block.tensor
        def _(pe):
            def turn(e, b):
                pe.wait_ge(gathered[b], 24 * e - 24 * b + 48)
                for j in range(KD // 2):
                    if not (isinstance(e, int) and e == 0 and j == 0):
                        pe.wait_ge(xT_ready, 4 * e + j)
                    for m in range(2):
                        for c, (_, _, n) in enumerate(SLOT_TILES):
                            k = 2 * j + m
                            last = pe.transpose(pT[:, m, starts[c]:starts[c] + n], xs[b][c][0:n, k * P:(k + 1) * P],
                                                eye[0:n, 0:n])
                    last.then_inc(x_turned, 1)

            def step(e, b, more):
                pe.wait_ge(gu_in[b], 16 * e - 16 * b + 32)
                pe.wait_ge(xT_ready, 4 * e + 4)
                for f in range(FT):
                    for out, w, done, free in ((pG, wg, gate_made, silued), (pU, wu, up_made, h_ready)):
                        if not (isinstance(e, int) and e == 0 and f < 2):
                            pe.wait_ge(free, FT * e + f - 1)
                        for k in range(KD):
                            last = pe.matmul(out[f % 2][:, 0:NTOK], w[b][:, k, f * P:(f + 1) * P], xT[:, k, :],
                                             start=(k == 0), stop=(k == KD - 1))
                        last.then_inc(done, 1)
                if more:
                    turn(e + 1, 1 - b)
                pe.wait_ge(d_in[b], 8 * e - 8 * b + 16)
                pe.wait_ge(h_ready, FT * e + FT)
                for c, (_, _, n) in enumerate(SLOT_TILES):
                    if not (isinstance(e, int) and e == 0 and c == 0):
                        pe.wait_ge(y_ready, NC * e + c)
                    for h in range(2):
                        for f in range(FT):
                            last = pe.matmul(pY[0:n, h * 512:(h + 1) * 512], hT[:, f, starts[c]:starts[c] + n],
                                             wd[b][:, f, h * 512:(h + 1) * 512], start=(f == 0), stop=(f == FT - 1))
                    last.then_inc(y_made, 1)
            pe.wait_ge(wts, 16)
            turn(0, 0)
            over_experts(pe, step)

        @block.vector
        def _(dve):
            def place(e, b):
                if not early(e):
                    dve.wait_ge(scattered, 16 * NC * (e - 1))
                for dst, name in ((now_g, "gather"), (now_s, "scatter"), (now_w, "gate")):
                    for_c = dst[b][:, :]
                    if name == "gate":
                        dve.tensor_copy(dst[b][:, 0:2], chosen[name][:, 0:2, bass.ds(e, 1)].rearrange("p c e -> p (c e)"))
                        dve.tensor_copy(dst[b][0:CAPS[1], 2:3], chosen[name][0:CAPS[1], 2, bass.ds(e, 1)]).then_inc(placed, 1)
                    else:
                        dve.tensor_copy(for_c, chosen[name][:, :, bass.ds(e, 1)].rearrange("p c e -> p (c e)")).then_inc(placed, 1)

            def step(e, b, more):
                if more:
                    place(e + 1, 1 - b)
                for f in range(FT):
                    dve.wait_ge(silued, FT * e + f + 1)
                    dve.wait_ge(up_made, FT * e + f + 1)
                    if f == 0 and not (isinstance(e, int) and e == 0):
                        dve.wait_ge(y_made, NC * e)
                    dve.tensor_tensor(hT[:, f, :], si[:, f % 2, :], pU[f % 2][:, 0:NTOK], ALU.mult).then_inc(h_ready, 1)
                if not early(e):
                    dve.wait_ge(scattered, 16 * NC * (e - 1))
                for c, (_, _, n) in enumerate(SLOT_TILES):
                    dve.wait_ge(y_made, NC * e + c + 1)
                    if c == 0:
                        dve.wait_ge(placed, 3 * e + 3)
                    dve.tensor_scalar(ys[b][c][0:n, :], pY[0:n, :], now_w[b][0:n, c:c + 1], None, ALU.mult
                                      ).then_inc(y_ready, 1)
            place(0, 0)
            over_experts(dve, step)


INPUTS = {
    "x_prompt": (1, GROUPS[0], D), "x_sample": (1, GROUPS[1], D), "attn_norm": (1, D), "w_in": (1, D, CH + CM),
    "conv_w": (1, 3, CH), "conv_b": (1, CH), "filt_w1": (1, FEAT, FH), "filt_b1": (1, FH), "filt_w2": (1, FH, FH),
    "filt_b2": (1, FH), "filt_w3": (1, FH, 4 * DH), "filt_freq": (1, FH), "filt_decay": (1, 2, 2, DH),
    "hyena_bias": (1, 2, DH), "q_a_norm": (1, QL), "w_uq": (1, QL, NH * QH), "kv_a_norm": (1, KVL),
    "w_ukv": (1, KVL, NH * (ND + VH)), "q_norm": (1, QH), "k_norm": (1, QH), "out_norm": (1, D), "w_out": (1, D, D),
    "mlp_norm": (1, D), "w_router": (1, D, E_N), "w_gate": (1, E_N, D, FE), "w_up": (1, E_N, D, FE),
    "w_down": (1, E_N, FE, D),
}
COLUMNS = {"attn_norm": P, "q_a_norm": P, "kv_a_norm": P, "out_norm": P, "filt_b1": FH, "filt_b2": FH, "filt_freq": FH}


def lay_out(name, a):
    a = np.ascontiguousarray(a)
    return np.ascontiguousarray(a.reshape(-1, COLUMNS[name]).T) if name in COLUMNS else a


def laid_shape(name):
    n = INPUTS[name][-1]
    return (COLUMNS[name], n // COLUMNS[name]) if name in COLUMNS else INPUTS[name]


SCRATCH = {
    "U": (U_ROWS, CH),
    "C": (T, CM),
    "QK": (2 * NH, QH, T),
    "V": (T, NH, VH),
    "YA": (T, DH), "YH": (T, DH),
    "A": (2 * GROUPS[0], DH),
    "B": (2 * GROUPS[0], DH),
    "Z": (2 * GROUPS[0], DH),
    "G": (2 * GROUPS[0], DH),
    "XN": (T, D),
    "LG": (E_N, T),
}
PHASES = ["project", "latent", "attend", "hyena", "merge", "moe"]


def build(nc, io, phases=PHASES):
    makers = {"project": project, "latent": latent, "attend": attend, "hyena": hyena,
              "merge": merge, "moe": moe}
    for name in phases:
        makers[name](nc, io)


def kernel(**inputs):
    import concourse.bacc as bacc
    from concourse.bass_utils import run_bass_kernel_spmd

    nc = bacc.Bacc("TRN2", target_bir_lowering=False, num_devices=1)
    arrays = {"in_" + name: lay_out(name, inputs[name]) for name in INPUTS}
    io = {name: nc.dram_tensor("in_" + name, laid_shape(name), F32, kind="ExternalInput").ap() for name in INPUTS}
    for name, a in tables().items():
        arrays[name] = a
        io[name] = nc.dram_tensor(name, a.shape, F32, kind="ExternalInput").ap()
    for name, shape in SCRATCH.items():
        io[name] = nc.dram_tensor("s_" + name, shape, F32, kind="Internal").ap()
    for name, L in (("y_prompt", GROUPS[0]), ("y_sample", GROUPS[1])):
        io[name] = nc.dram_tensor(name, (1, L, D), F32, kind="ExternalOutput").ap()
    build(nc, io)
    r = run_bass_kernel_spmd(nc, [arrays], core_ids=[0])
    return r.results[0]["y_prompt"], r.results[0]["y_sample"]
```

```python
import math
from contextlib import ExitStack

import numpy as np
import concourse.bass as bass
from concourse import mybir

F32, F16, BF16 = mybir.dt.float32, mybir.dt.float16, mybir.dt.bfloat16
I32, U32 = mybir.dt.int32, mybir.dt.uint32
ALU = mybir.AluOpType
ACT = mybir.ActivationFunctionType
AX = mybir.AxisListType

P = 128
D = 1024
KD = D // P
GROUPS = (2048, 256)
T = sum(GROUPS)
NT = T // P
NTP = GROUPS[0] // P
DH = 512
CH = 3 * DH
QL, KVL, RD = 256, 128, 32
CM = QL + KVL + RD
NH, ND, QH, VH = 8, 64, 96, 64
E_N, FE = 16, 512
FEAT, FH = 33, 64
N2 = 64
EPS = 1e-6
U_OFF = (1, GROUPS[0] + 3)
U_ROWS = T + 4
CAPS = tuple(2 * n // E_N for n in GROUPS)


def dft_tables(L):
    N = 2 * L
    N1, T1 = N // N2, L // N2
    J = P // T1
    q = np.arange(N1)
    k1 = np.where(q == 1, N1 // 2, q // 2)
    imag = (q > 1) & (q % 2 == 1)
    t1 = np.arange(T1)
    ang = 2 * np.pi * np.outer(t1, k1) / N1
    fwd = np.where(imag, -np.sin(ang), np.cos(ang))
    inv = fwd.T * np.where(q > 1, 2.0, 1.0)[:, None] / N
    first = np.zeros((2, J, T1, J // 2, N1))
    last = np.zeros((2, J // 2, N1, J, T1))
    for h in range(2):
        for jj in range(J // 2):
            first[h, h * (J // 2) + jj, :, jj, :] = fwd
            last[h, jj, :, h * (J // 2) + jj, :] = inv
    nb = N1 // 2 + 1
    t2 = np.arange(N2)[:, None]
    spec = np.zeros((nb, P, 5, P))
    for b in range(nb):
        k = b + N1 * np.arange(N2)[None, :]
        th = 2 * np.pi * ((t2 * k) % N) / N
        c, s = np.cos(th), np.sin(th)
        re = np.concatenate([c, s], 0)
        im = np.concatenate([-s, c], 0)
        gre = np.concatenate([c.T, -s.T], 0)
        gim = np.concatenate([s.T, c.T], 0)
        if b == 0:
            re[N2:] = im[N2:] = 0
            gim[:] = 0
        if b == nb - 1:
            re[N2:], im[N2:] = re[:N2].copy(), im[:N2].copy()
            re[:N2] = im[:N2] = 0
            gim, gre = gre.copy(), np.zeros_like(gre)
        inv1 = np.concatenate([gre, gim], 1)
        swapped = np.concatenate([inv1[N2:], inv1[:N2]], 0)
        order = np.arange(P).reshape(2, N2).T.reshape(-1)
        spec[b, :, 0] = np.concatenate([re, im], 1)[order]
        spec[b, :, 1] = inv1[:, order]
        spec[b, :, 2] = swapped[:, order]
        spec[b, :, 3] = np.concatenate([re, re], 1)[order]
        spec[b, :, 4] = np.concatenate([im, -im], 1)[order]
    return (first.reshape(2, P, P).transpose(1, 0, 2), last.reshape(2, P, P).transpose(1, 0, 2), spec)


def token_order(L):
    T1 = L // N2
    J = P // T1
    i, j, t1 = np.meshgrid(np.arange(N2 // J), np.arange(J), np.arange(T1), indexing="ij")
    return (64 * t1 + i * J + j).reshape(-1)


def feature_tables(L):
    f = np.float32
    t_idx = np.arange(L, dtype=f)[:, None]
    t = t_idx / f(L - 1)
    bands = np.linspace(1e-4, 15, 16, dtype=f)
    ang = f(2.0 * math.pi) * bands * t_idx / f(L)
    feats = np.concatenate([t, np.cos(ang), -np.sin(ang)], axis=-1).astype(f)
    order = token_order(L)
    return feats[order].T, -t[order, 0].reshape(-1, P).T, (order != 0).astype(f)


def tables():
    out = {}
    pos = np.concatenate([np.arange(L, dtype=np.float32) for L in GROUPS])
    inv = np.float32(10000.0) ** (-np.arange(0, RD, 2, dtype=np.float32) / np.float32(RD))
    ang = (pos[:, None] * inv).astype(np.float32)
    out["rope"] = np.concatenate([np.cos(ang), np.cos(ang), -np.sin(ang), np.sin(ang)], 1)
    out["eye"] = np.eye(P)
    for g, L in enumerate(GROUPS):
        out[f"first{g}"], out[f"last{g}"], out[f"spec{g}"] = dft_tables(L)
        out[f"feats{g}"], out[f"negt{g}"], mask = feature_tables(L)
        out[f"mask{g}"] = np.broadcast_to(mask, (FH, L))
    return {"tab_" + k: np.ascontiguousarray(v, dtype=np.float32) for k, v in out.items()}


def in_pairs(eng, n, step):
    step(0, 0)
    step(1, 1)
    if n > 2:
        with eng.Fori(1, n // 2) as i:
            step(2 * i, 0)
            step(2 * i + 1, 1)


def early(t):
    return isinstance(t, int) and t < 2


def rows(t, n=P):
    return bass.ds(t * n, n)


TAKEN = []


def semaphores(nc, ctx, prefix):
    def sem(name):
        TAKEN.append(nc.alloc_semaphore(prefix + name))
        return TAKEN[-1]
    return sem


def clear_semaphores(nc):
    nc.clear_and_free_semaphores(list(TAKEN))
    nc.all_engine_barrier()
    TAKEN.clear()


def project(nc, io):
    with ExitStack() as ctx:
        def sb(name, shape, dt=F32):
            return ctx.enter_context(nc.sbuf_tensor(name, shape, dt))

        sem = semaphores(nc, ctx, "")

        w = sb("pj_w", [P, KD, CH + CM])
        gain = sb("pj_gain", [P, KD])
        eye = sb("pj_eye", [P, P])
        zero = sb("pj_zero", [4, CH])
        x = sb("pj_x", [P, 2, D])
        sq = sb("pj_sq", [P, D])
        ms = sb("pj_ms", [P, 2])
        mse = sb("pj_mse", [P, 2])
        mhalf = sb("pj_mhalf", [P, 1])
        eps = sb("pj_eps", [P, 1])
        rstd = sb("pj_rstd", [P, 2])
        xn = sb("pj_xn", [P, 2, D])
        xT = [sb(f"pj_xT{b}", [P, KD, P]) for b in range(2)]
        u = sb("pj_u", [P, 2, CH + CM])
        pT = ctx.enter_context(nc.psum_tensor("pj_pT", [P, KD, P], F32))
        pU = [ctx.enter_context(nc.psum_tensor(f"pj_pU{c}", [P, 512], F32)) for c in range(4)]
        widths = [DH, DH, DH, CM]

        wts = sem("pj_wts")
        scaled = sem("pj_scaled")
        x_in = [sem(f"pj_x_in{b}") for b in range(2)]
        squared = sem("pj_squared")
        with_eps = sem("pj_with_eps")
        have_rstd = sem("pj_have_rstd")
        normed = sem("pj_normed")
        turned = sem("pj_turned")
        xT_ready = sem("pj_xT_ready")
        u_done = sem("pj_u_done")
        u_moved = sem("pj_u_moved")
        zeroed = sem("pj_zeroed")
        u_out = [sem(f"pj_u_out{b}") for b in range(2)]
        pads = sem("pj_pads")

        block = ctx.enter_context(nc.Block())

        @block.sync
        def _(sp):
            sp.dma_start(eye[:, :], io["tab_eye"]).then_inc(wts, 16)
            sp.dma_start(gain[:, :], io["attn_norm"]).then_inc(wts, 16)
            for k in range(KD):
                sp.dma_start(w[:, k, :], io["w_in"][0, k * P:(k + 1) * P, :]).then_inc(wts, 16)

            def load(t, b, src, again=False):
                if again:
                    sp.wait_ge(normed, t - 1)
                sp.dma_start(x[:, b, :], src).then_inc(x_in[b], 16)
            def store(t, b, row):
                sp.wait_ge(u_moved, 4 * t + 4)
                sp.dma_start(io["U"][bass.ds(row, P), :], u[:, b, 0:CH]).then_inc(u_out[b], 16)
                sp.dma_start(io["C"][rows(t), :], u[:, b, CH:]).then_inc(u_out[b], 16)

            for t in range(2):
                load(t, t, io["x_prompt"][0, rows(t), :])
            with sp.Fori(0, NTP // 2 - 1) as i:
                for b in range(2):
                    load(2 * i + b + 2, b, io["x_prompt"][0, rows(2 * i + b + 2), :], True)
                    store(2 * i + b, b, (2 * i + b) * P + U_OFF[0])
            for t in range(NTP - 2, NT):
                if t + 2 < NT:
                    load(t + 2, t % 2, io["x_sample"][0, rows(t + 2 - NTP), :], True)
                store(t, t % 2, t * P + U_OFF[0] if t < NTP else (t - NTP) * P + U_OFF[1])
            for b in range(2):
                sp.wait_ge(u_out[b], 16 * NT)

        @block.gpsimd
        def _(pool):
            pool.memset(zero[:, :], 0.0).then_inc(zeroed, 1)
            pool.memset(mhalf[:, :], -0.5).then_inc(zeroed, 1)
            pool.memset(eps[:, :], EPS).then_inc(zeroed, 1)
            pool.wait_ge(zeroed, 3)
            edges = [r for g, L in enumerate(GROUPS) for r in (U_OFF[g] - 1, U_OFF[g] + L)]
            for n, r in enumerate(edges):
                pool.dma_start(io["U"][r:r + 1, :], zero[n:n + 1, :]).then_inc(pads, 16)

            def root(t, b):
                pool.wait_ge(squared, t + 1)
                if not early(t):
                    pool.wait_ge(normed, t - 1)
                pool.tensor_tensor(mse[:, b:b + 1], ms[:, b:b + 1], eps[:, 0:1], ALU.add).then_inc(with_eps, 1)
                pool.wait_ge(with_eps, t + 1)
                pool.tensor_tensor(rstd[:, b:b + 1], mse[:, b:b + 1], mhalf[:, 0:1], ALU.pow).then_inc(have_rstd, 1)

            root(0, 0)
            root(1, 1)
            with pool.Fori(1, NT // 2) as i:
                root(2 * i, 0)
                root(2 * i + 1, 1)
            pool.wait_ge(pads, 64)

        @block.scalar
        def _(act):
            def step(t, b):
                act.wait_ge(x_in[b], 8 * t - 8 * b + 16)
                if not (isinstance(t, int) and t == 0):
                    act.wait_ge(squared, t)
                if not early(t):
                    act.wait_ge(have_rstd, t - 1)
                act.activation(sq[:, :], x[:, b, :], ACT.Square, scale=D ** -0.5,
                               accum_out=ms[:, b:b + 1]).then_inc(squared, 1)
                act.wait_ge(turned, t + 1)
                if not early(t):
                    act.wait_ge(u_done, 4 * t - 4)
                for h in range(2):
                    act.activation(xT[b][:, 4 * h:4 * h + 4, :], pT[:, 4 * h:4 * h + 4, :],
                                   ACT.Copy).then_inc(xT_ready, 1)
            in_pairs(act, NT, step)

        @block.tensor
        def _(pe):
            def turn(t, b):
                pe.wait_ge(normed, t + 1)
                if not (isinstance(t, int) and t == 0):
                    pe.wait_ge(xT_ready, 2 * t)
                for k in range(KD):
                    last = pe.transpose(pT[:, k, :], xn[:, b, k * P:(k + 1) * P], eye[:, :])
                last.then_inc(turned, 1)

            def products(t, b):
                pe.wait_ge(xT_ready, 2 * t + 2)
                for c in range(4):
                    if not (isinstance(t, int) and t == 0):
                        pe.wait_ge(u_moved, 4 * t - 3 + c)
                    for k in range(KD):
                        last = pe.matmul(pU[c][:, 0:widths[c]], xT[b][:, k, :],
                                         w[:, k, c * DH:c * DH + widths[c]], start=(k == 0), stop=(k == KD - 1))
                    last.then_inc(u_done, 1)

            pe.wait_ge(wts, 16 * (KD + 2))
            pe.wait_ge(scaled, KD)
            turn(0, 0)

            def step(t, b):
                turn(t + 1, 1 - b)
                products(t, b)
            step(0, 0)
            step(1, 1)
            with pe.Fori(1, NT // 2 - 1) as i:
                step(2 * i, 0)
                step(2 * i + 1, 1)
            step(NT - 2, 0)
            products(NT - 1, 1)

        @block.vector
        def _(dve):
            def norm(t, b):
                dve.wait_ge(have_rstd, t + 1)
                if not early(t):
                    dve.wait_ge(turned, t - 1)
                dve.tensor_scalar(xn[:, b, :], x[:, b, :], rstd[:, b:b + 1], None, ALU.mult).then_inc(normed, 1)

            def move(t, b):
                if not early(t):
                    dve.wait_ge(u_out[b], 16 * t - 16 * b)
                for c in range(4):
                    dve.wait_ge(u_done, 4 * t + c + 1)
                    dve.tensor_copy(u[:, b, c * DH:c * DH + widths[c]], pU[c][:, 0:widths[c]]).then_inc(u_moved, 1)

            norm(0, 0)
            dve.wait_ge(wts, 16 * (KD + 2))
            for k in range(KD):
                dve.tensor_scalar(w[:, k, :], w[:, k, :], gain[:, k:k + 1], None, ALU.mult).then_inc(scaled, 1)

            def step(t, b):
                norm(t + 1, 1 - b)
                move(t, b)
            step(0, 0)
            step(1, 1)
            with dve.Fori(1, NT // 2 - 1) as i:
                step(2 * i, 0)
                step(2 * i + 1, 1)
            step(NT - 2, 0)
            move(NT - 1, 1)


def latent(nc, io):
    H2 = 2 * NH
    with ExitStack() as ctx:
        def sb(name, shape, dt=F32):
            return ctx.enter_context(nc.sbuf_tensor(name, shape, dt))

        sem = semaphores(nc, ctx, "lt_")

        wq = sb("lt_wq", [P, 2, NH * QH])
        wkv = sb("lt_wkv", [P, NH * (ND + VH)])
        qan = sb("lt_qan", [P, 2])
        kvan = sb("lt_kvan", [P, 1])
        eye = sb("lt_eye", [P, P])
        gain = sb("lt_gain", [P, 2, QH])
        eps = sb("lt_eps", [P, H2])
        mhalf = sb("lt_mhalf", [P, H2])
        c = sb("lt_c", [P, 2, CM])
        rope = sb("lt_rope", [P, 2, 2 * RD])
        junk = sb("lt_junk", [P, QL])
        ms = sb("lt_ms", [P, 2, 2])
        mse = sb("lt_mse", [P, 2, 2])
        rc = sb("lt_rc", [P, 2, 2])
        cn = sb("lt_cn", [P, 2, QL + KVL])
        cT = [sb(f"lt_cT{b}", [P, 3, P]) for b in range(2)]
        qk = sb("lt_qk", [P, 2, H2, QH])
        sq = sb("lt_sq", [P, H2, QH])
        ss = sb("lt_ss", [P, H2])
        sse = sb("lt_sse", [P, H2])
        rh = sb("lt_rh", [P, H2])
        ra = sb("lt_ra", [P, H2, RD])
        rb = sb("lt_rb", [P, H2, RD])
        v = sb("lt_v", [P, 2, NH, VH])
        hT = sb("lt_hT", [QH, 2, H2, P])
        pT = ctx.enter_context(nc.psum_tensor("lt_pT", [P, 512], F32))
        pQ = ctx.enter_context(nc.psum_tensor("lt_pQ", [P, 1024], F32))
        pK = ctx.enter_context(nc.psum_tensor("lt_pK", [P, NH, ND + VH], F32))
        pH = [ctx.enter_context(nc.psum_tensor(f"lt_pH{b}", [P, 4, P], F32)) for b in range(2)]

        wts, scaled, consts = sem("wts"), sem("scaled"), sem("consts")
        c_in = [sem(f"c_in{b}") for b in range(2)]
        squared, with_eps, have_rc, c_normed = sem("squared"), sem("with_eps"), sem("have_rc"), sem("c_normed")
        turned, cT_ready, made = sem("turned"), sem("cT_ready"), sem("made")
        q_moved, k_moved, rope_moved, heads_sq = sem("q_moved"), sem("k_moved"), sem("rope_moved"), sem("heads_sq")
        summed, with_eps2, have_rh = sem("summed"), sem("with_eps2"), sem("have_rh")
        chain, roped = sem("chain"), sem("roped")
        heads_turned, hT_ready = sem("heads_turned"), sem("hT_ready")
        out_done = [sem(f"out_done{b}") for b in range(2)]
        WTS = 16 * 8

        block = ctx.enter_context(nc.Block())

        @block.sync
        def _(sp):
            sp.dma_start(eye[:, :], io["tab_eye"]).then_inc(wts, 16)
            sp.dma_start(qan[:, :], io["q_a_norm"]).then_inc(wts, 16)
            sp.dma_start(kvan[:, :], io["kv_a_norm"]).then_inc(wts, 16)
            sp.dma_start(gain[:, 0, :], io["q_norm"].to_broadcast([P, QH])).then_inc(wts, 16)
            sp.dma_start(gain[:, 1, :], io["k_norm"].to_broadcast([P, QH])).then_inc(wts, 16)
            sp.dma_start(wkv[:, :], io["w_ukv"][0]).then_inc(wts, 16)
            for k in range(2):
                sp.dma_start(wq[:, k, :], io["w_uq"][0, k * P:(k + 1) * P, :]).then_inc(wts, 16)

            for t in range(2):
                sp.dma_start(c[:, t, :], io["C"][rows(t), :]).then_inc(c_in[t], 16)
                sp.dma_start(rope[:, t, :], io["tab_rope"][rows(t), :]).then_inc(c_in[t], 16)

        def pipelined(eng, front, back):
            front(0, 0)
            front(1, 1)
            back(0, 0)
            with eng.Fori(1, NT // 2 - 1) as i:
                front(2 * i, 0)
                back(2 * i - 1, 1)
                front(2 * i + 1, 1)
                back(2 * i, 0)
            front(NT - 2, 0)
            back(NT - 3, 1)
            front(NT - 1, 1)
            back(NT - 2, 0)
            back(NT - 1, 1)

        @block.gpsimd
        def _(pool):
            pool.memset(eps[:, :], EPS).then_inc(consts, 1)
            pool.memset(mhalf[:, :], -0.5).then_inc(consts, 1)
            pool.wait_ge(consts, 2)

            def front(t, b):
                pool.wait_ge(squared, 2 * t + 2)
                if not early(t):
                    pool.wait_ge(c_normed, 2 * t - 2)
                pool.tensor_tensor(mse[:, b, :], ms[:, b, :], eps[:, 0:2], ALU.add).then_inc(with_eps, 1)
                pool.wait_ge(with_eps, t + 1)
                pool.tensor_tensor(rc[:, b, :], mse[:, b, :], mhalf[:, 0:2], ALU.pow).then_inc(have_rc, 1)

            def back(t, b):
                pool.wait_ge(summed, t + 1)
                pool.tensor_tensor(sse[:, :], ss[:, :], eps[:, :], ALU.add).then_inc(with_eps2, 1)
                pool.wait_ge(with_eps2, t + 1)
                if not (isinstance(t, int) and t == 0):
                    pool.wait_ge(chain, 6 * t - 5)
                pool.tensor_tensor(rh[:, :], sse[:, :], mhalf[:, :], ALU.pow).then_inc(have_rh, 1)

            pipelined(pool, front, back)

        @block.scalar
        def _(act):
            def front(t, b):
                act.wait_ge(c_in[b], 16 * t - 16 * b + 32)
                if not early(t):
                    act.wait_ge(have_rc, t - 1)
                if not (isinstance(t, int) and t == 0):
                    act.wait_ge(squared, 2 * t)
                act.activation(junk[:, :], c[:, b, 0:QL], ACT.Square, scale=QL ** -0.5,
                               accum_out=ms[:, b, 0:1]).then_inc(squared, 1)
                act.wait_ge(squared, 2 * t + 1)
                act.activation(junk[:, 0:KVL], c[:, b, QL:QL + KVL], ACT.Square, scale=KVL ** -0.5,
                               accum_out=ms[:, b, 1:2]).then_inc(squared, 1)
                act.wait_ge(turned, t + 1)
                if not early(t):
                    act.wait_ge(made, 2 * t - 2)
                act.activation(cT[b][:, :, :], pT[:, 0:3 * P].rearrange("p (k t) -> p k t", k=3),
                               ACT.Copy).then_inc(cT_ready, 1)
                act.wait_ge(made, 2 * t + 1)
                if not early(t):
                    act.wait_ge(heads_turned, 4 * t - 4)
                    act.wait_ge(out_done[b], 16 * t - 16 * b)
                act.activation(qk[:, b, 0:NH, :], pQ[:, 0:NH * QH].rearrange("p (h d) -> p h d", h=NH),
                               ACT.Copy).then_inc(q_moved, 1)
                act.wait_ge(made, 2 * t + 2)
                act.activation(qk[:, b, NH:, 0:ND], pK[:, :, 0:ND], ACT.Copy).then_inc(k_moved, 1)
                act.activation(v[:, b, :, :], pK[:, :, ND:], ACT.Copy).then_inc(k_moved, 1)
                act.wait_ge(q_moved, t + 1)
                act.wait_ge(k_moved, 2 * t + 2)
                act.wait_ge(rope_moved, t + 1)
                if not (isinstance(t, int) and t == 0):
                    act.wait_ge(summed, t)
                act.activation(sq[:, :, :], qk[:, b, :, :], ACT.Square, scale=QH ** -0.5).then_inc(heads_sq, 1)

            def back(t, b):
                if not (isinstance(t, int) and t >= NT - 2):
                    act.wait_ge(roped, t + 1)
                    ahead = bass.ds(t * P + 2 * P, P)
                    act.dma_start(c[:, b, :], io["C"][ahead, :]).then_inc(c_in[b], 16)
                    act.dma_start(rope[:, b, :], io["tab_rope"][ahead, :]).then_inc(c_in[b], 16)
                if not early(t):
                    act.wait_ge(out_done[b], 16 * t - 16 * b)
                for n in range(4):
                    act.wait_ge(heads_turned, 4 * t + n + 1)
                    act.activation(hT[:, b, 4 * n:4 * n + 4, :], pH[n % 2][0:QH, :, :], ACT.Copy).then_inc(hT_ready, 1)
                act.wait_ge(hT_ready, 4 * t + 4)
                act.dma_start(io["QK"][:, :, rows(t)].rearrange("h d t -> d h t"), hT[:, b, :, :]).then_inc(out_done[b], 16)
                act.dma_start(io["V"][rows(t), :, :], v[:, b, :, :]).then_inc(out_done[b], 16)

            pipelined(act, front, back)
            for b in range(2):
                act.wait_ge(out_done[b], 16 * NT)

        @block.tensor
        def _(pe):
            pe.wait_ge(wts, WTS)
            pe.wait_ge(scaled, 3)

            def front(t, b):
                pe.wait_ge(c_normed, 2 * t + 2)
                if not (isinstance(t, int) and t == 0):
                    pe.wait_ge(cT_ready, t)
                for k in range(3):
                    last = pe.transpose(pT[:, k * P:(k + 1) * P], cn[:, b, k * P:(k + 1) * P], eye[:, :])
                last.then_inc(turned, 1)
                pe.wait_ge(cT_ready, t + 1)
                if not (isinstance(t, int) and t == 0):
                    pe.wait_ge(q_moved, t)
                for n0, n1 in ((0, 512), (512, NH * QH)):
                    for k in range(2):
                        last = pe.matmul(pQ[:, n0:n1], cT[b][:, k, :], wq[:, k, n0:n1], start=(k == 0), stop=(k == 1))
                last.then_inc(made, 1)
                if not (isinstance(t, int) and t == 0):
                    pe.wait_ge(k_moved, 2 * t)
                for n in range(2):
                    last = pe.matmul(pK[:, 4 * n:4 * n + 4, :].rearrange("p h d -> p (h d)"), cT[b][:, 2, :],
                                     wkv[:, n * 512:(n + 1) * 512], start=True, stop=True)
                last.then_inc(made, 1)

            def back(t, b):
                pe.wait_ge(roped, t + 1)
                for n in range(4):
                    if not (isinstance(t, int) and t == 0 and n < 2):
                        pe.wait_ge(hT_ready, 4 * t + n - 1)
                    for m in range(4):
                        last = pe.transpose(pH[n % 2][0:QH, m, :], qk[:, b, 4 * n + m, :], eye[:, :])
                    last.then_inc(heads_turned, 1)

            pipelined(pe, front, back)

        @block.vector
        def _(dve):
            dve.wait_ge(wts, WTS)
            for k in range(2):
                dve.tensor_scalar(wq[:, k, :], wq[:, k, :], qan[:, k:k + 1], None, ALU.mult).then_inc(scaled, 1)
            dve.tensor_scalar(wkv[:, :], wkv[:, :], kvan[:, 0:1], None, ALU.mult).then_inc(scaled, 1)

            def front(t, b):
                dve.wait_ge(have_rc, t + 1)
                if not early(t):
                    dve.wait_ge(turned, t - 1)
                dve.tensor_scalar(cn[:, b, 0:QL], c[:, b, 0:QL], rc[:, b, 0:1], None, ALU.mult).then_inc(c_normed, 1)
                dve.tensor_scalar(cn[:, b, QL:], c[:, b, QL:QL + KVL], rc[:, b, 1:2], None, ALU.mult).then_inc(c_normed, 1)

                if not early(t):
                    dve.wait_ge(heads_turned, 4 * t - 4)
                dve.tensor_copy(qk[:, b, NH:, ND:], c[:, b, QL + KVL:].unsqueeze(1).to_broadcast([P, NH, RD])
                                ).then_inc(rope_moved, 1)

            def back(t, b):
                x = qk[:, b, :, :]
                turn = x[:, :, ND:]
                half = RD // 2
                dve.wait_ge(heads_sq, t + 1)
                if not (isinstance(t, int) and t == 0):
                    dve.wait_ge(with_eps2, t)
                dve.tensor_reduce(ss[:, :], sq[:, :, :], AX.X, ALU.add).then_inc(summed, 1)
                dve.wait_ge(have_rh, t + 1)
                dve.tensor_tensor(x, x, rh[:, :].unsqueeze(2).to_broadcast([P, H2, QH]), ALU.mult).then_inc(chain, 1)
                dve.wait_ge(chain, 6 * t + 1)
                for g in range(2):
                    dve.tensor_tensor(x[:, NH * g:NH * g + NH, :], x[:, NH * g:NH * g + NH, :],
                                      gain[:, g, :].unsqueeze(1).to_broadcast([P, NH, QH]), ALU.mult).then_inc(chain, 1)
                dve.wait_ge(chain, 6 * t + 3)
                cos, nsin, sin = (rope[:, b, n0:n1].unsqueeze(1).to_broadcast([P, H2, n1 - n0])
                                  for n0, n1 in ((0, RD), (RD, RD + half), (RD + half, 2 * RD)))
                dve.tensor_tensor(ra[:, :, :], turn, cos, ALU.mult).then_inc(chain, 1)
                dve.tensor_tensor(rb[:, :, 0:half], turn[:, :, half:], nsin, ALU.mult).then_inc(chain, 1)
                dve.tensor_tensor(rb[:, :, half:], turn[:, :, 0:half], sin, ALU.mult).then_inc(chain, 1)
                dve.wait_ge(chain, 6 * t + 6)
                dve.tensor_tensor(turn, ra[:, :, :], rb[:, :, :], ALU.add).then_inc(roped, 1)

            pipelined(dve, front, back)


MAX_UNIT = 32.0


TWO = 2


def attend(nc, io):
    for g in range(2):
        attend_group(nc, io, g)


def attend_group(nc, io, g):
    L = GROUPS[g]
    g0 = sum(GROUPS[:g])
    QB = min(512, L)
    NQ, KT, QT = L // QB, L // P, L // P
    NS = NQ * KT
    LONG = NS > 8
    LAG = 3 if LONG else 1
    AHEAD = 2 if LONG else 0
    CW = min(512, L)
    NC = L // CW
    SLOTS = QT * NC
    TQ = QB // P
    VC = 1 + 3 * VH
    VC2 = 1 + 2 * VH
    split_at = [1 + j // 2 if LONG else 0 for j in range(4 * NC)]
    slot_at = [8 + j * 45 // SLOTS if LONG else 0 for j in range(SLOTS)]
    turn_at = 55 if LONG else 0
    load_at = 14 if LONG else 1
    norm_at = 3 if LONG else 0
    store_at = 9 if LONG else 1
    v_at = [1, 3, 5, 7] if LONG else [1, 1, 1, 1]
    scale = QH ** -0.5
    with ExitStack() as ctx:
        def sb(name, shape, dt=F32):
            return ctx.enter_context(nc.sbuf_tensor(f"at{g}_{name}", shape, dt))

        def ps(name, shape):
            return ctx.enter_context(nc.psum_tensor(f"at{g}_{name}", shape, F32))

        sem = semaphores(nc, ctx, f"at{g}_")
        eye = sb("eye", [P, P])
        q, k, v = sb("q", [QH, L]), sb("k", [QH, L]), sb("v", [P, KT, VH])
        q1 = [sb(f"q1{b}", [QH + 1, L], F16) for b in range(2)]
        k1 = [sb(f"k1{b}", [QH + 1, L], F16) for b in range(2)]
        q2 = [sb(f"q2{b}", [QH, L], F16) for b in range(2)]
        k2 = [sb(f"k2{b}", [QH, L], F16) for b in range(2)]
        vv = [sb(f"vv{b}", [P, KT, VC], BF16) for b in range(2)]
        zero = sb("zero", [P, 1])
        vr = sb("vr", [P, KT, VH])
        mxs = sb("mxs", [P, QT, NC])
        mx = sb("mx", [P, QT])
        nmx = sb("nmx", [QT, P], F16)
        pf = sb("pf", [P, 4, QB])
        p1 = [sb(f"p1{r}", [P, QB], F16) for r in range(4)]
        p2 = [sb(f"p2{r}", [P, QB], F16) for r in range(4)]
        rec = sb("rec", [P, 2, TQ])
        osum = sb("osum", [P, 2, TQ, VH])
        o = sb("o", [P, 2, QT, VH])
        pM = [ps(f"pM{r}", [P, 512]) for r in range(2)]
        pS = [ps(f"pS{r}", [P, 512]) for r in range(2)]
        pO = [ps(f"pO{r}", [P, 2, 512]) for r in range(2)]

        consts, ready = sem("consts"), sem("ready")
        qk_in, v_in, split, v_split = sem("qk_in"), sem("v_in"), sem("split"), sem("v_split")
        slot_made, max_ready, max_turned, max_moved, max_in = (
            sem("slot_made"), sem("max_ready"), sem("max_turned"), sem("max_moved"), sem("max_in"))
        p_free, pS_free, o_free, pM_free = sem("p_free"), sem("pS_free"), sem("o_free"), sem("pM_free")
        s_made, even_done, odd_done = sem("s_made"), sem("even_done"), sem("odd_done")
        inverted = sem("inverted")
        o_stored = [sem(f"o_stored{b}") for b in range(2)]

        block = ctx.enter_context(nc.Block())

        def over_heads(eng, head, peel=False):
            if peel:
                head(0, 0, True)
                head(1, 1, True)
            with eng.Fori(int(peel), NH // 2 - 1) as i:
                head(2 * i, 0, True)
                head(2 * i + 1, 1, True)
            head(NH - 2, 0, True)
            head(NH - 1, 1, False)

        def load(eng, h):
            eng.dma_start(q[:, :], io["QK"][h, :, g0:g0 + L]).then_inc(qk_in, 16)
            eng.dma_start(k[:, :], io["QK"][h + NH, :, g0:g0 + L]).then_inc(qk_in, 16)
            eng.dma_start(v[:, :, :], io["V"][g0:g0 + L, h, :].rearrange("(k p) d -> p k d", p=P)).then_inc(v_in, 16)

        def rest(eng, h, b, n):
            r = (b * NS + n) % 4
            eng.wait_ge(p_free, NS * h + n + 1)
            eng.wait_ge(pS_free, NS * h + n + 3)
            eng.tensor_tensor(p2[r][:, :], pf[:, r, :], p1[r][:, :], ALU.subtract).then_inc(
                odd_done if n % 2 else even_done, 1)

        def rest_ahead(eng, h, b, n, more):
            if n + AHEAD < NS:
                rest(eng, h, b, n + AHEAD)
            elif more:
                rest(eng, h + 1, 1 - b, n + AHEAD - NS)

        @block.sync
        def _(sp):
            sp.dma_start(eye[:, :], io["tab_eye"]).then_inc(consts, 16)
            load(sp, 0)

            def put_max(h, b):
                sp.wait_ge(max_moved, h + 1)
                sp.dma_start(q1[b][QH:QH + 1, :], nmx[:, :]).then_inc(max_in, 16)
            with sp.Fori(0, NH // 2) as i:
                put_max(2 * i, 0)
                put_max(2 * i + 1, 1)
            sp.wait_ge(max_in, 16 * NH)

        @block.gpsimd
        def _(pool):
            pool.memset(zero[:, :], 0.0).then_inc(ready, 1)
            pool.wait_ge(ready, 1)
            for b in range(2):
                pool.memset(k1[b][QH:QH + 1, :], MAX_UNIT).then_inc(ready, 1)
                pool.wait_ge(ready, 2 * b + 2)
                pool.memset(vv[b][:, :, 0:1], 1.0).then_inc(ready, 1)
                pool.wait_ge(ready, 2 * b + 3)

            def split_v(h, b, m):
                parts = vv[b][:, :, 1:].rearrange("p k (s d) -> p s k d", s=3)
                pool.wait_ge(v_split, 4 * h + m) if m else pool.wait_ge(v_in, 16 * h + 16)
                nil = zero[:, :].unsqueeze(2).to_broadcast([P, KT, VH])
                if m == 0:
                    ins = pool.tensor_tensor(parts[:, 0, :, :], v[:, :, :], nil, ALU.add)
                elif m == 1:
                    ins = pool.tensor_tensor(vr[:, :, :], v[:, :, :], parts[:, 0, :, :], ALU.subtract)
                elif m == 2:
                    ins = pool.tensor_tensor(parts[:, 1, :, :], vr[:, :, :], nil, ALU.add)
                else:
                    ins = pool.tensor_tensor(parts[:, 2, :, :], vr[:, :, :], parts[:, 1, :, :], ALU.subtract)
                ins.then_inc(v_split, 1)

            def store(h, b):
                pool.wait_ge(o_free, NQ * h + NQ + 2)
                pool.dma_start(io["YA"][g0:g0 + L, bass.ds(h * VH, VH)].rearrange("(k p) d -> p k d", p=P),
                               o[:, b, :, :]).then_inc(o_stored[b], 16)

            def head(h, b, more):
                for n in range(NS):
                    if n % 2:
                        rest_ahead(pool, h, b, n, more)
                    if more:
                        for m in range(4):
                            if v_at[m] == n:
                                if m == 0:
                                    pool.wait_ge(p_free, NS * h + 4)
                                split_v(h + 1, 1 - b, m)
                    if n == store_at and not (isinstance(h, int) and h == 0):
                        store(h - 1, 1 - b)

            for m in range(4):
                split_v(0, 0, m)
            if AHEAD:
                rest(pool, 0, 0, 1)
            over_heads(pool, head, peel=True)
            store(NH - 1, 1)
            for b in range(2):
                pool.wait_ge(o_stored[b], 16 * NH // 2)

        @block.scalar
        def _(act):
            act.sem_inc(pS_free, 2)
            act.wait_ge(split, 4 * NC)
            act.wait_ge(v_split, 4)
            load(act, 1)

            def head(h, b, more):
                for n in range(NS):
                    r = b * NS + n
                    act.wait_ge(s_made, NS * h + n + 1)
                    act.wait_ge(p_free, NS * h + n + 1)
                    act.activation(pf[:, r % 4, :], pS[r % 2][:, 0:QB], ACT.Exp, scale=scale)
                    act.activation(p1[r % 4][:, :], pS[r % 2][:, 0:QB], ACT.Exp, scale=scale).then_inc(pS_free, 1)
                    if n == load_at and more and not (isinstance(h, int) and h == NH - 2):
                        act.wait_ge(split, 4 * NC * h + 8 * NC)
                        act.wait_ge(v_split, 4 * h + 8)
                        load(act, h + 2)

            over_heads(act, head)

        @block.tensor
        def _(pe):
            pe.sem_inc(p_free, 4)
            pe.wait_ge(consts, 16)
            pe.wait_ge(ready, 5)

            def slot(h, b, j):
                if j == 0:
                    pe.wait_ge(split, 4 * NC * h + 2 * NC)
                    if not (isinstance(h, int) and h == 0):
                        pe.wait_ge(max_moved, h)
                pe.wait_ge(pM_free, TWO * SLOTS * h + TWO * (j + 1))
                at = (j % NC) * CW
                pe.matmul(pM[j % 2][:, 0:CW], q1[b][0:QH, (j // NC) * P:(j // NC + 1) * P], k1[b][0:QH, at:at + CW],
                          start=True, stop=True).then_inc(slot_made, TWO)

            def turn_max(h):
                pe.wait_ge(max_ready, h + 1)
                pe.transpose(pM[0][0:QT, 0:P], mx[:, :], eye[:, :]).then_inc(max_turned, 1)

            def scores(h, b, n):
                r = b * NS + n
                qb, kt = n // KT, n % KT
                if n == 0:
                    pe.wait_ge(split, 4 * NC * h + 4 * NC)
                    pe.wait_ge(max_in, 16 * h + 16)
                pe.wait_ge(pS_free, NS * h + n + 1)
                keys, queries = slice(kt * P, (kt + 1) * P), slice(qb * QB, (qb + 1) * QB)
                pe.matmul(pS[r % 2][:, 0:QB], k1[b][:, keys], q1[b][:, queries], start=True, stop=False)
                pe.matmul(pS[r % 2][:, 0:QB], k1[b][0:QH, keys], q2[b][:, queries], start=False, stop=False)
                pe.matmul(pS[r % 2][:, 0:QB], k2[b][:, keys], q1[b][0:QH, queries], start=False, stop=True
                          ).then_inc(s_made, 1)

            def values(h, b, n):
                r = (b * NS + n) % 4
                qb, kt = n // KT, n % KT
                o_at = (b * NQ + qb) % 2
                pe.wait_ge(odd_done if n % 2 else even_done, NS // 2 * h + n // 2 + 1)
                if n == 0:
                    pe.wait_ge(v_split, 4 * h + 4)
                if kt == 0:
                    pe.wait_ge(o_free, NQ * h + qb + 1)
                for t in range(TQ):
                    for part, cols in ((p1, VC), (p2, VC2)):
                        last = pe.matmul(pO[o_at][:, t // 2, (t % 2) * VC:(t % 2) * VC + cols],
                                         part[r][:, t * P:(t + 1) * P], vv[b][:, kt, 0:cols],
                                         start=(kt == 0 and t % 2 == 0 and part is p1), stop=(kt == KT - 1),
                                         skip_group_check=True)
                last.then_inc(p_free, 1)

            def head(h, b, more):
                for n in range(NS):
                    if n + LAG < NS:
                        scores(h, b, n + LAG)
                    elif more:
                        scores(h + 1, 1 - b, n + LAG - NS)
                    values(h, b, n)
                    if more:
                        for j in range(SLOTS):
                            if slot_at[j] == n:
                                slot(h + 1, 1 - b, j)
                        if n == turn_at:
                            turn_max(h + 1)

            for j in range(SLOTS):
                slot(0, 0, j)
            turn_max(0)
            for n in range(LAG):
                scores(0, 0, n)
            over_heads(pe, head)

        @block.vector
        def _(dve):
            dve.sem_inc(pM_free, 2 * TWO)
            dve.sem_inc(o_free, 2)

            def split_qk(h, b, j):
                first, (x, x1, x2) = j < 2 * NC, ((q, q1[b], q2[b]), (k, k1[b], k2[b]))[j % 2]
                c = slice((j // 2 % NC) * CW, (j // 2 % NC + 1) * CW)
                if j == 0:
                    dve.wait_ge(qk_in, 32 * h + 32)
                if first:
                    dve.tensor_copy(x1[0:QH, c], x[:, c]).then_inc(split, 1)
                else:
                    dve.wait_ge(split, 4 * NC * h + j - 2 * NC + 1)
                    dve.tensor_tensor(x2[:, c], x[:, c], x1[0:QH, c], ALU.subtract).then_inc(split, 1)

            def slot(h, j):
                dve.wait_ge(slot_made, TWO * SLOTS * h + TWO * (j + 1))
                dve.tensor_reduce(mxs[:, j // NC, j % NC:j % NC + 1], pM[j % 2][:, 0:CW], AX.X, ALU.max
                                  ).then_inc(pM_free, TWO)

            def join(h):
                dve.wait_ge(pM_free, TWO * SLOTS * h + TWO * (SLOTS + 2))
                if not (isinstance(h, int) and h == 0):
                    dve.wait_ge(max_turned, h)
                dve.tensor_reduce(mx[:, :], mxs[:, :, :], AX.X, ALU.max).then_inc(max_ready, 1)
                dve.wait_ge(max_turned, h + 1)
                if not (isinstance(h, int) and h == 0):
                    dve.wait_ge(max_in, 16 * h)
                dve.tensor_scalar(nmx[:, :], pM[0][0:QT, 0:P], -1.0 / MAX_UNIT, None, ALU.mult).then_inc(max_moved, 1)

            def normalise(h, b, qb):
                o_at = (b * NQ + qb) % 2
                dve.wait_ge(p_free, NS * h + KT * (qb + 1) + 4)
                if qb == 0 and not early(h):
                    dve.wait_ge(o_stored[b], 8 * h - 8 * b)
                tiles = max(1, TQ // 2)
                sums = pO[o_at][:, 0:tiles, 0:(TQ // tiles) * VC].rearrange("p a (t d) -> p a t d", d=VC)
                shape = lambda x: x.rearrange("p (a t) d -> p a t d", a=tiles)
                dve.reciprocal(rec[:, o_at, :].rearrange("p (a t) -> p a t", a=tiles), sums[:, :, :, 0]).then_inc(inverted, 1)
                for a in range(tiles):
                    dve.tensor_reduce(osum[:, o_at, a * (TQ // tiles):(a + 1) * (TQ // tiles), :],
                                      sums[:, a, :, 1:].rearrange("p t (s d) -> p t d s", s=3), AX.X, ALU.add
                                      ).then_inc(inverted, 1)
                dve.wait_ge(inverted, (tiles + 1) * (NQ * h + qb + 1))
                dve.tensor_tensor(o[:, b, qb * TQ:(qb + 1) * TQ, :], osum[:, o_at, :, :],
                                  rec[:, o_at, :].unsqueeze(2).to_broadcast([P, TQ, VH]), ALU.mult).then_inc(o_free, 1)

            def head(h, b, more):
                for n in range(NS):
                    if n % 2 == 0:
                        rest_ahead(dve, h, b, n, more)
                    if n % KT == norm_at:
                        if n >= KT:
                            normalise(h, b, n // KT - 1)
                        elif not (isinstance(h, int) and h == 0):
                            normalise(h - 1, 1 - b, NQ - 1)
                    if more:
                        for j in range(4 * NC):
                            if split_at[j] == n:
                                split_qk(h + 1, 1 - b, j)
                        for j in range(SLOTS):
                            if slot_at[j] == n:
                                slot(h + 1, j)
                        if n == turn_at:
                            join(h + 1)

            for j in range(4 * NC):
                split_qk(0, 0, j)
            for j in range(SLOTS):
                slot(0, j)
            join(0)
            if AHEAD:
                rest(dve, 0, 0, 0)
            over_heads(dve, head, peel=True)
            normalise(NH - 1, 1, NQ - 1)


TWO_PI = (6.28125, 0.0019340515136718750, 2 * math.pi - 6.28125 - 0.0019340515136718750)
ROUND = 1.5 * 2.0 ** 23
PI_BELOW = 3.1415925


def hyena(nc, io):
    for g in range(2):
        hyena_group(nc, io, g)
        clear_semaphores(nc)


def hyena_group(nc, io, g):
    L = GROUPS[g]
    T1 = L // N2
    J = P // T1
    NI = N2 // J
    N1 = 2 * T1
    with ExitStack() as ctx:
        def sb(name, shape, dt=F32):
            return ctx.enter_context(nc.sbuf_tensor(f"hy{g}_{name}", shape, dt))

        s = {"g": g, "PARTS": J if J < 16 else 1, "L": L, "T1": T1, "J": J, "NI": NI, "N1": N1,
             "h2T": sb("h2T", [FH, L]), "h2M": sb("h2M", [FH, L]),
             "acc": sb("acc", [P, 2, DH]), "rn": sb("rn", [P, DH]),
             "z": sb("z", [P, 3 * NI, DH]),
             "first": sb("first", [P, 2, P]), "last": sb("last", [P, 2, P]), "ones": sb("ones", [P, P])}
        filter_features(nc, io, s)
        short_convolution(nc, io, s)
        for order in range(2):
            filter_first_stage(nc, io, s, order)
            signal_first_stage(nc, io, s, order)
            spectrum_products(nc, io, s, order)
            last_stage(nc, io, s, order)


def stage_rows(x, N1):
    return x[0:N2 * N1, :].rearrange("(t b r) c -> b t r c", b=N1 // 2, r=2)


def token_rows(x, s):
    return x.rearrange("(t i j) c -> i j t c", i=s["NI"], j=s["J"])


def copy_parts(eng, s, tile, dram, sem, store=False):
    a, b = dram.shape[0], dram.shape[1]
    n = 1 if a >= 16 else a
    for m in range(n):
        part, whole = (tile, dram) if n == 1 else (tile[m * b:(m + 1) * b, :], dram[m])
        eng.dma_start(*((whole, part) if store else (part, whole))).then_inc(sem, 16)


def filter_features(nc, io, s):
    g, L = s["g"], s["L"]
    C = min(512, L)
    with ExitStack() as ctx:
        def sb(name, shape):
            return ctx.enter_context(nc.sbuf_tensor(f"ff{g}_{name}", shape, F32))

        sem = semaphores(nc, ctx, f"ff{g}_")

        feats = sb("feats", [FEAT, L])
        mask = sb("mask", [FH, L])
        w1, w2 = sb("w1", [FEAT, FH]), sb("w2", [FH, FH])
        b1, b2, fr = sb("b1", [FH, 1]), sb("b2", [FH, 1]), sb("fr", [FH, 1])
        arg, turns, h1 = sb("arg", [FH, L]), sb("turns", [FH, L]), sb("h1", [FH, L])
        pA = ctx.enter_context(nc.psum_tensor(f"ff{g}_pA", [FH, L], F32))
        loaded, made, chain, sines, masked = sem("loaded"), sem("made"), sem("chain"), sem("sines"), sem("masked")
        layers = ((w1, feats, b1, h1), (w2, h1, b2, s["h2T"]))
        STEPS = 7
        block = ctx.enter_context(nc.Block())

        @block.sync
        def _(sp):
            for dst, src in ((feats, io[f"tab_feats{g}"]), (mask, io[f"tab_mask{g}"]), (w1, io["filt_w1"][0]),
                             (w2, io["filt_w2"][0]), (b1, io["filt_b1"]), (b2, io["filt_b2"]), (fr, io["filt_freq"]),
                             (s["first"], io[f"tab_first{g}"]), (s["last"], io[f"tab_last{g}"])):
                sp.dma_start(dst[:], src).then_inc(loaded, 16)
            sp.wait_ge(loaded, 144)

        @block.tensor
        def _(pe):
            pe.wait_ge(loaded, 144)
            for n, (w, x, _, _) in enumerate(layers):
                if n:
                    pe.wait_ge(sines, n)
                for c in range(0, L, C):
                    last = pe.matmul(pA[:, c:c + C], w[:, :], x[:, c:c + C], start=True, stop=True)
                last.then_inc(made, 1)

        @block.vector
        def _(dve):
            dve.memset(s["ones"][:, :], 1.0)
            for n, (_, _, b, out) in enumerate(layers):
                dve.wait_ge(made, n + 1)
                if n:
                    dve.wait_ge(sines, n)
                dve.tensor_scalar(arg[:, :], pA[:, :], b[:, 0:1], fr[:, 0:1], ALU.add, ALU.mult).then_inc(chain, 1)
                dve.wait_ge(chain, STEPS * n + 1)
                dve.tensor_scalar(turns[:, :], arg[:, :], 1 / (2 * math.pi), ROUND, ALU.mult, ALU.add).then_inc(chain, 1)
                dve.wait_ge(chain, STEPS * n + 2)
                dve.tensor_scalar(turns[:, :], turns[:, :], ROUND, None, ALU.subtract).then_inc(chain, 1)
                for m, part in enumerate(TWO_PI):
                    dve.wait_ge(chain, STEPS * n + 3 + m)
                    dve.scalar_tensor_tensor(arg[:, :], turns[:, :], -part, arg[:, :], ALU.mult, ALU.add).then_inc(chain, 1)
                dve.wait_ge(chain, STEPS * n + 6)
                dve.tensor_scalar(arg[:, :], arg[:, :], PI_BELOW, -PI_BELOW, ALU.min, ALU.max).then_inc(chain, 1)
            dve.wait_ge(sines, 2)
            dve.tensor_tensor(s["h2M"][:, :], s["h2T"][:, :], mask[:, :], ALU.mult).then_inc(masked, 1)
            dve.wait_ge(masked, 1)

        @block.scalar
        def _(act):
            for n, (_, _, _, out) in enumerate(layers):
                act.wait_ge(chain, STEPS * (n + 1))
                act.activation(out[:, :], arg[:, :], ACT.Sin).then_inc(sines, 1)


def short_convolution(nc, io, s):
    g, L, NI, J = s["g"], s["L"], s["NI"], s["J"]
    with ExitStack() as ctx:
        def sb(name, shape):
            return ctx.enter_context(nc.sbuf_tensor(f"sc{g}_{name}", shape, F32))

        sem = semaphores(nc, ctx, f"sc{g}_")

        PARTS = s["PARTS"]
        u = sb("u", [P, 2, 3, CH])
        taps = sb("taps", [P, 4, CH])
        wts, u_in = sem("wts"), [sem(f"u_in{b}") for b in range(2)]
        scaled, scaled_pool, summed = sem("scaled"), sem("scaled_pool"), sem("summed")
        shifted = [token_rows(io["U"][U_OFF[g] + d:U_OFF[g] + d + L, :], s) for d in (-1, 0, 1)]
        z = s["z"][:, :, :].rearrange("p (n i) c -> p i n c", n=3)
        block = ctx.enter_context(nc.Block())

        @block.sync
        def _(sp):
            for m in range(3):
                sp.dma_start(taps[:, m, :], io["conv_w"][0, m:m + 1, :].to_broadcast([P, CH])).then_inc(wts, 16)
            sp.dma_start(taps[:, 3, :], io["conv_b"].to_broadcast([P, CH])).then_inc(wts, 16)

        def load(eng, i, b):
            for m in range(3):
                copy_parts(eng, s, u[:, b, m, :], shifted[m][i], u_in[b])

        def in_tiles(eng, step):
            if NI > 2:
                with eng.Fori(0, NI // 2 - 1) as i:
                    step(2 * i, 0, True)
                    step(2 * i + 1, 1, True)
            step(NI - 2, 0, False)
            step(NI - 1, 1, False)

        @block.scalar
        def _(act):
            load(act, 0, 0)
            load(act, 1, 1)

            def step(i, b, more):
                if more:
                    act.wait_ge(summed, 4 * i + 4)
                    load(act, i + 2, b)
            in_tiles(act, step)

        @block.gpsimd
        def _(pool):
            pool.wait_ge(wts, 64)

            def step(i, b, more):
                pool.wait_ge(u_in[b], PARTS * (24 * i - 24 * b + 48))
                pool.tensor_tensor(u[:, b, 0, :], u[:, b, 0, :], taps[:, 0, :], ALU.mult).then_inc(scaled_pool, 1)
            in_tiles(pool, step)

        @block.vector
        def _(dve):
            dve.wait_ge(wts, 64)

            def step(i, b, more):
                dve.wait_ge(u_in[b], PARTS * (24 * i - 24 * b + 48))
                for m in (1, 2):
                    dve.tensor_tensor(u[:, b, m, :], u[:, b, m, :], taps[:, m, :], ALU.mult).then_inc(scaled, 1)
                dve.wait_ge(scaled, 2 * i + 2)
                dve.tensor_tensor(u[:, b, 1, :], u[:, b, 1, :], taps[:, 3, :], ALU.add).then_inc(summed, 1)
                dve.wait_ge(summed, 4 * i + 1)
                dve.tensor_tensor(u[:, b, 1, :], u[:, b, 1, :], u[:, b, 2, :], ALU.add).then_inc(summed, 1)
                dve.wait_ge(summed, 4 * i + 2)
                dve.wait_ge(scaled_pool, i + 1)
                dve.tensor_tensor(u[:, b, 1, :], u[:, b, 1, :], u[:, b, 0, :], ALU.add).then_inc(summed, 1)
                dve.wait_ge(summed, 4 * i + 3)
                dve.tensor_copy(z[:, i, :, :] if isinstance(i, int) else s["z"][:, :, :].rearrange(
                    "p (n i) c -> p i n c", n=3)[:, bass.ds(i, 1), :, :].rearrange("p i n c -> p (i n) c"),
                    u[:, b, 1, :].rearrange("p (n c) -> p n c", n=3)).then_inc(summed, 1)
            in_tiles(dve, step)


def filter_first_stage(nc, io, s, order):
    g, L, NI, N1 = s["g"], s["L"], s["NI"], s["N1"]
    with ExitStack() as ctx:
        def sb(name, shape):
            return ctx.enter_context(nc.sbuf_tensor(f"fs{g}{order}_{name}", shape, F32))

        sem = semaphores(nc, ctx, f"fs{g}{order}_")

        w3 = sb("w3", [FH, 2, DH])
        decay = sb("decay", [P, 2, DH])
        negt = sb("negt", [P, NI])
        hs = [[sb(f"hs{b}{d}", [FH, P]) for d in range(2)] for b in range(2)]
        win = sb("win", [P, 2, 2, DH])
        tap = sb("tap", [P, 2, 2, DH])
        size = sb("size", [P, 2, 2, DH])
        sd = sb("sd", [P, 2, 2, DH])
        a = sb("a", [P, 2, 4, DH])
        pH = [ctx.enter_context(nc.psum_tensor(f"fs{g}{order}_pH{d}", [P, DH], F32)) for d in range(2)]
        pA = [ctx.enter_context(nc.psum_tensor(f"fs{g}{order}_pA{m}", [P, DH], F32)) for m in range(4)]
        wts, zeroed, hs_ready, windows = sem("wts"), sem("zeroed"), sem("hs_ready"), sem("windows")
        h_made, tapped, sized, summed, mixed = sem("h_made"), sem("tapped"), sem("sized"), sem("summed"), sem("mixed")
        a_made, a_moved, total = sem("a_made"), sem("a_moved"), sem("total")
        a_out = [sem(f"a_out{b}") for b in range(2)]
        block = ctx.enter_context(nc.Block())

        def far_pairs(eng, step, lag):
            step(0, 0)
            step(1, 1)
            if NI > 2:
                step(2, 0)
                lag(0, 0)
                step(3, 1)
                lag(1, 1)
                with eng.Fori(1, NI // 2 - 1) as i:
                    for b in range(2):
                        step(2 * i + 2 + b, b)
                        lag(2 * i + b, b)
            lag(NI - 2, 0)
            lag(NI - 1, 1)

        def pairs(eng, step, lag=None):
            step(0, 0)
            step(1, 1)
            if lag:
                lag(0, 0)
            if NI > 2:
                with eng.Fori(1, NI // 2) as i:
                    step(2 * i, 0)
                    if lag:
                        lag(2 * i - 1, 1)
                    step(2 * i + 1, 1)
                    if lag:
                        lag(2 * i, 0)
            if lag:
                lag(NI - 1, 1)

        @block.sync
        def _(sp):
            for d in range(2):
                at = (2 * d + order) * DH
                sp.dma_start(w3[:, d, :], io["filt_w3"][0, :, at:at + DH]).then_inc(wts, 16)
                sp.dma_start(decay[:, d, :], io["filt_decay"][0, d, order:order + 1, :].to_broadcast([P, DH])).then_inc(wts, 16)
            sp.dma_start(negt[:, :], io[f"tab_negt{g}"]).then_inc(wts, 16)

        @block.gpsimd
        def _(pool):
            def step(i, b):
                pool.wait_ge(tapped, 2 * i + 2)
                if not early(i):
                    pool.wait_ge(a_made, 4 * i - 4)
                pool.tensor_tensor(sd[:, b, 0, :], tap[:, b, 0, :], tap[:, b, 1, :], ALU.add).then_inc(mixed, 1)
                pool.tensor_tensor(sd[:, b, 1, :], tap[:, b, 0, :], tap[:, b, 1, :], ALU.subtract).then_inc(mixed, 1)
            pairs(pool, step)

        @block.scalar
        def _(act):
            act.wait_ge(wts, 80)

            def step(i, b):
                if not early(i):
                    act.wait_ge(h_made, 2 * i - 2)
                    act.wait_ge(tapped, 2 * i - 2)
                for d, src in enumerate((s["h2T"], s["h2M"])):
                    act.activation(hs[b][d][:, :], src[:, rows(i)], ACT.Copy).then_inc(hs_ready, 1)
                for d in range(2):
                    act.activation(win[:, b, d, :], decay[:, d, :], ACT.Exp, scale=negt[:, bass.ds(i, 1)]).then_inc(windows, 1)

            def lag(i, b):
                act.wait_ge(tapped, 2 * i + 2)
                if not early(i):
                    act.wait_ge(summed, i - 1)
                act.activation(size[:, b, :, :], tap[:, b, :, :], ACT.Abs).then_inc(sized, 1)
                if not early(i):
                    act.wait_ge(a_out[b], 16 * i - 16 * b)
                for m in range(4):
                    act.wait_ge(a_made, 4 * i + m + 1)
                    act.activation(a[:, b, m, :], pA[m][:, :], ACT.Copy).then_inc(a_moved, 1)
                act.wait_ge(a_moved, 4 * i + 4)
                for h in range(2):
                    act.dma_start(io["F"][bass.ds(i * 2 * P + h * P, P), DH:], a[:, b, 2 * h:2 * h + 2, :]
                                  ).then_inc(a_out[b], 16)
            far_pairs(act, step, lag)
            for b in range(2):
                act.wait_ge(a_out[b], 16 * NI)

        @block.tensor
        def _(pe):
            pe.wait_ge(wts, 80)

            def step(i, b):
                for d in range(2):
                    pe.wait_ge(hs_ready, 2 * i + d + 1)
                    if not (isinstance(i, int) and i == 0):
                        pe.wait_ge(tapped, 2 * i + d - 1)
                    pe.matmul(pH[d][:, :], hs[b][d][:, :], w3[:, d, :], start=True, stop=True).then_inc(h_made, 1)

            def lag(i, b):
                for m in range(4):
                    pe.wait_ge(mixed, 2 * i + 2)
                    if not (isinstance(i, int) and i == 0):
                        pe.wait_ge(a_moved, 4 * i + m - 3)
                    pe.matmul(pA[m][:, :], s["first"][:, m // 2, :], sd[:, b, m % 2, :], start=True, stop=True
                              ).then_inc(a_made, 1)
            pairs(pe, step, lag)
            pe.wait_ge(summed, NI)
            pe.wait_ge(a_moved, 4 * NI)
            for d in range(2):
                last = pe.matmul(pA[0][:, :], s["ones"][:, :], s["acc"][:, d, :], start=(d == 0), stop=(d == 1))
            last.then_inc(total, 1)

        @block.vector
        def _(dve):
            dve.memset(s["acc"][:, :], 0.0).then_inc(zeroed, 1)
            dve.wait_ge(zeroed, 1)

            def step(i, b):
                if not early(i):
                    dve.wait_ge(mixed, 2 * i - 2)
                    dve.wait_ge(sized, i - 1)
                for d in range(2):
                    dve.wait_ge(windows, 2 * i + d + 1)
                    dve.wait_ge(h_made, 2 * i + d + 1)
                    dve.scalar_tensor_tensor(tap[:, b, d, :], win[:, b, d, :], 0.05, pH[d][:, :], ALU.add, ALU.mult
                                             ).then_inc(tapped, 1)

            def lag(i, b):
                dve.wait_ge(sized, i + 1)
                dve.wait_ge(summed, i)
                dve.tensor_tensor(s["acc"][:, :, :], s["acc"][:, :, :], size[:, b, :, :], ALU.add).then_inc(summed, 1)
            pairs(dve, step, lag)
            dve.wait_ge(total, 1)
            dve.reciprocal(s["rn"][:, :], pA[0][:, :]).then_inc(total, 1)
            dve.wait_ge(total, 2)


def signal_first_stage(nc, io, s, order):
    g, NI = s["g"], s["NI"]
    with ExitStack() as ctx:
        sem = semaphores(nc, ctx, f"sf{g}{order}_")

        a = ctx.enter_context(nc.sbuf_tensor(f"sf{g}{order}_a", [P, 2, 2, DH], F32))
        pA = [ctx.enter_context(nc.psum_tensor(f"sf{g}{order}_pA{m}", [P, DH], F32)) for m in range(4)]
        a_made, a_moved = sem("a_made"), sem("a_moved")
        a_out = [sem(f"a_out{b}") for b in range(2)]
        block = ctx.enter_context(nc.Block())

        @block.tensor
        def _(pe):
            def step(i, b):
                for h in range(2):
                    if not early(i):
                        pe.wait_ge(a_moved, 2 * i + h - 3)
                    pe.matmul(pA[2 * b + h][:, :], s["first"][:, h, :], s["z"][:, bass.ds(i, 1), :].rearrange(
                        "p i c -> p (i c)"), start=True, stop=True).then_inc(a_made, 1)
            in_pairs(pe, NI, step)

        @block.scalar
        def _(act):
            def step(i, b):
                if not early(i):
                    act.wait_ge(a_out[b], 8 * i - 8 * b)
                for h in range(2):
                    act.wait_ge(a_made, 2 * i + h + 1)
                    act.activation(a[:, b, h, :], pA[2 * b + h][:, :], ACT.Copy).then_inc(a_moved, 1)
                act.wait_ge(a_moved, 2 * i + 2)
                act.dma_start(io["F"][rows(i, 2 * P), 0:DH].rearrange("(h p) c -> p h c", h=2), a[:, b, :, :]
                              ).then_inc(a_out[b], 16)
            in_pairs(act, NI, step)
            for b in range(2):
                act.wait_ge(a_out[b], 8 * NI)


def spectrum_products(nc, io, s, order):
    g, N1 = s["g"], s["N1"]
    NB = N1 // 2
    with ExitStack() as ctx:
        def sb(name, shape):
            return ctx.enter_context(nc.sbuf_tensor(f"sp{g}{order}_{name}", shape, F32))

        def ps(name):
            return ctx.enter_context(nc.psum_tensor(f"sp{g}{order}_{name}", [P, DH], F32))

        sem = semaphores(nc, ctx, f"sp{g}{order}_")

        tab = [sb(f"tab{r}", [P, 5, P]) for r in range(4)]
        rows_in = [sb(f"rows{r}", [P, 3, DH]) for r in range(4)]
        kk = sb("kk", [P, 2, 2, DH])
        pk = sb("pk", [P, 2, 2, DH])
        gg = sb("gg", [P, 2, DH])
        pX = [ps(f"pX{b}") for b in range(2)]
        pK = [[ps(f"pK{b}{m}") for m in range(2)] for b in range(2)]
        pG = [ps(f"pG{b}") for b in range(2)]
        step_in = [sem(f"step_in{r}") for r in range(4)]
        spectra, copied, multiplied = sem("spectra"), sem("copied"), sem("multiplied")
        g_made, g_moved = sem("g_made"), sem("g_moved")
        g_out = [sem(f"g_out{b}") for b in range(2)]
        src, dst = stage_rows(io["F"], N1), stage_rows(io["G"], N1)
        block = ctx.enter_context(nc.Block())

        def load(eng, n, r):
            k1 = {0: NB, 1: 0}.get(n, n - 1) if isinstance(n, int) else n - 1
            pair = 0 if isinstance(n, int) and n < 2 else n - 1
            eng.dma_start(tab[r][:, :, :], io[f"tab_spec{g}"][k1]).then_inc(step_in[r], 16)
            eng.dma_start(rows_in[r][:, :, :], src[pair]).then_inc(step_in[r], 16)

        def over_steps(eng, step, lag):
            step(0, 0, 0)
            for n in range(1, 4):
                step(n, n, n % 2)
                lag(n - 1, n - 1, (n - 1) % 2)
            if NB > 4:
                with eng.Fori(1, NB // 4) as i:
                    for r in range(4):
                        step(4 * i + r, r, r % 2)
                        lag(4 * i + r - 1, (r - 1) % 4, (r - 1) % 2)
            step(NB, 0, 0)
            lag(NB - 1, 3, 1)
            lag(NB, 0, 0)

        @block.sync
        def _(sp):
            for n in range(4):
                load(sp, n, n)
            if NB > 4:
                with sp.Fori(0, NB // 4 - 1) as i:
                    for r in range(4):
                        sp.wait_ge(g_made, 8 * i + 2 * r + 2)
                        load(sp, 4 * i + r + 4, r)
            sp.wait_ge(g_made, 2 * (NB - 4) + 2)
            load(sp, NB, 0)

        @block.scalar
        def _(act):
            def step(n, r, b):
                for m in range(2):
                    act.wait_ge(spectra, 3 * n + m + 2)
                    if not early(n):
                        act.wait_ge(multiplied, 2 * n + m - 3)
                    act.activation(kk[:, b, m, :], pK[b][m][:, :], ACT.Copy).then_inc(copied, 1)

            def lag(n, r, b):
                if not (isinstance(n, int) and n == 0):
                    act.wait_ge(g_made, 2 * n + 2)
                    if not (isinstance(n, int) and n < 3):
                        act.wait_ge(g_out[b], 8 * (n - 2 + b))
                    act.activation(gg[:, b, :], pG[b][:, :], ACT.Copy).then_inc(g_moved, 1)
                    act.wait_ge(g_moved, n)
                    act.dma_start(dst[n - 1], gg[:, b, :]).then_inc(g_out[b], 16)
            over_steps(act, step, lag)
            for b in range(2):
                act.wait_ge(g_out[b], 8 * NB)

        @block.tensor
        def _(pe):
            def step(n, r, b):
                pe.wait_ge(step_in[r], 8 * n - 8 * r + 32)
                if not early(n):
                    pe.wait_ge(multiplied, 2 * n - 2)
                pe.matmul(pX[b][:, :], tab[r][:, 0, :], rows_in[r][:, 0, :], start=True, stop=True).then_inc(spectra, 1)
                for m in range(2):
                    pe.matmul(pK[b][m][:, :], tab[r][:, 3 + m, :], rows_in[r][:, 1 + m, :], start=True, stop=True
                              ).then_inc(spectra, 1)

            def lag(n, r, b):
                shared = isinstance(n, int) and n == 0
                out = pG[1] if shared else pG[b]
                if not (isinstance(n, int) and n < 3):
                    pe.wait_ge(g_moved, n - 2)
                for m in range(2):
                    pe.wait_ge(multiplied, 2 * n + m + 1)
                    pe.matmul(out[:, :], tab[r][:, 1 + m, :], pk[:, b, m, :],
                              start=(m == 0 and not (isinstance(n, int) and n == 1)),
                              stop=(m == 1 and not shared)).then_inc(g_made, 1)
            over_steps(pe, step, lag)

        @block.vector
        def _(dve):
            def step(n, r, b):
                for m in range(2):
                    dve.wait_ge(copied, 2 * n + m + 1)
                    dve.wait_ge(spectra, 3 * n + 3)
                    if not early(n):
                        dve.wait_ge(g_made, 2 * n + m - 3)
                    dve.tensor_tensor(pk[:, b, m, :], kk[:, b, m, :], pX[b][:, :], ALU.mult).then_inc(multiplied, 1)
            over_steps(dve, step, lambda n, r, b: None)


def last_stage(nc, io, s, order):
    g, L, NI, J = s["g"], s["L"], s["NI"], s["J"]
    g0 = sum(GROUPS[:g])
    with ExitStack() as ctx:
        def sb(name, shape):
            return ctx.enter_context(nc.sbuf_tensor(f"ls{g}{order}_{name}", shape, F32))

        sem = semaphores(nc, ctx, f"ls{g}{order}_")

        bias = sb("bias", [P, DH])
        gin = sb("gin", [P, 2, 2, DH])
        ynorm = sb("ynorm", [P, 2, DH])
        zb = sb("zb", [P, 2, DH])
        out = sb("out", [P, 2, DH])
        pY = [ctx.enter_context(nc.psum_tensor(f"ls{g}{order}_pY{b}", [P, DH], F32)) for b in range(2)]
        wts, y_made, chain, biased = sem("wts"), sem("y_made"), sem("chain"), sem("biased")
        g_in = [sem(f"g_in{b}") for b in range(2)]
        stored = [sem(f"stored{b}") for b in range(2)]
        dst = token_rows(io["YH"][g0:g0 + L, :], s)
        z = s["z"]
        block = ctx.enter_context(nc.Block())

        def tile_of(n, i):
            return z[:, bass.ds(n * NI + i, 1), :].rearrange("p i c -> p (i c)")

        def load(eng, i, b):
            eng.dma_start(gin[:, b, :, :], io["G"][rows(i, 2 * P), :].rearrange("(h p) c -> p h c", h=2)
                          ).then_inc(g_in[b], 16)

        def in_tiles(eng, step):
            if NI > 2:
                with eng.Fori(0, NI // 2 - 1) as i:
                    step(2 * i, 0, True)
                    step(2 * i + 1, 1, True)
            step(NI - 2, 0, False)
            step(NI - 1, 1, False)

        @block.sync
        def _(sp):
            sp.dma_start(bias[:, :], io["hyena_bias"][0, order:order + 1, :].to_broadcast([P, DH])).then_inc(wts, 16)

        @block.scalar
        def _(act):
            load(act, 0, 0)
            load(act, 1, 1)

            def step(i, b, more):
                if more:
                    act.wait_ge(y_made, i + 1)
                    load(act, i + 2, b)
                if order == 1:
                    act.wait_ge(chain, 3 * i + 3)
                    copy_parts(act, s, out[:, b, :], dst[i], stored[b], store=True)
            in_tiles(act, step)
            if order == 1:
                for b in range(2):
                    act.wait_ge(stored[b], s["PARTS"] * 8 * NI)

        @block.tensor
        def _(pe):
            def step(i, b):
                pe.wait_ge(g_in[b], 8 * i - 8 * b + 16)
                if not early(i):
                    pe.wait_ge(chain, 3 * i - 5)
                for h in range(2):
                    last = pe.matmul(pY[b][:, :], s["last"][:, h, :], gin[:, b, h, :], start=(h == 0), stop=(h == 1))
                last.then_inc(y_made, 1)
            in_pairs(pe, NI, step)

        @block.gpsimd
        def _(pool):
            pool.wait_ge(wts, 16)

            def step(i, b):
                if not early(i):
                    pool.wait_ge(chain, 3 * i - 4)
                pool.tensor_tensor(zb[:, b, :], tile_of(0, i), bias[:, :], ALU.mult).then_inc(biased, 1)
            in_pairs(pool, NI, step)

        @block.vector
        def _(dve):
            def step(i, b):
                dve.wait_ge(y_made, i + 1)
                dve.tensor_tensor(ynorm[:, b, :], s["rn"][:, :], pY[b][:, :], ALU.mult).then_inc(chain, 1)
                dve.wait_ge(chain, 3 * i + 1)
                dve.wait_ge(biased, i + 1)
                dve.tensor_tensor(ynorm[:, b, :], ynorm[:, b, :], zb[:, b, :], ALU.add).then_inc(chain, 1)
                dve.wait_ge(chain, 3 * i + 2)
                if order == 1 and not early(i):
                    dve.wait_ge(stored[b], s["PARTS"] * (8 * i - 8 * b))
                dve.tensor_tensor(out[:, b, :] if order == 1 else tile_of(0, i), ynorm[:, b, :], tile_of(1 + order, i),
                                  ALU.mult).then_inc(chain, 1)
            in_pairs(dve, NI, step)


def merge(nc, io):
    with ExitStack() as ctx:
        def sb(name, shape, dt=F32):
            return ctx.enter_context(nc.sbuf_tensor("mg_" + name, shape, dt))

        def ps(name, shape):
            return ctx.enter_context(nc.psum_tensor("mg_" + name, shape, F32))

        sem = semaphores(nc, ctx, "mg_")
        w = sb("w", [P, KD, D])
        wr = sb("wr", [P, KD, E_N])
        ogain = sb("ogain", [P, KD])
        mgain = sb("mgain", [P, D])
        eye = sb("eye", [P, P])
        eps, mhalf = sb("eps", [P, 2]), sb("mhalf", [P, 2])
        y = sb("y", [P, 2, D])
        x = sb("x", [P, 2, D])
        junk_y, junk_x = sb("junk_y", [P, D]), sb("junk_x", [P, D])
        my, mye, ry = sb("my", [P, 2, 2]), sb("mye", [P, 2, 2]), sb("ry", [P, 2, 2])
        mx, mxe, rx = sb("mx", [P, 2]), sb("mxe", [P, 2]), sb("rx", [P, 2])
        yn = sb("yn", [P, 2, D])
        yT = [sb(f"yT{b}", [P, KD, P]) for b in range(2)]
        x2 = sb("x2", [P, 2, D])
        xn = sb("xn", [P, 2, D])
        xT = sb("xT", [P, KD, P])
        lg = sb("lg", [E_N, 2, P])
        pY, pX = ps("pY", [P, KD, P]), ps("pX", [P, KD, P])
        pU, pL = ps("pU", [P, D]), ps("pL", [E_N, P])

        wts, scaled, consts = sem("wts"), sem("scaled"), sem("consts")
        t_in = [sem(f"t_in{b}") for b in range(2)]
        squared, eps_y, root_y, y_normed = sem("squared"), sem("eps_y"), sem("root_y"), sem("y_normed")
        y_turned, yT_ready, produced, added = sem("y_turned"), sem("yT_ready"), sem("produced"), sem("added")
        x_squared, eps_x, root_x, x_normed = sem("x_squared"), sem("eps_x"), sem("root_x"), sem("x_normed")
        x_turned, xT_ready, routed, lg_ready = sem("x_turned"), sem("xT_ready"), sem("routed"), sem("lg_ready")
        x2_out = [sem(f"x2_out{b}") for b in range(2)]
        xn_out = [sem(f"xn_out{b}") for b in range(2)]
        lg_out = [sem(f"lg_out{b}") for b in range(2)]
        WTS = 16 * (KD + 4)
        block = ctx.enter_context(nc.Block())

        def over_tiles(eng, step):
            step(0, 0)
            step(1, 1)
            with eng.Fori(1, NTP // 2 - 1) as i:
                step(2 * i, 0)
                step(2 * i + 1, 1)
            for t in range(NTP - 2, NT):
                step(t, t % 2)

        def x_rows(t, names):
            name = names[0] if not isinstance(t, int) or t < NTP else names[1]
            return io[name][0, rows(t if name == names[0] else t - NTP), :]

        def load(eng, t, b):
            eng.dma_start(y[:, b, 0:DH], io["YH"][rows(t), :]).then_inc(t_in[b], 16)
            eng.dma_start(y[:, b, DH:], io["YA"][rows(t), :]).then_inc(t_in[b], 16)
            eng.dma_start(x[:, b, :], x_rows(t, ("x_prompt", "x_sample"))).then_inc(t_in[b], 16)

        @block.sync
        def _(sp):
            sp.dma_start(eye[:, :], io["tab_eye"]).then_inc(wts, 16)
            sp.dma_start(ogain[:, :], io["out_norm"]).then_inc(wts, 16)
            sp.dma_start(mgain[:, :], io["mlp_norm"].to_broadcast([P, D])).then_inc(wts, 16)
            sp.dma_start(wr[:, :, :], io["w_router"][0].rearrange("(k p) e -> p k e", p=P)).then_inc(wts, 16)
            for k in range(KD):
                sp.dma_start(w[:, k, :], io["w_out"][0, k * P:(k + 1) * P, :]).then_inc(wts, 16)

        @block.gpsimd
        def _(pool):
            pool.memset(eps[:, :], EPS).then_inc(consts, 1)
            pool.memset(mhalf[:, :], -0.5).then_inc(consts, 1)
            pool.wait_ge(consts, 2)

            def of_y(t, b):
                pool.wait_ge(squared, 2 * t + 2)
                if not early(t):
                    pool.wait_ge(y_normed, 2 * t - 2)
                pool.tensor_tensor(mye[:, b, :], my[:, b, :], eps[:, :], ALU.add).then_inc(eps_y, 1)
                pool.wait_ge(eps_y, t + 1)
                pool.tensor_tensor(ry[:, b, :], mye[:, b, :], mhalf[:, :], ALU.pow).then_inc(root_y, 1)

            def step(t, b):
                if not (isinstance(t, int) and t == NT - 1):
                    of_y(t + 1, 1 - b)
                pool.wait_ge(x_squared, t + 1)
                if not early(t):
                    pool.wait_ge(x_normed, t - 1)
                pool.tensor_tensor(mxe[:, b:b + 1], mx[:, b:b + 1], eps[:, 0:1], ALU.add).then_inc(eps_x, 1)
                pool.wait_ge(eps_x, t + 1)
                pool.tensor_tensor(rx[:, b:b + 1], mxe[:, b:b + 1], mhalf[:, 0:1], ALU.pow).then_inc(root_x, 1)
            of_y(0, 0)
            over_tiles(pool, step)

        @block.scalar
        def _(act):
            load(act, 0, 0)
            load(act, 1, 1)

            def square_y(t, b):
                act.wait_ge(t_in[b], 24 * t - 24 * b + 48)
                act.wait_ge(squared, 2 * t)
                if not early(t):
                    act.wait_ge(root_y, t - 1)
                for h in range(2):
                    act.activation(junk_y[:, h * DH:(h + 1) * DH], y[:, b, h * DH:(h + 1) * DH], ACT.Square,
                                   scale=DH ** -0.5, accum_out=my[:, b, h:h + 1]).then_inc(squared, 1)

            def copy_yT(t, b):
                act.wait_ge(y_turned, t + 1)
                if not early(t):
                    act.wait_ge(produced, t - 1)
                for h in range(2):
                    act.activation(yT[b][:, 4 * h:4 * h + 4, :], pY[:, 4 * h:4 * h + 4, :], ACT.Copy).then_inc(yT_ready, 1)

            def copy_xT(t, b):
                act.wait_ge(x_turned, t + 1)
                if not (isinstance(t, int) and t == 0):
                    act.wait_ge(routed, t)
                for h in range(2):
                    act.activation(xT[:, 4 * h:4 * h + 4, :], pX[:, 4 * h:4 * h + 4, :], ACT.Copy).then_inc(xT_ready, 1)

            def copy_logits(t, b):
                act.wait_ge(routed, t + 1)
                act.wait_ge(lg_out[b], 8 * t - 8 * b)
                act.activation(lg[:, b, :], pL[:, :], ACT.Copy).then_inc(lg_ready, 1)
                act.wait_ge(lg_ready, t + 1)
                act.dma_start(io["LG"][:, rows(t)], lg[:, b, :]).then_inc(lg_out[b], 16)
                act.dma_start(io["XN"][rows(t), :], xn[:, b, :]).then_inc(xn_out[b], 16)

            def step(t, b):
                if not (isinstance(t, int) and t == NT - 1):
                    square_y(t + 1, 1 - b)
                if not (isinstance(t, int) and t == 0):
                    copy_xT(t - 1, 1 - b)
                if not (isinstance(t, int) and t == NT - 1):
                    copy_yT(t + 1, 1 - b)
                if not (isinstance(t, int) and t == 0):
                    copy_logits(t - 1, 1 - b)
                act.wait_ge(added, 2 * t + 2)
                act.wait_ge(x_squared, t)
                if not early(t):
                    act.wait_ge(root_x, t - 1)
                act.activation(junk_x[:, :], x2[:, b, :], ACT.Square, scale=D ** -0.5,
                               accum_out=mx[:, b:b + 1]).then_inc(x_squared, 1)
                act.dma_start(x_rows(t, ("y_prompt", "y_sample")), x2[:, b, :]).then_inc(x2_out[b], 16)
                if not (isinstance(t, int) and t + 2 >= NT):
                    load(act, t + 2, b)

            square_y(0, 0)
            copy_yT(0, 0)
            over_tiles(act, step)
            copy_xT(NT - 1, 1)
            copy_logits(NT - 1, 1)
            for b in range(2):
                for out in (x2_out, xn_out, lg_out):
                    act.wait_ge(out[b], 16 * NT // 2)

        @block.tensor
        def _(pe):
            pe.wait_ge(wts, WTS)
            pe.wait_ge(scaled, KD)

            def turn_y(t, b):
                pe.wait_ge(y_normed, 2 * t + 2)
                if not (isinstance(t, int) and t == 0):
                    pe.wait_ge(yT_ready, 2 * t)
                for k in range(KD):
                    last = pe.transpose(pY[:, k, :], yn[:, b, k * P:(k + 1) * P], eye[:, :])
                last.then_inc(y_turned, 1)

            def turn_x(t, b):
                pe.wait_ge(x_normed, t + 1)
                if not (isinstance(t, int) and t == 0):
                    pe.wait_ge(xT_ready, 2 * t)
                for k in range(KD):
                    last = pe.transpose(pX[:, k, :], xn[:, b, k * P:(k + 1) * P], eye[:, :])
                last.then_inc(x_turned, 1)

            def route(t, b):
                pe.wait_ge(xT_ready, 2 * t + 2)
                if not (isinstance(t, int) and t == 0):
                    pe.wait_ge(lg_ready, t)
                for k in range(KD):
                    last = pe.matmul(pL[:, :], wr[:, k, :], xT[:, k, :], start=(k == 0), stop=(k == KD - 1))
                last.then_inc(routed, 1)

            def step(t, b):
                pe.wait_ge(yT_ready, 2 * t + 2)
                if not (isinstance(t, int) and t == 0):
                    pe.wait_ge(added, 2 * t)
                for h in range(2):
                    for k in range(KD):
                        last = pe.matmul(pU[:, h * 512:(h + 1) * 512], yT[b][:, k, :], w[:, k, h * 512:(h + 1) * 512],
                                         start=(k == 0), stop=(k == KD - 1))
                last.then_inc(produced, 1)
                if not (isinstance(t, int) and t == 0):
                    turn_x(t - 1, 1 - b)
                if not (isinstance(t, int) and t == NT - 1):
                    turn_y(t + 1, 1 - b)
                if not (isinstance(t, int) and t == 0):
                    route(t - 1, 1 - b)
            turn_y(0, 0)
            over_tiles(pe, step)
            turn_x(NT - 1, 1)
            route(NT - 1, 1)

        @block.vector
        def _(dve):
            def norm_y(t, b):
                dve.wait_ge(root_y, t + 1)
                if not early(t):
                    dve.wait_ge(y_turned, t - 1)
                for h in range(2):
                    dve.tensor_scalar(yn[:, b, h * DH:(h + 1) * DH], y[:, b, h * DH:(h + 1) * DH], ry[:, b, h:h + 1],
                                      None, ALU.mult).then_inc(y_normed, 1)

            def step(t, b):
                if not (isinstance(t, int) and t == NT - 1):
                    norm_y(t + 1, 1 - b)
                dve.wait_ge(produced, t + 1)
                dve.wait_ge(x2_out[b], 8 * t - 8 * b)
                for h in range(2):
                    dve.tensor_tensor(x2[:, b, h * 512:(h + 1) * 512], x[:, b, h * 512:(h + 1) * 512],
                                      pU[:, h * 512:(h + 1) * 512], ALU.add).then_inc(added, 1)
                dve.wait_ge(root_x, t + 1)
                if not early(t):
                    dve.wait_ge(x_turned, t - 1)
                    dve.wait_ge(xn_out[b], 8 * t - 8 * b)
                dve.scalar_tensor_tensor(xn[:, b, :], x2[:, b, :], rx[:, b:b + 1], mgain[:, :], ALU.mult, ALU.mult
                                         ).then_inc(x_normed, 1)
            norm_y(0, 0)
            dve.wait_ge(wts, WTS)
            for k in range(KD):
                dve.tensor_scalar(w[:, k, :], w[:, k, :], ogain[:, k:k + 1], None, ALU.mult).then_inc(scaled, 1)
            over_tiles(dve, step)


SLOT_TILES = ((0, 0, P), (0, P, P), (1, 0, CAPS[1]))
NTOK = sum(n for _, _, n in SLOT_TILES)


def moe(nc, io):
    with ExitStack() as ctx:
        def sb(name, dt=F32):
            return ctx.enter_context(nc.sbuf_tensor("mo_" + name, [P, len(SLOT_TILES), E_N], dt))

        chosen = {"gather": sb("gather", I32), "scatter": sb("scatter", I32), "gate": sb("gate")}
        choose(nc, io, chosen)
        experts(nc, io, chosen)


def choose(nc, io, chosen):
    assert CAPS[0] == 2 * P
    with ExitStack() as ctx:
        def sb(name, shape, dt=F32):
            return ctx.enter_context(nc.sbuf_tensor("ch_" + name, shape, dt))

        def ps(name, shape):
            return ctx.enter_context(nc.psum_tensor("ch_" + name, shape, F32))

        sem = semaphores(nc, ctx, "ch_")
        eye = sb("eye", [P, P])
        lg = sb("lg", [E_N, T])
        ex = sb("ex", [P, NT, E_N])
        top, tot, inv = sb("top", [P, NT]), sb("tot", [P, NT]), sb("inv", [P, NT])
        aff = sb("aff", [E_N, T])
        val = sb("val", [E_N, NTOK])
        idx = sb("idx", [E_N, NTOK], U32)
        idf = sb("idf", [E_N, NTOK])
        pT = ps("pT", [P, NT, E_N])
        pA = ps("pA", [E_N, 5 * 512])
        pC = ps("pC", [P, 2, len(SLOT_TILES), E_N])
        loaded, turned, chain, exps, back = sem("loaded"), sem("turned"), sem("chain"), sem("exps"), sem("back")
        aff_ready, picked, columns, placed = sem("aff_ready"), sem("picked"), sem("columns"), sem("placed")
        inverted, eights = sem("summed"), sem("eights")
        block = ctx.enter_context(nc.Block())

        @block.sync
        def _(sp):
            sp.dma_start(eye[:, :], io["tab_eye"]).then_inc(loaded, 16)
            sp.dma_start(lg[:, :], io["LG"]).then_inc(loaded, 16)

        @block.tensor
        def _(pe):
            pe.wait_ge(loaded, 32)
            for t in range(NT):
                last = pe.transpose(pT[:, t, :], lg[:, t * P:(t + 1) * P], eye[0:E_N, 0:E_N])
            last.then_inc(turned, 1)
            pe.wait_ge(chain, 4)
            for t in range(NT):
                last = pe.transpose(pA[:, t * P:(t + 1) * P], ex[:, t, :], eye[:, :])
            last.then_inc(back, 1)
            pe.wait_ge(picked, 2)
            s0 = 0
            for c, (g, a, n) in enumerate(SLOT_TILES):
                for m, src in enumerate((idf, val)):
                    last = pe.transpose(pC[0:n, m, c, :], src[:, s0:s0 + n], eye[0:E_N, 0:E_N])
                s0 += n
            last.then_inc(columns, 1)

        @block.scalar
        def _(act):
            act.wait_ge(chain, 2)
            act.activation(ex[:, :, :], ex[:, :, :], ACT.Exp).then_inc(exps, 1)
            act.wait_ge(back, 1)
            act.activation(aff[:, GROUPS[0]:], pA[:, GROUPS[0]:T], ACT.Copy).then_inc(aff_ready, 1)
            act.activation(aff[:, 0:GROUPS[0]], pA[:, 0:GROUPS[0]], ACT.Copy).then_inc(aff_ready, 1)

        @block.vector
        def _(dve):
            def step(ins, sem, n):
                ins.then_inc(sem, 1)
                dve.wait_ge(sem, n)

            dve.wait_ge(turned, 1)
            step(dve.tensor_reduce(top[:, :], pT[:, :, :], AX.X, ALU.max), chain, 1)
            step(dve.tensor_tensor(ex[:, :, :], pT[:, :, :], top[:, :].unsqueeze(2).to_broadcast([P, NT, E_N]),
                                   ALU.subtract), chain, 2)
            dve.wait_ge(exps, 1)
            dve.tensor_reduce(tot[:, :], ex[:, :, :], AX.X, ALU.add).then_inc(inverted, 1)
            dve.wait_ge(inverted, 1)
            step(dve.reciprocal(inv[:, :], tot[:, :]), chain, 3)
            step(dve.tensor_tensor(ex[:, :, :], ex[:, :, :], inv[:, :].unsqueeze(2).to_broadcast([P, NT, E_N]),
                                   ALU.mult), chain, 4)
            dve.memset(chosen["gather"][:, :, :], 0).then_inc(placed, 1)
            dve.memset(chosen["scatter"][:, :, :], 0).then_inc(placed, 1)
            count = 0
            for g, order in ((1, 1), (0, 2)):
                dve.wait_ge(aff_ready, order)
                rest = aff[:, sum(GROUPS[:g]):sum(GROUPS[:g + 1])]
                s0 = sum(CAPS[:g])
                for r in range(CAPS[g] // 8):
                    v8, i8 = val[:, s0 + 8 * r:s0 + 8 * r + 8], idx[:, s0 + 8 * r:s0 + 8 * r + 8]
                    step(dve.max(v8, rest), eights, count + 1)
                    step(dve.max_index(i8, v8, rest), eights, count + 2)
                    step(dve.match_replace(rest, v8, rest, -1.0), eights, count + 3)
                    count += 3
            step(dve.tensor_copy(idf[:, :], idx[:, :]), picked, 1)
            dve.tensor_copy(val[:, 0:1], val[:, 0:1]).then_inc(picked, 1)
            dve.wait_ge(columns, 1)
            dve.wait_ge(placed, 2)
            for c, (g, a, n) in enumerate(SLOT_TILES):
                dve.tensor_copy(chosen["scatter"][0:n, c, :], pC[0:n, 0, c, :]).then_inc(placed, 1)
                dve.tensor_scalar(chosen["gather"][0:n, c, :], pC[0:n, 0, c, :], float(sum(GROUPS[:g])), None, ALU.add
                                  ).then_inc(placed, 1)
                dve.tensor_copy(chosen["gate"][0:n, c, :], pC[0:n, 1, c, :]).then_inc(placed, 1)
            dve.wait_ge(placed, 2 + 3 * len(SLOT_TILES))


def experts(nc, io, chosen):
    NC = len(SLOT_TILES)
    FT = FE // P
    starts = [sum(n for _, _, n in SLOT_TILES[:c]) for c in range(NC)]
    with ExitStack() as ctx:
        def sb(name, shape, dt=F32):
            return ctx.enter_context(nc.sbuf_tensor("ex_" + name, shape, dt))

        def ps(name, shape):
            return ctx.enter_context(nc.psum_tensor("ex_" + name, shape, F32))

        sem = semaphores(nc, ctx, "ex_")
        eye = sb("eye", [P, P])
        wg = [sb(f"wg{b}", [P, KD, FE]) for b in range(2)]
        wu = [sb(f"wu{b}", [P, KD, FE]) for b in range(2)]
        wd = [sb(f"wd{b}", [P, FT, D]) for b in range(2)]
        now_g = [sb(f"now_g{b}", [P, NC], I32) for b in range(2)]
        now_s = [sb(f"now_s{b}", [P, NC], I32) for b in range(2)]
        now_w = [sb(f"now_w{b}", [P, NC]) for b in range(2)]
        xs = [[sb(f"xs{b}{c}", [P, D]) for c in range(NC)] for b in range(2)]
        xT = sb("xT", [P, KD, NTOK])
        si = sb("si", [P, 2, NTOK])
        hT = sb("hT", [P, FT, NTOK])
        ys = [[sb(f"ys{b}{c}", [P, D]) for c in range(NC)] for b in range(2)]
        pT = ps("pT", [P, 2, 512])
        pG = [ps(f"pG{r}", [P, 512]) for r in range(2)]
        pU = [ps(f"pU{r}", [P, 512]) for r in range(2)]
        pY = ps("pY", [P, D])

        mark = sb("mark", [P, 2])
        wts, ticks = sem("wts"), sem("ticks")
        gu_in = [sem(f"gu_in{b}") for b in range(2)]
        d_in = [sem(f"d_in{b}") for b in range(2)]
        placed = sem("placed")
        gathered = [sem(f"gathered{b}") for b in range(2)]
        x_turned, xT_ready, gate_made, up_made = sem("x_turned"), sem("xT_ready"), sem("gate_made"), sem("up_made")
        silued, h_ready, y_made, y_ready = sem("silued"), sem("h_ready"), sem("y_made"), sem("y_ready")
        scattered = sem("scattered")
        block = ctx.enter_context(nc.Block())

        def over_experts(eng, step):
            step(0, 0, True)
            step(1, 1, True)
            with eng.Fori(1, E_N // 2 - 1) as i:
                step(2 * i, 0, True)
                step(2 * i + 1, 1, True)
            step(E_N - 2, 0, True)
            step(E_N - 1, 1, False)

        def load_gu(eng, e, b):
            for w, name in ((wg, "w_gate"), (wu, "w_up")):
                eng.dma_start(w[b][:, :, :], io[name][0, e, :, :].rearrange("(k p) f -> p k f", p=P)).then_inc(gu_in[b], 16)

        def load_d(eng, e, b):
            eng.dma_start(wd[b][:, :, :], io["w_down"][0, e, :, :].rearrange("(k p) f -> p k f", p=P)).then_inc(d_in[b], 16)

        @block.sync
        def _(sp):
            sp.dma_start(eye[:, :], io["tab_eye"]).then_inc(wts, 16)
            for b in range(2):
                load_gu(sp, b, b)
                load_d(sp, b, b)

            def step(e, b):
                sp.wait_ge(up_made, FT * e + FT)
                load_gu(sp, e + 2, b)
                sp.wait_ge(y_made, NC * e + NC)
                load_d(sp, e + 2, b)
            with sp.Fori(0, E_N // 2 - 1) as i:
                step(2 * i, 0)
                step(2 * i + 1, 1)

        @block.gpsimd
        def _(pool):
            pool.memset(mark[:, :], 0.0).then_inc(ticks, 1)
            pool.wait_ge(ticks, 1)

            def tick(n):
                pool.wait_ge(ticks, n + 1)
                pool.tensor_tensor(mark[:, 1:2], mark[:, 0:1], mark[:, 0:1], ALU.add).then_inc(ticks, 1)

            def gather(e, b):
                pool.wait_ge(placed, 3 * e + 3)
                if not early(e):
                    pool.wait_ge(x_turned, 4 * e - 4)
                tick((NC + 1) * e - NC if not isinstance(e, int) or e else 0)
                for c, (g, _, n) in enumerate(SLOT_TILES):
                    pool.indirect_dma_start(out=xs[b][c][0:n, :], out_offset=None, in_=io["XN"],
                                            in_offset=bass.IndirectOffsetOnAxis(ap=now_g[b][0:n, c:c + 1], axis=0)
                                            ).then_inc(gathered[b], 16)

            def step(e, b, more):
                if more:
                    gather(e + 1, 1 - b)
                if not (isinstance(e, int) and e == 0):
                    pool.wait_ge(scattered, 16 * NC * e)
                for c, (g, _, n) in enumerate(SLOT_TILES):
                    pool.wait_ge(y_ready, NC * e + c + 1)
                    tick((NC + 1) * e + 1 + more + c)
                    out = io[("y_prompt", "y_sample")[g]][0]
                    pool.indirect_dma_start(out=out, out_offset=bass.IndirectOffsetOnAxis(ap=now_s[b][0:n, c:c + 1], axis=0),
                                            in_=ys[b][c][0:n, :], in_offset=None, compute_op=ALU.add).then_inc(scattered, 16)
            gather(0, 0)
            over_experts(pool, step)
            pool.wait_ge(scattered, 16 * NC * E_N)

        @block.scalar
        def _(act):
            def copies(e, b):
                for j in range(KD // 2):
                    act.wait_ge(x_turned, 4 * e + j + 1)
                    if j == 0 and not (isinstance(e, int) and e == 0):
                        act.wait_ge(up_made, FT * e)
                    act.activation(xT[:, 2 * j:2 * j + 2, :], pT[:, :, 0:NTOK], ACT.Copy).then_inc(xT_ready, 1)

            def step(e, b, more):
                for f in range(FT):
                    act.wait_ge(gate_made, FT * e + f + 1)
                    if not (isinstance(e, int) and e == 0 and f < 2):
                        act.wait_ge(h_ready, FT * e + f - 1)
                    act.activation(si[:, f % 2, :], pG[f % 2][:, 0:NTOK], ACT.Silu).then_inc(silued, 1)
                if more:
                    copies(e + 1, 1 - b)
            copies(0, 0)
            over_experts(act, step)

        @block.tensor
        def _(pe):
            def turn(e, b):
                pe.wait_ge(gathered[b], 24 * e - 24 * b + 48)
                for j in range(KD // 2):
                    if not (isinstance(e, int) and e == 0 and j == 0):
                        pe.wait_ge(xT_ready, 4 * e + j)
                    for m in range(2):
                        for c, (_, _, n) in enumerate(SLOT_TILES):
                            k = 2 * j + m
                            last = pe.transpose(pT[:, m, starts[c]:starts[c] + n], xs[b][c][0:n, k * P:(k + 1) * P],
                                                eye[0:n, 0:n])
                    last.then_inc(x_turned, 1)

            def step(e, b, more):
                pe.wait_ge(gu_in[b], 16 * e - 16 * b + 32)
                pe.wait_ge(xT_ready, 4 * e + 4)
                for f in range(FT):
                    for out, w, done, free in ((pG, wg, gate_made, silued), (pU, wu, up_made, h_ready)):
                        if not (isinstance(e, int) and e == 0 and f < 2):
                            pe.wait_ge(free, FT * e + f - 1)
                        for k in range(KD):
                            last = pe.matmul(out[f % 2][:, 0:NTOK], w[b][:, k, f * P:(f + 1) * P], xT[:, k, :],
                                             start=(k == 0), stop=(k == KD - 1))
                        last.then_inc(done, 1)
                if more:
                    turn(e + 1, 1 - b)
                pe.wait_ge(d_in[b], 8 * e - 8 * b + 16)
                pe.wait_ge(h_ready, FT * e + FT)
                for c, (_, _, n) in enumerate(SLOT_TILES):
                    if not (isinstance(e, int) and e == 0 and c == 0):
                        pe.wait_ge(y_ready, NC * e + c)
                    for h in range(2):
                        for f in range(FT):
                            last = pe.matmul(pY[0:n, h * 512:(h + 1) * 512], hT[:, f, starts[c]:starts[c] + n],
                                             wd[b][:, f, h * 512:(h + 1) * 512], start=(f == 0), stop=(f == FT - 1))
                    last.then_inc(y_made, 1)
            pe.wait_ge(wts, 16)
            turn(0, 0)
            over_experts(pe, step)

        @block.vector
        def _(dve):
            def place(e, b):
                if not early(e):
                    dve.wait_ge(scattered, 16 * NC * (e - 1))
                for dst, name in ((now_g, "gather"), (now_s, "scatter"), (now_w, "gate")):
                    for_c = dst[b][:, :]
                    if name == "gate":
                        dve.tensor_copy(dst[b][:, 0:2], chosen[name][:, 0:2, bass.ds(e, 1)].rearrange("p c e -> p (c e)"))
                        dve.tensor_copy(dst[b][0:CAPS[1], 2:3], chosen[name][0:CAPS[1], 2, bass.ds(e, 1)]).then_inc(placed, 1)
                    else:
                        dve.tensor_copy(for_c, chosen[name][:, :, bass.ds(e, 1)].rearrange("p c e -> p (c e)")).then_inc(placed, 1)

            def step(e, b, more):
                if more:
                    place(e + 1, 1 - b)
                for f in range(FT):
                    dve.wait_ge(silued, FT * e + f + 1)
                    dve.wait_ge(up_made, FT * e + f + 1)
                    if f == 0 and not (isinstance(e, int) and e == 0):
                        dve.wait_ge(y_made, NC * e)
                    dve.tensor_tensor(hT[:, f, :], si[:, f % 2, :], pU[f % 2][:, 0:NTOK], ALU.mult).then_inc(h_ready, 1)
                if not early(e):
                    dve.wait_ge(scattered, 16 * NC * (e - 1))
                for c, (_, _, n) in enumerate(SLOT_TILES):
                    dve.wait_ge(y_made, NC * e + c + 1)
                    if c == 0:
                        dve.wait_ge(placed, 3 * e + 3)
                    dve.tensor_scalar(ys[b][c][0:n, :], pY[0:n, :], now_w[b][0:n, c:c + 1], None, ALU.mult
                                      ).then_inc(y_ready, 1)
            place(0, 0)
            over_experts(dve, step)


INPUTS = {
    "x_prompt": (1, GROUPS[0], D), "x_sample": (1, GROUPS[1], D), "attn_norm": (1, D), "w_in": (1, D, CH + CM),
    "conv_w": (1, 3, CH), "conv_b": (1, CH), "filt_w1": (1, FEAT, FH), "filt_b1": (1, FH), "filt_w2": (1, FH, FH),
    "filt_b2": (1, FH), "filt_w3": (1, FH, 4 * DH), "filt_freq": (1, FH), "filt_decay": (1, 2, 2, DH),
    "hyena_bias": (1, 2, DH), "q_a_norm": (1, QL), "w_uq": (1, QL, NH * QH), "kv_a_norm": (1, KVL),
    "w_ukv": (1, KVL, NH * (ND + VH)), "q_norm": (1, QH), "k_norm": (1, QH), "out_norm": (1, D), "w_out": (1, D, D),
    "mlp_norm": (1, D), "w_router": (1, D, E_N), "w_gate": (1, E_N, D, FE), "w_up": (1, E_N, D, FE),
    "w_down": (1, E_N, FE, D),
}
COLUMNS = {"attn_norm": P, "q_a_norm": P, "kv_a_norm": P, "out_norm": P, "filt_b1": FH, "filt_b2": FH, "filt_freq": FH}


def lay_out(name, a):
    a = np.ascontiguousarray(a)
    return np.ascontiguousarray(a.reshape(-1, COLUMNS[name]).T) if name in COLUMNS else a


def laid_shape(name):
    n = INPUTS[name][-1]
    return (COLUMNS[name], n // COLUMNS[name]) if name in COLUMNS else INPUTS[name]


SCRATCH = {
    "U": (U_ROWS, CH),
    "C": (T, CM),
    "QK": (2 * NH, QH, T),
    "V": (T, NH, VH),
    "YA": (T, DH), "YH": (T, DH),
    "F": (2 * GROUPS[0], 3 * DH),
    "G": (2 * GROUPS[0], DH),
    "XN": (T, D),
    "LG": (E_N, T),
}
PHASES = ["project", "latent", "attend", "hyena", "merge", "moe"]


def build(nc, io, phases=PHASES):
    makers = {"project": project, "latent": latent, "attend": attend, "hyena": hyena,
              "merge": merge, "moe": moe}
    TAKEN.clear()
    for name in phases:
        makers[name](nc, io)
        if name == "attend":
            clear_semaphores(nc)


def kernel(**inputs):
    import concourse.bacc as bacc
    from concourse.bass_utils import run_bass_kernel_spmd

    nc = bacc.Bacc("TRN2", target_bir_lowering=False, num_devices=1)
    arrays = {"in_" + name: lay_out(name, inputs[name]) for name in INPUTS}
    io = {name: nc.dram_tensor("in_" + name, laid_shape(name), F32, kind="ExternalInput").ap() for name in INPUTS}
    for name, a in tables().items():
        arrays[name] = a
        io[name] = nc.dram_tensor(name, a.shape, F32, kind="ExternalInput").ap()
    for name, shape in SCRATCH.items():
        io[name] = nc.dram_tensor("s_" + name, shape, F32, kind="Internal").ap()
    for name, L in (("y_prompt", GROUPS[0]), ("y_sample", GROUPS[1])):
        io[name] = nc.dram_tensor(name, (1, L, D), F32, kind="ExternalOutput").ap()
    build(nc, io)
    r = run_bass_kernel_spmd(nc, [arrays], core_ids=[0])
    return r.results[0]["y_prompt"], r.results[0]["y_sample"]
```

```python
import math
from contextlib import ExitStack

import numpy as np
import concourse.bass as bass
from concourse import mybir

F32, F16, BF16 = mybir.dt.float32, mybir.dt.float16, mybir.dt.bfloat16
I32, U32 = mybir.dt.int32, mybir.dt.uint32
ALU = mybir.AluOpType
ACT = mybir.ActivationFunctionType
AX = mybir.AxisListType

P = 128
D = 1024
KD = D // P
GROUPS = (2048, 256)
T = sum(GROUPS)
NT = T // P
NTP = GROUPS[0] // P
DH = 512
CH = 3 * DH
QL, KVL, RD = 256, 128, 32
CM = QL + KVL + RD
NH, ND, QH, VH = 8, 64, 96, 64
E_N, FE = 16, 512
FEAT, FH = 33, 64
N2 = 64
EPS = 1e-6
CAPS = tuple(2 * n // E_N for n in GROUPS)


def dft_tables(L):
    N = 2 * L
    N1, T1 = N // N2, L // N2
    J = P // T1
    q = np.arange(N1)
    k1 = np.where(q == 1, N1 // 2, q // 2)
    imag = (q > 1) & (q % 2 == 1)
    t1 = np.arange(T1)
    ang = 2 * np.pi * np.outer(t1, k1) / N1
    fwd = np.where(imag, -np.sin(ang), np.cos(ang))
    inv = fwd.T * np.where(q > 1, 2.0, 1.0)[:, None] / N
    first = np.zeros((2, J, T1, J // 2, N1))
    last = np.zeros((2, J // 2, N1, J, T1))
    for h in range(2):
        for jj in range(J // 2):
            first[h, h * (J // 2) + jj, :, jj, :] = fwd
            last[h, jj, :, h * (J // 2) + jj, :] = inv
    nb = N1 // 2 + 1
    t2 = np.arange(N2)[:, None]
    spec = np.zeros((nb, P, 5, P))
    for b in range(nb):
        k = b + N1 * np.arange(N2)[None, :]
        th = 2 * np.pi * ((t2 * k) % N) / N
        c, s = np.cos(th), np.sin(th)
        re = np.concatenate([c, s], 0)
        im = np.concatenate([-s, c], 0)
        gre = np.concatenate([c.T, -s.T], 0)
        gim = np.concatenate([s.T, c.T], 0)
        if b == 0:
            re[N2:] = im[N2:] = 0
            gim[:] = 0
        if b == nb - 1:
            re[N2:], im[N2:] = re[:N2].copy(), im[:N2].copy()
            re[:N2] = im[:N2] = 0
            gim, gre = gre.copy(), np.zeros_like(gre)
        inv1 = np.concatenate([gre, gim], 1)
        swapped = np.concatenate([inv1[N2:], inv1[:N2]], 0)
        order = np.arange(P).reshape(2, N2).T.reshape(-1)
        spec[b, :, 0] = np.concatenate([re, im], 1)[order]
        spec[b, :, 1] = inv1[:, order]
        spec[b, :, 2] = swapped[:, order]
        spec[b, :, 3] = np.concatenate([re, re], 1)[order]
        spec[b, :, 4] = np.concatenate([im, -im], 1)[order]
    return (first.reshape(2, P, P).transpose(1, 0, 2), last.reshape(2, P, P).transpose(1, 0, 2), spec)


def token_order(L):
    T1 = L // N2
    J = P // T1
    i, j, t1 = np.meshgrid(np.arange(N2 // J), np.arange(J), np.arange(T1), indexing="ij")
    return (64 * t1 + i * J + j).reshape(-1)


def feature_tables(L):
    f = np.float32
    t_idx = np.arange(L, dtype=f)[:, None]
    t = t_idx / f(L - 1)
    bands = np.linspace(1e-4, 15, 16, dtype=f)
    ang = f(2.0 * math.pi) * bands * t_idx / f(L)
    feats = np.concatenate([t, np.cos(ang), -np.sin(ang)], axis=-1).astype(f)
    order = token_order(L)
    return feats[order].T, -t[order, 0].reshape(-1, P).T


def tables():
    out = {}
    pos = np.concatenate([np.arange(L, dtype=np.float32) for L in GROUPS])
    inv = np.float32(10000.0) ** (-np.arange(0, RD, 2, dtype=np.float32) / np.float32(RD))
    ang = (pos[:, None] * inv).astype(np.float32)
    out["rope"] = np.concatenate([np.cos(ang), np.cos(ang), -np.sin(ang), np.sin(ang)], 1)
    out["eye"] = np.eye(P)
    for g, L in enumerate(GROUPS):
        out[f"first{g}"], out[f"last{g}"], out[f"spec{g}"] = dft_tables(L)
        feats, out[f"negt{g}"] = feature_tables(L)
        out["feats"] = np.concatenate([out["feats"], feats], 1) if g else feats
    return {"tab_" + k: np.ascontiguousarray(v, dtype=np.float32) for k, v in out.items()}


def in_pairs(eng, n, step):
    step(0, 0)
    step(1, 1)
    if n > 2:
        with eng.Fori(1, n // 2) as i:
            step(2 * i, 0)
            step(2 * i + 1, 1)


def early(t):
    return isinstance(t, int) and t < 2


def rows(t, n=P):
    return bass.ds(t * n, n)


TAKEN = []


def semaphores(nc, ctx, prefix):
    def sem(name):
        TAKEN.append(nc.alloc_semaphore(prefix + name))
        return TAKEN[-1]
    return sem


def clear_semaphores(nc):
    nc.clear_and_free_semaphores(list(TAKEN))
    nc.all_engine_barrier()
    TAKEN.clear()


TWO_PI = (6.28125, 0.0019340515136718750, 2 * math.pi - 6.28125 - 0.0019340515136718750)
ROUND = 1.5 * 2.0 ** 23
PI_BELOW = 3.1415925


def features(nc, io, load_weights):
    W = T // 2
    CHUNKS = [(c, min(c + 512, W)) for c in range(0, W, 512)]
    with ExitStack() as ctx:
        def sb(name, shape):
            return ctx.enter_context(nc.sbuf_tensor(f"ff_{name}", shape, F32))

        sem = semaphores(nc, ctx, "ff_")

        feats = sb("feats", [2 * FEAT, W])
        w1, w2 = sb("w1", [2 * FEAT, P]), sb("w2", [P, P])
        b1, b2, fr = sb("b1", [P, 1]), sb("b2", [P, 1]), sb("fr", [P, 1])
        arg, turns, h1, h2 = sb("arg", [P, W]), sb("turns", [P, W]), sb("h1", [P, W]), sb("h2", [P, W])
        pA = ctx.enter_context(nc.psum_tensor("ff_pA", [P, 3, 512], F32))
        cleared, loaded, made, chain, sines = sem("cleared"), sem("loaded"), sem("made"), sem("chain"), sem("sines")
        stored = sem("stored")
        layers = ((w1, feats, b1, h1), (w2, h1, b2, h2))
        STEPS = 6 + len(CHUNKS)
        LOADS = 16 * 2 * 6
        block = ctx.enter_context(nc.Block())

        @block.sync
        def _(sp):
            sp.wait_ge(cleared, 2)
            for half in range(2):
                f, h = slice(half * FEAT, (half + 1) * FEAT), slice(half * FH, (half + 1) * FH)
                for dst, src in ((feats[f, :], io["tab_feats"][:, half * W:(half + 1) * W]), (w1[f, h], io["filt_w1"][0]),
                                 (w2[h, h], io["filt_w2"][0]), (b1[h, :], io["filt_b1"]), (b2[h, :], io["filt_b2"]),
                                 (fr[h, :], io["filt_freq"])):
                    sp.dma_start(dst, src).then_inc(loaded, 16)
            load_weights(sp)
            sp.wait_ge(sines, 2)
            for half in range(2):
                sp.dma_start(io["H"][:, half * W:(half + 1) * W], h2[half * FH:(half + 1) * FH, :]).then_inc(stored, 16)
            sp.wait_ge(stored, 32)

        @block.tensor
        def _(pe):
            pe.wait_ge(loaded, LOADS)
            for n, (w, x, _, _) in enumerate(layers):
                if n:
                    pe.wait_ge(sines, n)
                for m, (c0, c1) in enumerate(CHUNKS):
                    last = pe.matmul(pA[:, m, 0:c1 - c0], w[:, :], x[:, c0:c1], start=True, stop=True)
                last.then_inc(made, 1)

        @block.vector
        def _(dve):
            dve.memset(w1[:, :], 0.0).then_inc(cleared, 1)
            dve.memset(w2[:, :], 0.0).then_inc(cleared, 1)
            for n, (_, _, b, out) in enumerate(layers):
                dve.wait_ge(made, n + 1)
                if n:
                    dve.wait_ge(sines, n)
                for m, (c0, c1) in enumerate(CHUNKS):
                    dve.tensor_scalar(arg[:, c0:c1], pA[:, m, 0:c1 - c0], b[:, 0:1], fr[:, 0:1], ALU.add, ALU.mult
                                      ).then_inc(chain, 1)
                at = STEPS * n + len(CHUNKS)
                dve.wait_ge(chain, at)
                dve.tensor_scalar(turns[:, :], arg[:, :], 1 / (2 * math.pi), ROUND, ALU.mult, ALU.add).then_inc(chain, 1)
                dve.wait_ge(chain, at + 1)
                dve.tensor_scalar(turns[:, :], turns[:, :], ROUND, None, ALU.subtract).then_inc(chain, 1)
                for m, part in enumerate(TWO_PI):
                    dve.wait_ge(chain, at + 2 + m)
                    dve.scalar_tensor_tensor(arg[:, :], turns[:, :], -part, arg[:, :], ALU.mult, ALU.add).then_inc(chain, 1)
                dve.wait_ge(chain, at + 5)
                dve.tensor_scalar(arg[:, :], arg[:, :], PI_BELOW, -PI_BELOW, ALU.min, ALU.max).then_inc(chain, 1)

        @block.scalar
        def _(act):
            for n, (_, _, _, out) in enumerate(layers):
                act.wait_ge(chain, STEPS * (n + 1))
                act.activation(out[:, :], arg[:, :], ACT.Sin).then_inc(sines, 1)


def project(nc, io):
    with ExitStack() as ctx:
        w = ctx.enter_context(nc.sbuf_tensor("pj_w", [P, KD, CH + CM], F32))
        sem = semaphores(nc, ctx, "pj_")
        w_in = [sem(f"w_in{k}") for k in range(KD)]
        gain = ctx.enter_context(nc.sbuf_tensor("pj_gain", [P, KD], F32))
        eye = ctx.enter_context(nc.sbuf_tensor("pj_eye", [P, P], F32))
        x = ctx.enter_context(nc.sbuf_tensor("pj_x", [P, 2, D], F32))
        wts = sem("wts")
        x_in = [sem(f"x_in{b}") for b in range(2)]

        def load_weights(eng):
            eng.dma_start(eye[:, :], io["tab_eye"]).then_inc(wts, 16)
            eng.dma_start(gain[:, :], io["attn_norm"]).then_inc(wts, 16)
            for t in range(2):
                eng.dma_start(x[:, t, :], io["x_prompt"][0, rows(t), :]).then_inc(x_in[t], 16)
            for k in range(KD):
                eng.dma_start(w[:, k, :], io["w_in"][0, k * P:(k + 1) * P, :]).then_inc(w_in[k], 16)
        features(nc, io, load_weights)
        project_tiles(nc, io, {"w": w, "w_in": w_in, "gain": gain, "eye": eye, "x": x, "wts": wts, "x_in": x_in})


def project_tiles(nc, io, loaded):
    with ExitStack() as ctx:
        def sb(name, shape, dt=F32):
            return ctx.enter_context(nc.sbuf_tensor(name, shape, dt))

        sem = semaphores(nc, ctx, "")

        w, w_in, gain, eye, x, wts, x_in = (loaded[n] for n in ("w", "w_in", "gain", "eye", "x", "wts", "x_in"))
        zero = sb("pj_zero", [1, CH])
        taps = sb("pj_taps", [P, 4, CH])
        before, after = sb("pj_before", [P, 2, CH]), sb("pj_after", [P, 2, CH])
        mixed = sb("pj_mixed", [P, 2, CH])
        sq = sb("pj_sq", [P, D])
        ms = sb("pj_ms", [P, 2])
        mse = sb("pj_mse", [P, 2])
        mhalf = sb("pj_mhalf", [P, 1])
        eps = sb("pj_eps", [P, 1])
        rstd = sb("pj_rstd", [P, 2])
        xn = sb("pj_xn", [P, 2, D])
        xT = [sb(f"pj_xT{b}", [P, KD, P]) for b in range(2)]
        u = sb("pj_u", [P, 2, CH + CM])
        pT = ctx.enter_context(nc.psum_tensor("pj_pT", [P, KD, P], F32))
        pU = [ctx.enter_context(nc.psum_tensor(f"pj_pU{c}", [P, 512], F32)) for c in range(4)]
        widths = [DH, DH, DH, CM]

        scaled = sem("pj_scaled")
        squared = sem("pj_squared")
        with_eps = sem("pj_with_eps")
        have_rstd = sem("pj_have_rstd")
        normed = sem("pj_normed")
        turned = sem("pj_turned")
        xT_ready = sem("pj_xT_ready")
        u_done = sem("pj_u_done")
        u_moved = sem("pj_u_moved")
        zeroed = sem("pj_zeroed")
        u_out = [sem(f"pj_u_out{b}") for b in range(2)]
        taps_in = sem("pj_taps_in")
        shifted = [sem(f"pj_shifted{b}") for b in range(2)]
        scaled_pool, scaled_dve, summed = sem("pj_scaled_pool"), sem("pj_scaled_dve"), sem("pj_summed")
        z_out = [sem(f"pj_z_out{b}") for b in range(2)]

        block = ctx.enter_context(nc.Block())

        @block.sync
        def _(sp):
            for m in range(3):
                sp.dma_start(taps[:, m, :], io["conv_w"][0, m:m + 1, :].to_broadcast([P, CH])).then_inc(taps_in, 16)
            sp.dma_start(taps[:, 3, :], io["conv_b"].to_broadcast([P, CH])).then_inc(taps_in, 16)

            def load(t, b, src):
                sp.wait_ge(normed, t - 1)
                sp.dma_start(x[:, b, :], src).then_inc(x_in[b], 16)

            def store_z(t, b):
                sp.wait_ge(summed, 2 * t + 2)
                sp.dma_start(io["Z"][rows(t), :], mixed[:, b, :]).then_inc(z_out[b], 16)

            def pass_on(t, b):
                if not early(t):
                    store_z(t - 2, b)
                sp.wait_ge(u_moved, 4 * t + 4)
                if isinstance(t, int) and t in (0, NTP):
                    if t:
                        sp.dma_start(after[P - 1:P, 1 - b, :], zero[:, :]).then_inc(shifted[1 - b], 16)
                    sp.dma_start(before[0:1, b, :], zero[:, :]).then_inc(shifted[b], 16)
                else:
                    sp.dma_start(after[P - 1:P, 1 - b, :], u[0:1, b, 0:CH]).then_inc(shifted[1 - b], 16)
                    sp.dma_start(before[0:1, b, :], u[P - 1:P, 1 - b, 0:CH]).then_inc(shifted[b], 16)
                sp.dma_start(before[1:P, b, :], u[0:P - 1, b, 0:CH]).then_inc(shifted[b], 16)
                sp.dma_start(after[0:P - 1, b, :], u[1:P, b, 0:CH]).then_inc(shifted[b], 16)
                sp.dma_start(io["C"][rows(t), :], u[:, b, CH:]).then_inc(u_out[b], 16)

            sp.wait_ge(zeroed, 3)
            for t in range(2):
                load(t + 2, t, io["x_prompt"][0, rows(t + 2), :])
                pass_on(t, t)
            with sp.Fori(1, NTP // 2 - 1) as i:
                for b in range(2):
                    load(2 * i + b + 2, b, io["x_prompt"][0, rows(2 * i + b + 2), :])
                    pass_on(2 * i + b, b)
            for t in range(NTP - 2, NT):
                if t + 2 < NT:
                    load(t + 2, t % 2, io["x_sample"][0, rows(t + 2 - NTP), :])
                pass_on(t, t % 2)
            sp.dma_start(after[P - 1:P, 1, :], zero[:, :]).then_inc(shifted[1], 16)
            for t in (NT - 2, NT - 1):
                store_z(t, t % 2)
            for b in range(2):
                sp.wait_ge(u_out[b], 8 * NT)
                sp.wait_ge(z_out[b], 8 * NT)

        @block.gpsimd
        def _(pool):
            pool.memset(zero[:, :], 0.0).then_inc(zeroed, 1)
            pool.memset(mhalf[:, :], -0.5).then_inc(zeroed, 1)
            pool.memset(eps[:, :], EPS).then_inc(zeroed, 1)
            pool.wait_ge(zeroed, 3)
            def root(t, b):
                pool.wait_ge(squared, t + 1)
                if not early(t):
                    pool.wait_ge(normed, t - 1)
                pool.tensor_tensor(mse[:, b:b + 1], ms[:, b:b + 1], eps[:, 0:1], ALU.add).then_inc(with_eps, 1)
                pool.wait_ge(with_eps, t + 1)
                pool.tensor_tensor(rstd[:, b:b + 1], mse[:, b:b + 1], mhalf[:, 0:1], ALU.pow).then_inc(have_rstd, 1)

            def convolve(t, b):
                pool.wait_ge(shifted[b], 32 * t - 32 * b + 64)
                pool.tensor_tensor(before[:, b, :], before[:, b, :], taps[:, 0, :], ALU.mult).then_inc(scaled_pool, 1)
                pool.wait_ge(scaled_pool, 2 * t + 1)
                pool.tensor_tensor(before[:, b, :], before[:, b, :], taps[:, 3, :], ALU.add).then_inc(scaled_pool, 1)

            root(0, 0)
            root(1, 1)
            pool.wait_ge(taps_in, 64)
            root(2, 0)
            root(3, 1)
            convolve(0, 0)
            with pool.Fori(2, NT // 2) as i:
                for b in range(2):
                    root(2 * i + b, b)
                    convolve(2 * i + b - 3, 1 - b)
            for t in range(NT - 3, NT):
                convolve(t, t % 2)

        @block.scalar
        def _(act):
            def step(t, b):
                act.wait_ge(x_in[b], 8 * t - 8 * b + 16)
                if not (isinstance(t, int) and t == 0):
                    act.wait_ge(squared, t)
                if not early(t):
                    act.wait_ge(have_rstd, t - 1)
                act.activation(sq[:, :], x[:, b, :], ACT.Square, scale=D ** -0.5,
                               accum_out=ms[:, b:b + 1]).then_inc(squared, 1)
                act.wait_ge(turned, t + 1)
                if not early(t):
                    act.wait_ge(u_done, 4 * t - 4)
                for h in range(2):
                    act.activation(xT[b][:, 4 * h:4 * h + 4, :], pT[:, 4 * h:4 * h + 4, :],
                                   ACT.Copy).then_inc(xT_ready, 1)
            in_pairs(act, NT, step)

        @block.tensor
        def _(pe):
            def turn(t, b):
                pe.wait_ge(normed, t + 1)
                if not (isinstance(t, int) and t == 0):
                    pe.wait_ge(xT_ready, 2 * t)
                for k in range(KD):
                    last = pe.transpose(pT[:, k, :], xn[:, b, k * P:(k + 1) * P], eye[:, :])
                last.then_inc(turned, 1)

            def products(t, b):
                pe.wait_ge(xT_ready, 2 * t + 2)
                for c in range(4):
                    if not (isinstance(t, int) and t == 0):
                        pe.wait_ge(u_moved, 4 * t - 3 + c)
                    for k in range(KD):
                        if isinstance(t, int) and t == 0 and c == 0:
                            pe.wait_ge(scaled, k + 1)
                        last = pe.matmul(pU[c][:, 0:widths[c]], xT[b][:, k, :],
                                         w[:, k, c * DH:c * DH + widths[c]], start=(k == 0), stop=(k == KD - 1))
                    last.then_inc(u_done, 1)

            pe.wait_ge(wts, 32)
            turn(0, 0)

            def step(t, b):
                turn(t + 1, 1 - b)
                products(t, b)
            step(0, 0)
            step(1, 1)
            with pe.Fori(1, NT // 2 - 1) as i:
                step(2 * i, 0)
                step(2 * i + 1, 1)
            step(NT - 2, 0)
            products(NT - 1, 1)

        @block.vector
        def _(dve):
            def norm(t, b):
                dve.wait_ge(have_rstd, t + 1)
                if not early(t):
                    dve.wait_ge(turned, t - 1)
                dve.tensor_scalar(xn[:, b, :], x[:, b, :], rstd[:, b:b + 1], None, ALU.mult).then_inc(normed, 1)

            def move(t, b):
                if not early(t):
                    dve.wait_ge(u_out[b], 8 * t - 8 * b)
                    dve.wait_ge(scaled_dve, 2 * t - 2)
                if not (isinstance(t, int) and t == 0):
                    dve.wait_ge(shifted[1 - b], 32 * t + 32 * b - 16)
                for c in range(4):
                    dve.wait_ge(u_done, 4 * t + c + 1)
                    dve.tensor_copy(u[:, b, c * DH:c * DH + widths[c]], pU[c][:, 0:widths[c]]).then_inc(u_moved, 1)

            def convolve(t, b):
                dve.wait_ge(shifted[b], 32 * t - 32 * b + 64)
                if not early(t):
                    dve.wait_ge(z_out[b], 8 * t - 8 * b)
                dve.tensor_tensor(mixed[:, b, :], u[:, b, 0:CH], taps[:, 1, :], ALU.mult).then_inc(scaled_dve, 1)
                dve.tensor_tensor(after[:, b, :], after[:, b, :], taps[:, 2, :], ALU.mult).then_inc(scaled_dve, 1)
                dve.wait_ge(scaled_dve, 2 * t + 2)
                dve.tensor_tensor(mixed[:, b, :], mixed[:, b, :], after[:, b, :], ALU.add).then_inc(summed, 1)
                dve.wait_ge(scaled_pool, 2 * t + 2)
                dve.wait_ge(summed, 2 * t + 1)
                dve.tensor_tensor(mixed[:, b, :], mixed[:, b, :], before[:, b, :], ALU.add).then_inc(summed, 1)

            norm(0, 0)
            dve.wait_ge(wts, 32)
            for k in range(KD):
                dve.wait_ge(w_in[k], 16)
                dve.tensor_scalar(w[:, k, :], w[:, k, :], gain[:, k:k + 1], None, ALU.mult).then_inc(scaled, 1)
            dve.wait_ge(taps_in, 64)
            norm(1, 1)

            norm(2, 0)
            move(0, 0)
            norm(3, 1)
            move(1, 1)
            convolve(0, 0)
            with dve.Fori(1, NT // 2 - 1) as i:
                for b in range(2):
                    norm(2 * i + b + 2, b)
                    move(2 * i + b, b)
                    convolve(2 * i + b - 1, 1 - b)
            for t in (NT - 2, NT - 1):
                move(t, t % 2)
                convolve(t - 1, 1 - t % 2)
            convolve(NT - 1, 1)


def latent(nc, io):
    H2 = 2 * NH
    with ExitStack() as ctx:
        def sb(name, shape, dt=F32):
            return ctx.enter_context(nc.sbuf_tensor(name, shape, dt))

        sem = semaphores(nc, ctx, "lt_")

        wq = sb("lt_wq", [P, 2, NH * QH])
        wkv = sb("lt_wkv", [P, NH * (ND + VH)])
        qan = sb("lt_qan", [P, 2])
        kvan = sb("lt_kvan", [P, 1])
        eye = sb("lt_eye", [P, P])
        gain = sb("lt_gain", [P, 2, QH])
        eps = sb("lt_eps", [P, H2])
        mhalf = sb("lt_mhalf", [P, H2])
        c = sb("lt_c", [P, NT, CM])
        rope = sb("lt_rope", [P, NT, 2 * RD])
        size, size_in = sb("lt_size", [P, 2, 2]), sb("lt_size_in", [P, 2])
        backs = sb("lt_backs", [P, 2, QH])
        junk = sb("lt_junk", [P, QL])
        ms = sb("lt_ms", [P, 2, 2])
        mse = sb("lt_mse", [P, 2, 2])
        rc = sb("lt_rc", [P, 2, 2])
        cn = sb("lt_cn", [P, 2, QL + KVL])
        cT = [sb(f"lt_cT{b}", [P, 3, P]) for b in range(2)]
        qk = sb("lt_qk", [P, 2, H2, QH])
        sq = sb("lt_sq", [P, H2, QH])
        ss = sb("lt_ss", [P, H2])
        sse = sb("lt_sse", [P, H2])
        rh = sb("lt_rh", [P, H2])
        ra = sb("lt_ra", [P, H2, RD])
        rb = sb("lt_rb", [P, H2, RD])
        v = sb("lt_v", [P, 2, NH, VH])
        hT = sb("lt_hT", [QH, 2, H2, P])
        pT = ctx.enter_context(nc.psum_tensor("lt_pT", [P, 512], F32))
        pQ = ctx.enter_context(nc.psum_tensor("lt_pQ", [P, 1024], F32))
        pK = ctx.enter_context(nc.psum_tensor("lt_pK", [P, NH, ND + VH], F32))
        pH = [ctx.enter_context(nc.psum_tensor(f"lt_pH{b}", [P, 4, P], F32)) for b in range(2)]

        wts, scaled, consts = sem("wts"), sem("scaled"), sem("consts")
        c_in, c_rest_in = sem("c_in"), sem("c_rest_in")
        squared, with_eps, have_rc, c_normed = sem("squared"), sem("with_eps"), sem("have_rc"), sem("c_normed")
        turned, cT_ready, made = sem("turned"), sem("cT_ready"), sem("made")
        q_moved, k_moved, rope_moved, heads_sq = sem("q_moved"), sem("k_moved"), sem("rope_moved"), sem("heads_sq")
        summed, with_eps2, have_rh = sem("summed"), sem("with_eps2"), sem("have_rh")
        chain, roped = sem("chain"), sem("roped")
        heads_turned, hT_ready = sem("heads_turned"), sem("hT_ready")
        out_done = [sem(f"out_done{b}") for b in range(2)]
        sized, sized_out = sem("sized"), sem("sized_out")
        WTS = 16 * 9

        block = ctx.enter_context(nc.Block())

        @block.sync
        def _(sp):
            sp.dma_start(c[:, 0:3, :], io["C"][0:3 * P, :].rearrange("(n p) c -> p n c", p=P)).then_inc(c_in, 16)
            sp.dma_start(eye[:, :], io["tab_eye"]).then_inc(wts, 16)
            sp.dma_start(qan[:, :], io["q_a_norm"]).then_inc(wts, 16)
            sp.dma_start(kvan[:, :], io["kv_a_norm"]).then_inc(wts, 16)
            sp.dma_start(gain[:, 0, :], io["q_norm"].to_broadcast([P, QH])).then_inc(wts, 16)
            sp.dma_start(gain[:, 1, :], io["k_norm"].to_broadcast([P, QH])).then_inc(wts, 16)
            sp.dma_start(wkv[:, :], io["w_ukv"][0]).then_inc(wts, 16)
            for k in range(2):
                sp.dma_start(wq[:, k, :], io["w_uq"][0, k * P:(k + 1) * P, :]).then_inc(wts, 16)

            sp.dma_start(rope[:, :, :], io["tab_rope"].rearrange("(n p) c -> p n c", p=P)).then_inc(wts, 16)
            sp.dma_start(c[:, 3:, :], io["C"][3 * P:, :].rearrange("(n p) c -> p n c", p=P)).then_inc(c_rest_in, 16)
            sp.wait_ge(sized, 6)
            sp.dma_start(io["S"], size_in[:, 0:1]).then_inc(sized_out, 16)
            sp.wait_ge(sized_out, 16)

        def columns(t, n0, n1):
            return c[:, bass.ds(t, 1), n0:n1].rearrange("p n c -> p (n c)")

        def live(t):
            return not isinstance(t, int) or 0 <= t < NT

        def first(t):
            return isinstance(t, int) and t == 0

        def over_steps(eng, step):
            for t in range(-3, 2):
                step(t, t % 2)
            with eng.Fori(1, NT // 2 - 2) as i:
                step(2 * i, 0)
                step(2 * i + 1, 1)
            for t in range(NT - 4, NT):
                step(t, t % 2)

        @block.gpsimd
        def _(pool):
            pool.memset(eps[:, :], EPS).then_inc(consts, 1)
            pool.memset(mhalf[:, :], -0.5).then_inc(consts, 1)
            pool.wait_ge(consts, 2)

            def root_c(t, b):
                pool.wait_ge(squared, 2 * t + 2)
                if not early(t):
                    pool.wait_ge(c_normed, 2 * t - 2)
                pool.tensor_tensor(mse[:, b, :], ms[:, b, :], eps[:, 0:2], ALU.add).then_inc(with_eps, 1)
                pool.wait_ge(with_eps, t + 1)
                pool.tensor_tensor(rc[:, b, :], mse[:, b, :], mhalf[:, 0:2], ALU.pow).then_inc(have_rc, 1)

            def root_heads(t, b):
                for g in range(2):
                    heads = slice(NH * g, NH * g + NH)
                    pool.wait_ge(summed, 2 * t + g + 1)
                    pool.tensor_tensor(sse[:, heads], ss[:, heads], eps[:, heads], ALU.add).then_inc(with_eps2, 1)
                    pool.wait_ge(with_eps2, 2 * t + g + 1)
                    if g == 0 and not first(t):
                        pool.wait_ge(chain, 7 * t - 4)
                    pool.tensor_tensor(rh[:, heads], sse[:, heads], mhalf[:, heads], ALU.pow).then_inc(have_rh, 1)

            def step(t, b):
                if live(t):
                    root_heads(t, b)
                if live(t + 3):
                    root_c(t + 3, 1 - b)
            over_steps(pool, step)

        @block.scalar
        def _(act):
            def square(t, b):
                if first(t):
                    act.wait_ge(c_in, 16)
                if isinstance(t, int) and t == 3:
                    act.wait_ge(c_rest_in, 16)
                if not early(t):
                    act.wait_ge(have_rc, t - 1)
                if not first(t):
                    act.wait_ge(squared, 2 * t)
                act.activation(junk[:, :], columns(t, 0, QL), ACT.Square, scale=QL ** -0.5,
                               accum_out=ms[:, b, 0:1]).then_inc(squared, 1)
                act.wait_ge(squared, 2 * t + 1)
                act.activation(junk[:, 0:KVL], columns(t, QL, QL + KVL), ACT.Square, scale=KVL ** -0.5,
                               accum_out=ms[:, b, 1:2]).then_inc(squared, 1)

            def copy_cT(t, b):
                act.wait_ge(turned, t + 1)
                if not early(t):
                    act.wait_ge(made, 2 * t - 2)
                act.activation(cT[b][:, :, :], pT[:, 0:3 * P].rearrange("p (k t) -> p k t", k=3),
                               ACT.Copy).then_inc(cT_ready, 1)

            def move_heads(t, b):
                act.wait_ge(made, 2 * t + 1)
                if not early(t):
                    act.wait_ge(heads_turned, 4 * t - 4)
                    act.wait_ge(out_done[b], 16 * t - 16 * b)
                act.activation(qk[:, b, 0:NH, :], pQ[:, 0:NH * QH].rearrange("p (h d) -> p h d", h=NH),
                               ACT.Copy).then_inc(q_moved, 1)
                act.wait_ge(made, 2 * t + 2)
                act.activation(qk[:, b, NH:, 0:ND], pK[:, :, 0:ND], ACT.Copy).then_inc(k_moved, 1)
                act.activation(v[:, b, :, :], pK[:, :, ND:], ACT.Copy).then_inc(k_moved, 1)

            def square_heads(t, b):
                act.wait_ge(q_moved, t + 1)
                act.wait_ge(k_moved, 2 * t + 2)
                act.wait_ge(rope_moved, t + 1)
                if not first(t):
                    act.wait_ge(summed, 2 * t)
                act.activation(sq[:, :, :], qk[:, b, :, :], ACT.Square, scale=QH ** -0.5).then_inc(heads_sq, 1)

            def put(t, b):
                if not early(t):
                    act.wait_ge(out_done[b], 16 * t - 16 * b)
                for n in range(4):
                    act.wait_ge(heads_turned, 4 * t + n + 1)
                    act.activation(hT[:, b, 4 * n:4 * n + 4, :], pH[n % 2][0:QH, :, :], ACT.Copy).then_inc(hT_ready, 1)
                act.wait_ge(hT_ready, 4 * t + 4)
                act.dma_start(io["QK"][:, :, rows(t)].rearrange("h d t -> d h t"), hT[:, b, :, :]).then_inc(out_done[b], 16)
                act.dma_start(io["V"][rows(t), :, :], v[:, b, :, :]).then_inc(out_done[b], 16)

            def step(t, b):
                if live(t + 1):
                    move_heads(t + 1, 1 - b)
                if live(t + 2):
                    copy_cT(t + 2, b)
                if live(t + 1):
                    square_heads(t + 1, 1 - b)
                if live(t + 3):
                    square(t + 3, 1 - b)
                if live(t):
                    put(t, b)

            over_steps(act, step)
            for b in range(2):
                act.wait_ge(out_done[b], 16 * NT)

        @block.tensor
        def _(pe):
            pe.wait_ge(wts, WTS)
            pe.wait_ge(scaled, 3)

            def turn(t, b):
                pe.wait_ge(c_normed, 2 * t + 2)
                if not first(t):
                    pe.wait_ge(cT_ready, t)
                for k in range(3):
                    last = pe.transpose(pT[:, k * P:(k + 1) * P], cn[:, b, k * P:(k + 1) * P], eye[:, :])
                last.then_inc(turned, 1)

            def make_heads(t, b):
                pe.wait_ge(cT_ready, t + 1)
                if not first(t):
                    pe.wait_ge(q_moved, t)
                for n0, n1 in ((0, 512), (512, NH * QH)):
                    for k in range(2):
                        last = pe.matmul(pQ[:, n0:n1], cT[b][:, k, :], wq[:, k, n0:n1], start=(k == 0), stop=(k == 1))
                last.then_inc(made, 1)
                if not first(t):
                    pe.wait_ge(k_moved, 2 * t)
                for n in range(2):
                    last = pe.matmul(pK[:, 4 * n:4 * n + 4, :].rearrange("p h d -> p (h d)"), cT[b][:, 2, :],
                                     wkv[:, n * 512:(n + 1) * 512], start=True, stop=True)
                last.then_inc(made, 1)

            def turn_heads(t, b):
                pe.wait_ge(roped, t + 1)
                for n in range(4):
                    if not (first(t) and n < 2):
                        pe.wait_ge(hT_ready, 4 * t + n - 1)
                    for m in range(4):
                        last = pe.transpose(pH[n % 2][0:QH, m, :], qk[:, b, 4 * n + m, :], eye[:, :])
                    last.then_inc(heads_turned, 1)

            def step(t, b):
                if live(t + 1):
                    make_heads(t + 1, 1 - b)
                if live(t + 2):
                    turn(t + 2, b)
                if live(t):
                    turn_heads(t, b)
            over_steps(pe, step)

        @block.vector
        def _(dve):
            dve.wait_ge(wts, WTS)
            for k in range(2):
                dve.tensor_scalar(wq[:, k, :], wq[:, k, :], qan[:, k:k + 1], None, ALU.mult).then_inc(scaled, 1)
            dve.tensor_scalar(wkv[:, :], wkv[:, :], kvan[:, 0:1], None, ALU.mult).then_inc(scaled, 1)

            dve.tensor_scalar(backs[:, :, :], gain[:, :, :], -1.0, None, ALU.mult).then_inc(sized, 1)
            dve.tensor_reduce(size[:, 0, :], gain[:, :, :], AX.X, ALU.max).then_inc(sized, 1)
            dve.wait_ge(sized, 2)
            dve.tensor_reduce(size[:, 1, :], backs[:, :, :], AX.X, ALU.max).then_inc(sized, 1)
            dve.wait_ge(sized, 3)
            dve.scalar_tensor_tensor(size_in[:, :], size[:, 0, :], 1e-18, size[:, 1, :], ALU.max, ALU.max).then_inc(sized, 1)
            dve.wait_ge(sized, 4)
            dve.reciprocal(size[:, 0, :], size_in[:, :]).then_inc(sized, 1)
            dve.wait_ge(sized, 5)
            for g in range(2):
                dve.tensor_scalar(gain[:, g, :], gain[:, g, :], size[:, 0, g:g + 1], None, ALU.mult).then_inc(scaled, 1)
            dve.scalar_tensor_tensor(size_in[:, 0:1], size_in[:, 0:1], QH ** -0.5, size_in[:, 1:2], ALU.mult, ALU.mult
                                     ).then_inc(sized, 1)
            dve.wait_ge(scaled, 5)

            def norm_c(t, b):
                dve.wait_ge(have_rc, t + 1)
                if not early(t):
                    dve.wait_ge(turned, t - 1)
                dve.tensor_scalar(cn[:, b, 0:QL], columns(t, 0, QL), rc[:, b, 0:1], None, ALU.mult).then_inc(c_normed, 1)
                dve.tensor_scalar(cn[:, b, QL:], columns(t, QL, QL + KVL), rc[:, b, 1:2], None, ALU.mult).then_inc(c_normed, 1)

            def share_rope(t, b):
                if not early(t):
                    dve.wait_ge(heads_turned, 4 * t - 4)
                dve.tensor_copy(qk[:, b, NH:, ND:], columns(t, QL + KVL, CM).unsqueeze(1).to_broadcast([P, NH, RD])
                                ).then_inc(rope_moved, 1)

            def add_squares(t, b):
                dve.wait_ge(heads_sq, t + 1)
                if not first(t):
                    dve.wait_ge(with_eps2, 2 * t)
                for g in range(2):
                    heads = slice(NH * g, NH * g + NH)
                    dve.tensor_reduce(ss[:, heads], sq[:, heads, :], AX.X, ALU.add).then_inc(summed, 1)

            def norm_heads(t, b):
                x = qk[:, b, :, :]
                turn = x[:, :, ND:]
                half = RD // 2
                for g in range(2):
                    part = x[:, NH * g:NH * g + NH, :]
                    dve.wait_ge(have_rh, 2 * t + g + 1)
                    dve.tensor_tensor(part, part, rh[:, NH * g:NH * g + NH].unsqueeze(2).to_broadcast([P, NH, QH]), ALU.mult
                                      ).then_inc(chain, 1)
                    dve.wait_ge(chain, 7 * t + 2 * g + 1)
                    dve.tensor_tensor(part, part, gain[:, g, :].unsqueeze(1).to_broadcast([P, NH, QH]), ALU.mult
                                      ).then_inc(chain, 1)
                dve.wait_ge(chain, 7 * t + 4)
                angles = rope[:, bass.ds(t, 1), :].rearrange("p n c -> p (n c)")
                cos, nsin, sin = (angles[:, n0:n1].unsqueeze(1).to_broadcast([P, H2, n1 - n0])
                                  for n0, n1 in ((0, RD), (RD, RD + half), (RD + half, 2 * RD)))
                dve.tensor_tensor(ra[:, :, :], turn, cos, ALU.mult).then_inc(chain, 1)
                dve.tensor_tensor(rb[:, :, 0:half], turn[:, :, half:], nsin, ALU.mult).then_inc(chain, 1)
                dve.tensor_tensor(rb[:, :, half:], turn[:, :, 0:half], sin, ALU.mult).then_inc(chain, 1)
                dve.wait_ge(chain, 7 * t + 7)
                dve.tensor_tensor(turn, ra[:, :, :], rb[:, :, :], ALU.add).then_inc(roped, 1)

            def step(t, b):
                if live(t):
                    add_squares(t, b)
                if live(t + 1):
                    share_rope(t + 1, 1 - b)
                if live(t + 2):
                    norm_c(t + 2, b)
                if live(t):
                    norm_heads(t, b)
            over_steps(dve, step)


MAX_UNIT = 32.0


TWO = 2


def attend(nc, io):
    attend_long(nc, io)
    attend_short(nc, io)


def attend_long(nc, io):
    L = GROUPS[0]
    QB = min(512, L)
    NQ, KT, QT = L // QB, L // P, L // P
    NS = NQ * KT
    LAG = 3
    AHEAD = 2
    CW = min(512, L)
    NC = L // CW
    SLOTS = QT * NC
    TQ = QB // P
    VC = 1 + 3 * VH
    VC2 = 1 + 2 * VH
    split_at = [1 + j // 2 for j in range(4 * NC)]
    slot_at = [8 + j * 45 // SLOTS for j in range(SLOTS)]
    turn_at = 55
    load_at = 14
    norm_at = 3
    store_at = 9
    v_at = [1, 3, 5, 7]
    with ExitStack() as ctx:
        def sb(name, shape, dt=F32):
            return ctx.enter_context(nc.sbuf_tensor("at_" + name, shape, dt))

        def ps(name, shape):
            return ctx.enter_context(nc.psum_tensor("at_" + name, shape, F32))

        sem = semaphores(nc, ctx, "at_")
        eye = sb("eye", [P, P])
        q, k, v = sb("q", [QH, L]), sb("k", [QH, L]), sb("v", [P, KT, VH])
        q1 = [sb(f"q1{b}", [QH + 1, L], F16) for b in range(2)]
        k1 = [sb(f"k1{b}", [QH + 1, L], F16) for b in range(2)]
        q2 = [sb(f"q2{b}", [QH, L], F16) for b in range(2)]
        k2 = [sb(f"k2{b}", [QH, L], F16) for b in range(2)]
        vv = [sb(f"vv{b}", [P, KT, VC], BF16) for b in range(2)]
        zero = sb("zero", [P, 1])
        scale = sb("scale", [P, 1])
        vr = sb("vr", [P, KT, VH])
        mxs = sb("mxs", [P, QT, NC])
        mx = sb("mx", [P, QT])
        nmx = sb("nmx", [QT, P], F16)
        pf = sb("pf", [P, 4, QB])
        p1 = [sb(f"p1{r}", [P, QB], F16) for r in range(4)]
        p2 = [sb(f"p2{r}", [P, QB], F16) for r in range(4)]
        rec = sb("rec", [P, 2, TQ])
        osum = sb("osum", [P, 2, TQ, VH])
        o = sb("o", [P, 2, QT, VH])
        pM = [ps(f"pM{r}", [P, 512]) for r in range(2)]
        pS = [ps(f"pS{r}", [P, 512]) for r in range(2)]
        pO = [ps(f"pO{r}", [P, 2, 512]) for r in range(2)]

        consts, ready = sem("consts"), sem("ready")
        qk_in, v_in, split, v_split = sem("qk_in"), sem("v_in"), sem("split"), sem("v_split")
        slot_made, max_ready, max_turned, max_moved, max_in = (
            sem("slot_made"), sem("max_ready"), sem("max_turned"), sem("max_moved"), sem("max_in"))
        p_free, pS_free, o_free, pM_free = sem("p_free"), sem("pS_free"), sem("o_free"), sem("pM_free")
        s_made, even_done, odd_done = sem("s_made"), sem("even_done"), sem("odd_done")
        inverted = sem("inverted")
        o_stored = [sem(f"o_stored{b}") for b in range(2)]

        block = ctx.enter_context(nc.Block())

        def over_heads(eng, head, peel=False):
            if peel:
                head(0, 0, True)
                head(1, 1, True)
            with eng.Fori(int(peel), NH // 2 - 1) as i:
                head(2 * i, 0, True)
                head(2 * i + 1, 1, True)
            head(NH - 2, 0, True)
            head(NH - 1, 1, False)

        def load(eng, h):
            eng.dma_start(q[:, :], io["QK"][h, :, 0:L]).then_inc(qk_in, 16)
            eng.dma_start(k[:, :], io["QK"][h + NH, :, 0:L]).then_inc(qk_in, 16)
            eng.dma_start(v[:, :, :], io["V"][0:L, h, :].rearrange("(k p) d -> p k d", p=P)).then_inc(v_in, 16)

        def rest(eng, h, b, n):
            r = (b * NS + n) % 4
            eng.wait_ge(p_free, NS * h + n + 1)
            eng.wait_ge(pS_free, NS * h + n + 3)
            eng.tensor_tensor(p2[r][:, :], pf[:, r, :], p1[r][:, :], ALU.subtract).then_inc(
                odd_done if n % 2 else even_done, 1)

        def rest_ahead(eng, h, b, n, more):
            if n + AHEAD < NS:
                rest(eng, h, b, n + AHEAD)
            elif more:
                rest(eng, h + 1, 1 - b, n + AHEAD - NS)

        @block.sync
        def _(sp):
            sp.dma_start(eye[:, :], io["tab_eye"]).then_inc(consts, 16)
            sp.dma_start(scale[:, :], io["S"]).then_inc(consts, 16)
            load(sp, 0)

            def put_max(h, b):
                sp.wait_ge(max_moved, h + 1)
                sp.dma_start(q1[b][QH:QH + 1, :], nmx[:, :]).then_inc(max_in, 16)
            with sp.Fori(0, NH // 2) as i:
                put_max(2 * i, 0)
                put_max(2 * i + 1, 1)
            sp.wait_ge(max_in, 16 * NH)

        @block.gpsimd
        def _(pool):
            pool.memset(zero[:, :], 0.0).then_inc(ready, 1)
            pool.wait_ge(ready, 1)
            for b in range(2):
                pool.memset(k1[b][QH:QH + 1, :], MAX_UNIT).then_inc(ready, 1)
                pool.wait_ge(ready, 2 * b + 2)
                pool.memset(vv[b][:, :, 0:1], 1.0).then_inc(ready, 1)
                pool.wait_ge(ready, 2 * b + 3)

            def split_v(h, b, m):
                parts = vv[b][:, :, 1:].rearrange("p k (s d) -> p s k d", s=3)
                pool.wait_ge(v_split, 4 * h + m) if m else pool.wait_ge(v_in, 16 * h + 16)
                nil = zero[:, :].unsqueeze(2).to_broadcast([P, KT, VH])
                if m == 0:
                    ins = pool.tensor_tensor(parts[:, 0, :, :], v[:, :, :], nil, ALU.add)
                elif m == 1:
                    ins = pool.tensor_tensor(vr[:, :, :], v[:, :, :], parts[:, 0, :, :], ALU.subtract)
                elif m == 2:
                    ins = pool.tensor_tensor(parts[:, 1, :, :], vr[:, :, :], nil, ALU.add)
                else:
                    ins = pool.tensor_tensor(parts[:, 2, :, :], vr[:, :, :], parts[:, 1, :, :], ALU.subtract)
                ins.then_inc(v_split, 1)

            def store(h, b):
                pool.wait_ge(o_free, NQ * h + NQ + 2)
                pool.dma_start(io["YA"][0:L, bass.ds(h * VH, VH)].rearrange("(k p) d -> p k d", p=P),
                               o[:, b, :, :]).then_inc(o_stored[b], 16)

            def head(h, b, more):
                for n in range(NS):
                    if n % 2:
                        rest_ahead(pool, h, b, n, more)
                    if more:
                        for m in range(4):
                            if v_at[m] == n:
                                if m == 0:
                                    pool.wait_ge(p_free, NS * h + 4)
                                split_v(h + 1, 1 - b, m)
                    if n == store_at and not (isinstance(h, int) and h == 0):
                        store(h - 1, 1 - b)

            for m in range(4):
                split_v(0, 0, m)
            rest(pool, 0, 0, 1)
            over_heads(pool, head, peel=True)
            store(NH - 1, 1)
            for b in range(2):
                pool.wait_ge(o_stored[b], 16 * NH // 2)

        @block.scalar
        def _(act):
            act.sem_inc(pS_free, 2)
            act.wait_ge(consts, 32)
            act.wait_ge(split, 4 * NC)
            act.wait_ge(v_split, 4)
            load(act, 1)

            def head(h, b, more):
                for n in range(NS):
                    r = b * NS + n
                    act.wait_ge(s_made, NS * h + n + 1)
                    act.wait_ge(p_free, NS * h + n + 1)
                    act.activation(pf[:, r % 4, :], pS[r % 2][:, 0:QB], ACT.Exp, scale=scale[:, 0:1])
                    act.activation(p1[r % 4][:, :], pS[r % 2][:, 0:QB], ACT.Exp, scale=scale[:, 0:1]).then_inc(pS_free, 1)
                    if n == load_at and more and not (isinstance(h, int) and h == NH - 2):
                        act.wait_ge(split, 4 * NC * h + 8 * NC)
                        act.wait_ge(v_split, 4 * h + 8)
                        load(act, h + 2)

            over_heads(act, head)

        @block.tensor
        def _(pe):
            pe.sem_inc(p_free, 4)
            pe.wait_ge(consts, 32)
            pe.wait_ge(ready, 5)

            def slot(h, b, j):
                if j == 0:
                    pe.wait_ge(split, 4 * NC * h + 2 * NC)
                    if not (isinstance(h, int) and h == 0):
                        pe.wait_ge(max_moved, h)
                pe.wait_ge(pM_free, TWO * SLOTS * h + TWO * (j + 1))
                at = (j % NC) * CW
                pe.matmul(pM[j % 2][:, 0:CW], q1[b][0:QH, (j // NC) * P:(j // NC + 1) * P], k1[b][0:QH, at:at + CW],
                          start=True, stop=True).then_inc(slot_made, TWO)

            def turn_max(h):
                pe.wait_ge(max_ready, h + 1)
                pe.transpose(pM[0][0:QT, 0:P], mx[:, :], eye[:, :]).then_inc(max_turned, 1)

            def scores(h, b, n):
                r = b * NS + n
                qb, kt = n // KT, n % KT
                if n == 0:
                    pe.wait_ge(split, 4 * NC * h + 4 * NC)
                    pe.wait_ge(max_in, 16 * h + 16)
                pe.wait_ge(pS_free, NS * h + n + 1)
                keys, queries = slice(kt * P, (kt + 1) * P), slice(qb * QB, (qb + 1) * QB)
                pe.matmul(pS[r % 2][:, 0:QB], k1[b][:, keys], q1[b][:, queries], start=True, stop=False)
                pe.matmul(pS[r % 2][:, 0:QB], k1[b][0:QH, keys], q2[b][:, queries], start=False, stop=False)
                pe.matmul(pS[r % 2][:, 0:QB], k2[b][:, keys], q1[b][0:QH, queries], start=False, stop=True
                          ).then_inc(s_made, 1)

            def values(h, b, n):
                r = (b * NS + n) % 4
                qb, kt = n // KT, n % KT
                o_at = (b * NQ + qb) % 2
                pe.wait_ge(odd_done if n % 2 else even_done, NS // 2 * h + n // 2 + 1)
                if n == 0:
                    pe.wait_ge(v_split, 4 * h + 4)
                if kt == 0:
                    pe.wait_ge(o_free, NQ * h + qb + 1)
                for t in range(TQ):
                    for part, cols in ((p1, VC), (p2, VC2)):
                        last = pe.matmul(pO[o_at][:, t // 2, (t % 2) * VC:(t % 2) * VC + cols],
                                         part[r][:, t * P:(t + 1) * P], vv[b][:, kt, 0:cols],
                                         start=(kt == 0 and t % 2 == 0 and part is p1), stop=(kt == KT - 1),
                                         skip_group_check=True)
                last.then_inc(p_free, 1)

            def head(h, b, more):
                for n in range(NS):
                    if n + LAG < NS:
                        scores(h, b, n + LAG)
                    elif more:
                        scores(h + 1, 1 - b, n + LAG - NS)
                    values(h, b, n)
                    if more:
                        for j in range(SLOTS):
                            if slot_at[j] == n:
                                slot(h + 1, 1 - b, j)
                        if n == turn_at:
                            turn_max(h + 1)

            for j in range(SLOTS):
                slot(0, 0, j)
            turn_max(0)
            for n in range(LAG):
                scores(0, 0, n)
            over_heads(pe, head)

        @block.vector
        def _(dve):
            dve.sem_inc(pM_free, 2 * TWO)
            dve.sem_inc(o_free, 2)

            def split_qk(h, b, j):
                first, (x, x1, x2) = j < 2 * NC, ((q, q1[b], q2[b]), (k, k1[b], k2[b]))[j % 2]
                c = slice((j // 2 % NC) * CW, (j // 2 % NC + 1) * CW)
                if j == 0:
                    dve.wait_ge(qk_in, 32 * h + 32)
                if first:
                    dve.tensor_copy(x1[0:QH, c], x[:, c]).then_inc(split, 1)
                else:
                    dve.wait_ge(split, 4 * NC * h + j - 2 * NC + 1)
                    dve.tensor_tensor(x2[:, c], x[:, c], x1[0:QH, c], ALU.subtract).then_inc(split, 1)

            def slot(h, j):
                dve.wait_ge(slot_made, TWO * SLOTS * h + TWO * (j + 1))
                dve.tensor_reduce(mxs[:, j // NC, j % NC:j % NC + 1], pM[j % 2][:, 0:CW], AX.X, ALU.max
                                  ).then_inc(pM_free, TWO)

            def join(h):
                dve.wait_ge(pM_free, TWO * SLOTS * h + TWO * (SLOTS + 2))
                if not (isinstance(h, int) and h == 0):
                    dve.wait_ge(max_turned, h)
                dve.tensor_reduce(mx[:, :], mxs[:, :, :], AX.X, ALU.max).then_inc(max_ready, 1)
                dve.wait_ge(max_turned, h + 1)
                if not (isinstance(h, int) and h == 0):
                    dve.wait_ge(max_in, 16 * h)
                dve.tensor_scalar(nmx[:, :], pM[0][0:QT, 0:P], -1.0 / MAX_UNIT, None, ALU.mult).then_inc(max_moved, 1)

            def normalise(h, b, qb):
                o_at = (b * NQ + qb) % 2
                dve.wait_ge(p_free, NS * h + KT * (qb + 1) + 4)
                if qb == 0 and not early(h):
                    dve.wait_ge(o_stored[b], 8 * h - 8 * b)
                tiles = max(1, TQ // 2)
                sums = pO[o_at][:, 0:tiles, 0:(TQ // tiles) * VC].rearrange("p a (t d) -> p a t d", d=VC)
                shape = lambda x: x.rearrange("p (a t) d -> p a t d", a=tiles)
                dve.reciprocal(rec[:, o_at, :].rearrange("p (a t) -> p a t", a=tiles), sums[:, :, :, 0]).then_inc(inverted, 1)
                for a in range(tiles):
                    dve.tensor_reduce(osum[:, o_at, a * (TQ // tiles):(a + 1) * (TQ // tiles), :],
                                      sums[:, a, :, 1:].rearrange("p t (s d) -> p t d s", s=3), AX.X, ALU.add
                                      ).then_inc(inverted, 1)
                dve.wait_ge(inverted, (tiles + 1) * (NQ * h + qb + 1))
                dve.tensor_tensor(o[:, b, qb * TQ:(qb + 1) * TQ, :], osum[:, o_at, :, :],
                                  rec[:, o_at, :].unsqueeze(2).to_broadcast([P, TQ, VH]), ALU.mult).then_inc(o_free, 1)

            def head(h, b, more):
                for n in range(NS):
                    if n % 2 == 0:
                        rest_ahead(dve, h, b, n, more)
                    if n % KT == norm_at:
                        if n >= KT:
                            normalise(h, b, n // KT - 1)
                        elif not (isinstance(h, int) and h == 0):
                            normalise(h - 1, 1 - b, NQ - 1)
                    if more:
                        for j in range(4 * NC):
                            if split_at[j] == n:
                                split_qk(h + 1, 1 - b, j)
                        for j in range(SLOTS):
                            if slot_at[j] == n:
                                slot(h + 1, j)
                        if n == turn_at:
                            join(h + 1)

            for j in range(4 * NC):
                split_qk(0, 0, j)
            for j in range(SLOTS):
                slot(0, j)
            join(0)
            rest(dve, 0, 0, 0)
            over_heads(dve, head, peel=True)
            normalise(NH - 1, 1, NQ - 1)


def attend_short(nc, io):
    L, g0 = GROUPS[1], GROUPS[0]
    KT = L // P
    NS = NH * KT
    LAG = 2
    VC, VC2 = 1 + 3 * VH, 1 + 2 * VH
    with ExitStack() as ctx:
        def sb(name, shape, dt=F32):
            return ctx.enter_context(nc.sbuf_tensor("as_" + name, shape, dt))

        def ps(name):
            return ctx.enter_context(nc.psum_tensor("as_" + name, [P, 512], F32))

        sem = semaphores(nc, ctx, "as_")
        eye, scale, zero = sb("eye", [P, P]), sb("scale", [P, 1]), sb("zero", [P, 1])
        q, k = sb("q", [QH, NH, L]), sb("k", [QH, NH, L])
        q1, k1 = sb("q1", [QH + 1, NH, L], F16), sb("k1", [QH + 1, NH, L], F16)
        q2, k2 = sb("q2", [QH, NH, L], F16), sb("k2", [QH, NH, L], F16)
        v, vr = sb("v", [P, KT, NH, VH]), sb("vr", [P, KT, NH, VH])
        vv = sb("vv", [P, KT, NH, VC], BF16)
        mx, nmx = sb("mx", [P, NS]), sb("nmx", [NS, P], F16)
        pf = sb("pf", [P, 4, L])
        p1, p2 = ([sb(f"p{m}{n}", [P, L], F16) for n in range(4)] for m in (1, 2))
        rec, osum = sb("rec", [P, 2, KT]), sb("osum", [P, 2, KT, VH])
        o = sb("o", [P, KT, NH, VH])
        pM, pS, pO = [ps(f"pM{n}") for n in range(2)], [ps(f"pS{n}") for n in range(2)], [ps(f"pO{n}") for n in range(4)]

        q_in, k_in, v_in, consts, ready = sem("q_in"), sem("k_in"), sem("v_in"), sem("consts"), sem("ready")
        cast, split, v_split = sem("cast"), sem("split"), sem("v_split")
        slot_made, reduced, turned, moved, max_in = (
            sem("slot_made"), sem("reduced"), sem("turned"), sem("moved"), sem("max_in"))
        s_made, exps, rests, used = sem("s_made"), sem("exps"), [sem("rest_even"), sem("rest_odd")], sem("used")
        inverted, normed, stored = sem("inverted"), sem("normed"), sem("stored")
        block = ctx.enter_context(nc.Block())

        def rest(eng, n):
            eng.wait_ge(exps, n + 1)
            if n >= 4:
                eng.wait_ge(used, n - 3)
            eng.tensor_tensor(p2[n % 4][:, :], pf[:, n % 4, :], p1[n % 4][:, :], ALU.subtract).then_inc(rests[n % 2], 1)

        @block.sync
        def _(sp):
            sp.dma_start(q[:, :, :], io["QK"][0:NH, :, g0:g0 + L].rearrange("h d t -> d h t")).then_inc(q_in, 16)
            sp.dma_start(k[:, :, :], io["QK"][NH:, :, g0:g0 + L].rearrange("h d t -> d h t")).then_inc(k_in, 16)
            sp.dma_start(v[:, :, :, :], io["V"][g0:g0 + L, :, :].rearrange("(k p) h d -> p k h d", p=P)).then_inc(v_in, 16)
            sp.dma_start(eye[:, :], io["tab_eye"]).then_inc(consts, 16)
            sp.dma_start(scale[:, :], io["S"]).then_inc(consts, 16)
            sp.wait_ge(moved, 1)
            sp.dma_start(q1[QH:QH + 1, :, :], nmx[:, :]).then_inc(max_in, 16)
            sp.wait_ge(normed, NH)
            sp.dma_start(io["YA"][g0:g0 + L, :].rearrange("(k p) c -> p k c", p=P),
                         o[:, :, :, :].rearrange("p k h d -> p k (h d)")).then_inc(stored, 16)
            sp.wait_ge(stored, 16)

        @block.gpsimd
        def _(pool):
            pool.memset(zero[:, :], 0.0).then_inc(ready, 1)
            pool.wait_ge(ready, 1)
            pool.memset(k1[QH:QH + 1, :, :], MAX_UNIT).then_inc(ready, 1)
            pool.wait_ge(ready, 2)
            pool.memset(vv[:, :, :, 0:1], 1.0).then_inc(ready, 1)
            pool.wait_ge(ready, 3)
            pool.wait_ge(v_in, 16)
            for kt in range(KT):
                parts = vv[:, kt, :, 1:].rearrange("p h (s d) -> p s h d", s=3)
                nil = zero[:, :].unsqueeze(2).to_broadcast([P, NH, VH])
                for m, (out, a, b, op) in enumerate(((parts[:, 0], v[:, kt], nil, ALU.add),
                                                     (vr[:, kt], v[:, kt], parts[:, 0], ALU.subtract),
                                                     (parts[:, 1], vr[:, kt], nil, ALU.add),
                                                     (parts[:, 2], vr[:, kt], parts[:, 1], ALU.subtract))):
                    if m or kt:
                        pool.wait_ge(v_split, 4 * kt + m)
                    pool.tensor_tensor(out, a, b, op).then_inc(v_split, 1)
            for n in range(1, NS, 2):
                rest(pool, n)

        @block.scalar
        def _(act):
            for x, x1, here in ((q, q1, q_in), (k, k1, k_in)):
                act.wait_ge(here, 16)
                act.activation(x1[0:QH, :, :], x[:, :, :], ACT.Copy).then_inc(cast, 1)
            act.wait_ge(consts, 32)
            for n in range(NS):
                act.wait_ge(s_made, n + 1)
                if n >= 4:
                    act.wait_ge(used, n - 3)
                act.activation(pf[:, n % 4, :], pS[n % 2][:, 0:L], ACT.Exp, scale=scale[:, 0:1])
                act.activation(p1[n % 4][:, :], pS[n % 2][:, 0:L], ACT.Exp, scale=scale[:, 0:1]).then_inc(exps, 1)

        @block.tensor
        def _(pe):
            pe.wait_ge(cast, 2)
            for h in range(NH):
                if h >= 2:
                    pe.wait_ge(reduced, h - 1)
                for t in range(KT):
                    last = pe.matmul(pM[h % 2][:, t * L:(t + 1) * L], q1[0:QH, h, t * P:(t + 1) * P], k1[0:QH, h, :],
                                     start=True, stop=True)
                last.then_inc(slot_made, 1)
            pe.wait_ge(reduced, NH)
            pe.wait_ge(consts, 32)
            pe.transpose(pM[0][0:NS, 0:P], mx[:, :], eye[:, :]).then_inc(turned, 1)
            pe.wait_ge(max_in, 16)
            pe.wait_ge(split, 2)
            pe.wait_ge(ready, 3)
            pe.wait_ge(v_split, 4 * KT)

            def scores(n):
                h, keys = n // KT, slice(n % KT * P, (n % KT + 1) * P)
                if n >= 2:
                    pe.wait_ge(exps, n - 1)
                out = pS[n % 2][:, 0:L]
                pe.matmul(out, k1[:, h, keys], q1[:, h, :], start=True, stop=False)
                pe.matmul(out, k1[0:QH, h, keys], q2[:, h, :], start=False, stop=False)
                pe.matmul(out, k2[:, h, keys], q1[0:QH, h, :], start=False, stop=True).then_inc(s_made, 1)

            def values(n):
                h, kt = n // KT, n % KT
                pe.wait_ge(rests[n % 2], n // 2 + 1)
                if kt == 0 and h >= 4:
                    pe.wait_ge(normed, h - 3)
                for t in range(KT):
                    for part, cols in ((p1, VC), (p2, VC2)):
                        last = pe.matmul(pO[h % 4][:, t * VC:t * VC + cols], part[n % 4][:, t * P:(t + 1) * P],
                                         vv[:, kt, h, 0:cols], start=(kt == 0 and t == 0 and part is p1),
                                         stop=(kt == KT - 1), skip_group_check=True)
                last.then_inc(used, 1)

            for n in range(LAG):
                scores(n)
            for n in range(NS):
                if n + LAG < NS:
                    scores(n + LAG)
                values(n)

        @block.vector
        def _(dve):
            for h in range(NH):
                dve.wait_ge(slot_made, h + 1)
                dve.tensor_reduce(mx[:, KT * h:KT * h + KT], pM[h % 2][:, :].rearrange("p (t k) -> p t k", t=KT), AX.X,
                                  ALU.max).then_inc(reduced, 1)
            dve.wait_ge(turned, 1)
            dve.tensor_scalar(nmx[:, :], pM[0][0:NS, 0:P], -1.0 / MAX_UNIT, None, ALU.mult).then_inc(moved, 1)
            for x, x1, x2 in ((q, q1, q2), (k, k1, k2)):
                dve.tensor_tensor(x2[:, :, :], x[:, :, :], x1[0:QH, :, :], ALU.subtract).then_inc(split, 1)

            def normalise(h):
                b = h % 2
                dve.wait_ge(used, KT * h + KT)
                sums = pO[h % 4][:, 0:KT * VC].rearrange("p (t d) -> p t d", d=VC)
                if h >= 2:
                    dve.wait_ge(normed, h - 1)
                dve.reciprocal(rec[:, b, :], sums[:, :, 0]).then_inc(inverted, 1)
                dve.tensor_reduce(osum[:, b, :, :], sums[:, :, 1:].rearrange("p t (s d) -> p t d s", s=3), AX.X, ALU.add
                                  ).then_inc(inverted, 1)
                dve.wait_ge(inverted, 2 * h + 2)
                dve.tensor_tensor(o[:, :, h, :], osum[:, b, :, :], rec[:, b, :].unsqueeze(2).to_broadcast([P, KT, VH]),
                                  ALU.mult).then_inc(normed, 1)

            for n in range(0, NS, 2):
                rest(dve, n)
                if n >= 4:
                    normalise(n // 2 - 2)
            for h in range(NH - 2, NH):
                normalise(h)


def hyena(nc, io):
    with ExitStack() as ctx:
        def sb(name, shape, dt=F32):
            return ctx.enter_context(nc.sbuf_tensor(f"hy_{name}", shape, dt))

        s = {"hidden": sb("hidden", [FH, T]),
             "norm": sb("norm", [P, 2, 2, DH]),
             "z": sb("z", [P, NT, CH]),
             "first": sb("first", [P, 2, 2, P]), "last": sb("last", [P, 2, 2, P]), "ones": sb("ones", [P, P])}
        for order in range(2):
            first_stage(nc, io, s, order)
            spectrum_products(nc, io, s, order)
            last_stage(nc, io, s, order)
        clear_semaphores(nc)


def group_of(i):
    return 1 if isinstance(i, int) and i >= NTP else 0


def stage_rows(x, g):
    N1, r0 = 2 * GROUPS[g] // N2, 2 * sum(GROUPS[:g])
    return x[r0:r0 + N2 * N1, :].rearrange("(t b r) c -> b t r c", b=N1 // 2, r=2)


def copy_tokens(eng, tile, dram, i, sem, store=False):
    g = group_of(i)
    L = GROUPS[g]
    J = P // (L // N2)
    rows_of = dram[sum(GROUPS[:g]):sum(GROUPS[:g]) + L, :].rearrange("(t i j) c -> i j t c", i=N2 // J, j=J)
    here = rows_of[i - g * NTP]
    n = 1 if g else J
    for m in range(n):
        part, whole = (tile, here) if n == 1 else (tile[m * P // J:(m + 1) * P // J, :], here[m])
        eng.dma_start(*((whole, part) if store else (part, whole))).then_inc(sem, 16)


COPIES = tuple(P // (L // N2) if P // (L // N2) < 16 else 1 for L in GROUPS)


def copies_before(i, b):
    if not group_of(i):
        return COPIES[0] // 2 * (i - b)
    return COPIES[0] * NTP // 2 + COPIES[1] * ((i - NTP) // 2)


def first_stage(nc, io, s, order):
    with ExitStack() as ctx:
        def sb(name, shape):
            return ctx.enter_context(nc.sbuf_tensor(f"fs{order}_{name}", shape, F32))

        sem = semaphores(nc, ctx, f"fs{order}_")

        w3 = sb("w3", [FH, 2, DH])
        decay = sb("decay", [P, 2, DH])
        negt = sb("negt", [P, NT])
        hs = [sb(f"hs{b}", [FH, P]) for b in range(2)]
        hs_back = sb("hs_back", [FH, P])
        win = sb("win", [P, 2, 2, DH])
        tap = sb("tap", [P, 2, 2, DH])
        size = sb("size", [P, 2, DH])
        sd = sb("sd", [P, 2, 2, DH])
        a = sb("a", [P, 2, 2, 3, DH])
        pH = [ctx.enter_context(nc.psum_tensor(f"fs{order}_pH{d}", [P, DH], F32)) for d in range(2)]
        pZ = [ctx.enter_context(nc.psum_tensor(f"fs{order}_pZ{h}", [P, DH], F32)) for h in range(2)]
        pA = [ctx.enter_context(nc.psum_tensor(f"fs{order}_pA{m}", [P, DH], F32)) for m in range(4)]
        wts, zeroed, hs_ready, windows = sem("wts"), sem("zeroed"), sem("hs_ready"), sem("windows")
        h_made, tapped, sized, summed, mixed = sem("h_made"), sem("tapped"), sem("sized"), sem("summed"), sem("mixed")
        a_made, a_moved, total = sem("a_made"), sem("a_moved"), sem("total")
        hidden_in, back_made, cleared, z_made, z_moved = sem("hidden_in"), sem("back_made"), sem("cleared"), sem("z_made"), sem("z_moved")
        z_in = [sem(f"z_in{b}") for b in range(2)]
        a_out = [sem(f"a_out{b}") for b in range(2)]
        block = ctx.enter_context(nc.Block())

        def far_pairs(eng, step, lag):
            step(0, 0)
            step(1, 1)
            step(2, 0)
            lag(0, 0)
            step(3, 1)
            lag(1, 1)
            with eng.Fori(1, NTP // 2 - 1) as i:
                for b in range(2):
                    step(2 * i + 2 + b, b)
                    lag(2 * i + b, b)
            step(NTP, 0)
            lag(NTP - 2, 0)
            step(NTP + 1, 1)
            for t in range(NTP - 1, NT):
                lag(t, t % 2)

        def pairs(eng, step, lag=None):
            lag = lag or (lambda i, b: None)
            step(0, 0)
            step(1, 1)
            lag(0, 0)
            with eng.Fori(1, NTP // 2) as i:
                step(2 * i, 0)
                lag(2 * i - 1, 1)
                step(2 * i + 1, 1)
                lag(2 * i, 0)
            for t in range(NTP, NT):
                step(t, t % 2)
                lag(t - 1, 1 - t % 2)
            lag(NT - 1, 1)

        @block.sync
        def _(sp):
            if order == 0:
                sp.dma_start(s["hidden"][:, :], io["H"]).then_inc(hidden_in, 16)
                for g in range(2):
                    sp.dma_start(s["first"][:, g, :, :], io[f"tab_first{g}"]).then_inc(hidden_in, 16)
                    sp.dma_start(s["last"][:, g, :, :], io[f"tab_last{g}"]).then_inc(hidden_in, 16)
            for d in range(2):
                at = (2 * d + order) * DH
                sp.dma_start(w3[:, d, :], io["filt_w3"][0, :, at:at + DH]).then_inc(wts, 16)
                sp.dma_start(decay[:, d, :], io["filt_decay"][0, d, order:order + 1, :].to_broadcast([P, DH])).then_inc(wts, 16)
            for g, at in enumerate((0, NTP)):
                sp.dma_start(negt[:, at:at + GROUPS[g] // P], io[f"tab_negt{g}"]).then_inc(wts, 16)
            if order == 0:
                def load_z(i, b):
                    if not early(i):
                        sp.wait_ge(z_in[b], 16 * copies_before(i, b))
                    copy_tokens(sp, s["z"][:, i, :] if isinstance(i, int) else s["z"][:, bass.ds(i, 1), :].rearrange(
                        "p i c -> p (i c)"), io["Z"], i, z_in[b])
                load_z(0, 0)
                load_z(1, 1)
                with sp.Fori(1, NTP // 2) as i:
                    load_z(2 * i, 0)
                    load_z(2 * i + 1, 1)
                for i in range(NTP, NT):
                    load_z(i, i % 2)

        @block.gpsimd
        def _(pool):
            def step(i, b):
                pool.wait_ge(tapped, 2 * i + 2)
                if not early(i):
                    pool.wait_ge(a_made, 4 * i - 4)
                pool.tensor_tensor(sd[:, b, 0, :], tap[:, b, 0, :], tap[:, b, 1, :], ALU.add).then_inc(mixed, 1)
                pool.tensor_tensor(sd[:, b, 1, :], tap[:, b, 0, :], tap[:, b, 1, :], ALU.subtract).then_inc(mixed, 1)
            pairs(pool, step)

        @block.scalar
        def _(act):
            act.wait_ge(wts, 96)
            if order == 0:
                act.wait_ge(hidden_in, 80)

            def step(i, b):
                if not early(i):
                    act.wait_ge(h_made, 2 * i - 2)
                    act.wait_ge(tapped, 2 * i - 2)
                act.activation(hs[b][:, :], s["hidden"][:, rows(i)], ACT.Copy).then_inc(hs_ready, 1)
                if isinstance(i, int) and i in (0, NTP):
                    act.activation(hs_back[:, :], s["hidden"][:, rows(i)], ACT.Copy).then_inc(back_made, 1)
                for d in range(2):
                    act.activation(win[:, b, d, :], decay[:, d, :], ACT.Exp, scale=negt[:, bass.ds(i, 1)]).then_inc(windows, 1)

            def lag(i, b):
                act.wait_ge(tapped, 2 * i + 2)
                if not (isinstance(i, int) and i == 0):
                    act.wait_ge(summed, i)
                act.activation(size[:, :, :], tap[:, b, :, :], ACT.Abs).then_inc(sized, 1)
                if not early(i):
                    act.wait_ge(a_out[b], 16 * i - 16 * b)
                for h in range(2):
                    for m in range(2):
                        act.wait_ge(a_made, 4 * i + 2 * h + m + 1)
                        act.activation(a[:, b, h, 1 + m, :], pA[2 * h + m][:, :], ACT.Copy).then_inc(a_moved, 1)
                for h in range(2):
                    act.wait_ge(z_made, 2 * i + h + 1)
                    act.activation(a[:, b, h, 0, :], pZ[h][:, :], ACT.Copy).then_inc(z_moved, 1)
                act.wait_ge(a_moved, 4 * i + 4)
                act.wait_ge(z_moved, 2 * i + 2)
                for h in range(2):
                    act.dma_start(io["F"][bass.ds(i * 2 * P + h * P, P), :], a[:, b, h, :, :]).then_inc(a_out[b], 16)
            far_pairs(act, step, lag)
            for b in range(2):
                act.wait_ge(a_out[b], 16 * NT)

        @block.tensor
        def _(pe):
            pe.wait_ge(wts, 96)

            def step(i, b):
                for d in range(2):
                    pe.wait_ge(hs_ready, i + 1)
                    if not (isinstance(i, int) and i == 0):
                        pe.wait_ge(tapped, 2 * i + d - 1)
                    hidden = hs[b]
                    if d == 1 and isinstance(i, int) and i in (0, NTP):
                        pe.wait_ge(cleared, 1 + i // NTP)
                        hidden = hs_back
                    pe.matmul(pH[d][:, :], hidden[:, :], w3[:, d, :], start=True, stop=True).then_inc(h_made, 1)

            def lag(i, b):
                for m in range(4):
                    pe.wait_ge(mixed, 2 * i + 2)
                    if not (isinstance(i, int) and i == 0):
                        pe.wait_ge(a_moved, 4 * i + m - 3)
                    pe.matmul(pA[m][:, :], s["first"][:, group_of(i), m // 2, :], sd[:, b, m % 2, :], start=True, stop=True
                              ).then_inc(a_made, 1)
                if order == 0:
                    pe.wait_ge(z_in[b], 16 * (copies_before(i, b) + COPIES[group_of(i)]))
                for h in range(2):
                    if not (isinstance(i, int) and i == 0):
                        pe.wait_ge(z_moved, 2 * i + h - 1)
                    pe.matmul(pZ[h][:, :], s["first"][:, group_of(i), h, :], tile_of(s, 0, i), start=True, stop=True
                              ).then_inc(z_made, 1)
            pairs(pe, step, lag)
            pe.wait_ge(summed, NT)
            pe.wait_ge(a_moved, 4 * NT)
            for g in range(2):
                for d in range(2):
                    last = pe.matmul(pA[g][:, :], s["ones"][:, :], s["norm"][:, g, d, :], start=(d == 0), stop=(d == 1))
                last.then_inc(total, 1)

        @block.vector
        def _(dve):
            dve.memset(s["norm"][:, :, :, :], 0.0).then_inc(zeroed, 1)
            dve.wait_ge(zeroed, 1)
            if order == 0:
                dve.memset(s["ones"][:, :], 1.0)

            def clear_back(n):
                dve.wait_ge(back_made, n)
                dve.memset(hs_back[:, 0:1], 0.0).then_inc(cleared, 1)

            def step(i, b):
                if isinstance(i, int) and i in (0, NTP):
                    clear_back(1 + i // NTP)
                if not early(i):
                    dve.wait_ge(mixed, 2 * i - 2)
                    dve.wait_ge(sized, i - 1)
                for d in range(2):
                    dve.wait_ge(windows, 2 * i + d + 1)
                    dve.wait_ge(h_made, 2 * i + d + 1)
                    dve.scalar_tensor_tensor(tap[:, b, d, :], win[:, b, d, :], 0.05, pH[d][:, :], ALU.add, ALU.mult
                                             ).then_inc(tapped, 1)

            def lag(i, b):
                dve.wait_ge(sized, i + 1)
                dve.wait_ge(summed, i)
                sums = s["norm"][:, group_of(i), :, :]
                dve.tensor_tensor(sums, sums, size[:, :, :], ALU.add).then_inc(summed, 1)
            pairs(dve, step, lag)
            dve.wait_ge(total, 2)
            for g in range(2):
                dve.reciprocal(s["norm"][:, g, 0, :], pA[g][:, :]).then_inc(total, 1)
            dve.wait_ge(total, 4)


def tile_of(s, n, i):
    return s["z"][:, bass.ds(i, 1), n * DH:(n + 1) * DH].rearrange("p i c -> p (i c)")


def spectrum_products(nc, io, s, order):
    NB = [L // N2 for L in GROUPS]
    N0 = NB[0] + 1
    STEPS = N0 + NB[1] + 1
    with ExitStack() as ctx:
        def sb(name, shape):
            return ctx.enter_context(nc.sbuf_tensor(f"sp{order}_{name}", shape, F32))

        def ps(name):
            return ctx.enter_context(nc.psum_tensor(f"sp{order}_{name}", [P, DH], F32))

        sem = semaphores(nc, ctx, f"sp{order}_")

        tab = [sb(f"tab{r}", [P, 5, P]) for r in range(4)]
        rows_in = [sb(f"rows{r}", [P, 3, DH]) for r in range(4)]
        kk = sb("kk", [P, 2, 2, DH])
        pk = sb("pk", [P, 2, 2, DH])
        gg = sb("gg", [P, 2, DH])
        pX = [ps(f"pX{b}") for b in range(2)]
        pK = [[ps(f"pK{b}{m}") for m in range(2)] for b in range(2)]
        pG = [ps(f"pG{b}") for b in range(2)]
        step_in = [sem(f"step_in{r}") for r in range(4)]
        spectra, copied, multiplied = sem("spectra"), sem("copied"), sem("multiplied")
        g_made, g_moved = sem("g_made"), sem("g_moved")
        g_out = [sem(f"g_out{b}") for b in range(2)]
        src, dst = ([stage_rows(io[x], g) for g in range(2)] for x in ("F", "G"))
        block = ctx.enter_context(nc.Block())

        def place(n):
            return (1, n - N0) if isinstance(n, int) and n >= N0 else (0, n)

        def starts(n):
            return isinstance(n, int) and n in (0, N0)

        def results(n):
            return n - 1 if place(n)[0] else n

        def load(eng, n, r):
            g, n = place(n)
            k1 = {0: NB[g], 1: 0}.get(n, n - 1) if isinstance(n, int) else n - 1
            pair = 0 if isinstance(n, int) and n < 2 else n - 1
            eng.dma_start(tab[r][:, :, :], io[f"tab_spec{g}"][k1]).then_inc(step_in[r], 16)
            eng.dma_start(rows_in[r][:, :, :], src[g][pair]).then_inc(step_in[r], 16)

        def over_steps(eng, step, lag):
            step(0, 0, 0)
            for n in range(1, 4):
                step(n, n, n % 2)
                lag(n - 1, n - 1, (n - 1) % 2)
            with eng.Fori(1, NB[0] // 4) as i:
                for r in range(4):
                    step(4 * i + r, r, r % 2)
                    lag(4 * i + r - 1, (r - 1) % 4, (r - 1) % 2)
            for n in range(NB[0], STEPS):
                step(n, n % 4, n % 2)
                lag(n - 1, (n - 1) % 4, (n - 1) % 2)
            lag(STEPS - 1, (STEPS - 1) % 4, (STEPS - 1) % 2)

        @block.sync
        def _(sp):
            for n in range(4):
                load(sp, n, n)
            with sp.Fori(0, NB[0] // 4 - 1) as i:
                for r in range(4):
                    sp.wait_ge(g_made, 8 * i + 2 * r + 2)
                    load(sp, 4 * i + r + 4, r)
            for n in range(NB[0], STEPS):
                sp.wait_ge(g_made, 2 * (n - 4) + 2)
                load(sp, n, n % 4)

        @block.scalar
        def _(act):
            def step(n, r, b):
                for m in range(2):
                    act.wait_ge(spectra, 3 * n + m + 2)
                    if not early(n):
                        act.wait_ge(multiplied, 2 * n + m - 3)
                    act.activation(kk[:, b, m, :], pK[b][m][:, :], ACT.Copy).then_inc(copied, 1)

            def lag(n, r, b):
                if starts(n):
                    return
                g, m = place(n)
                act.wait_ge(g_made, 2 * n + 2)
                if not (isinstance(n, int) and n < 3):
                    act.wait_ge(g_out[b], 8 * NB[0] + 16 * ((m - 1) // 2) if g else 8 * (n - 2 + b))
                act.activation(gg[:, b, :], pG[b][:, :], ACT.Copy).then_inc(g_moved, 1)
                act.wait_ge(g_moved, results(n))
                act.dma_start(dst[g][m - 1], gg[:, b, :]).then_inc(g_out[b], 16)
            over_steps(act, step, lag)
            for b in range(2):
                act.wait_ge(g_out[b], 8 * sum(NB))

        @block.tensor
        def _(pe):
            def step(n, r, b):
                pe.wait_ge(step_in[r], 8 * n - 8 * r + 32)
                if not early(n):
                    pe.wait_ge(multiplied, 2 * n - 2)
                pe.matmul(pX[b][:, :], tab[r][:, 0, :], rows_in[r][:, 0, :], start=True, stop=True).then_inc(spectra, 1)
                for m in range(2):
                    pe.matmul(pK[b][m][:, :], tab[r][:, 3 + m, :], rows_in[r][:, 1 + m, :], start=True, stop=True
                              ).then_inc(spectra, 1)

            def lag(n, r, b):
                shared, joins = starts(n), isinstance(n, int) and starts(n - 1)
                out = pG[1 - b] if shared else pG[b]
                if not joins and not (isinstance(n, int) and n < 3):
                    pe.wait_ge(g_moved, n - 1 if shared else results(n) - 2)
                for m in range(2):
                    pe.wait_ge(multiplied, 2 * n + m + 1)
                    pe.matmul(out[:, :], tab[r][:, 1 + m, :], pk[:, b, m, :], start=(m == 0 and not joins),
                              stop=(m == 1 and not shared)).then_inc(g_made, 1)
            over_steps(pe, step, lag)

        @block.vector
        def _(dve):
            def step(n, r, b):
                for m in range(2):
                    dve.wait_ge(copied, 2 * n + m + 1)
                    dve.wait_ge(spectra, 3 * n + 3)
                    if not early(n):
                        dve.wait_ge(g_made, 2 * n + m - 3)
                    dve.tensor_tensor(pk[:, b, m, :], kk[:, b, m, :], pX[b][:, :], ALU.mult).then_inc(multiplied, 1)
            over_steps(dve, step, lambda n, r, b: None)


def last_stage(nc, io, s, order):
    with ExitStack() as ctx:
        def sb(name, shape):
            return ctx.enter_context(nc.sbuf_tensor(f"ls{order}_{name}", shape, F32))

        sem = semaphores(nc, ctx, f"ls{order}_")

        bias = sb("bias", [P, DH])
        gin = sb("gin", [P, 4, 2, DH])
        ynorm = sb("ynorm", [P, 2, DH])
        zb = sb("zb", [P, 2, DH])
        out = sb("out", [P, 2, DH])
        pY = [ctx.enter_context(nc.psum_tensor(f"ls{order}_pY{b}", [P, DH], F32)) for b in range(2)]
        wts, y_made, chain, biased = sem("wts"), sem("y_made"), sem("chain"), sem("biased")
        g_in = [sem(f"g_in{n}") for n in range(4)]
        stored = [sem(f"stored{b}") for b in range(2)]
        block = ctx.enter_context(nc.Block())

        def load(eng, i, n):
            eng.dma_start(gin[:, n, :, :], io["G"][rows(i, 2 * P), :].rearrange("(h p) c -> p h c", h=2)
                          ).then_inc(g_in[n], 16)

        def in_tiles(eng, step):
            for i in range(4):
                step(i, i, i % 2, True)
            with eng.Fori(1, NTP // 4 - 1) as i:
                for n in range(4):
                    step(4 * i + n, n, n % 2, True)
            for i in range(NTP - 4, NT):
                step(i, i % 4, i % 2, i + 4 < NT)

        @block.sync
        def _(sp):
            sp.dma_start(bias[:, :], io["hyena_bias"][0, order:order + 1, :].to_broadcast([P, DH])).then_inc(wts, 16)

        @block.scalar
        def _(act):
            for n in range(4):
                load(act, n, n)

            def step(i, n, b, more):
                if more:
                    act.wait_ge(y_made, i + 1)
                    load(act, i + 4, n)
                if order == 1:
                    act.wait_ge(chain, 3 * i + 3)
                    copy_tokens(act, out[:, b, :], io["YH"], i, stored[b], store=True)
            in_tiles(act, step)
            if order == 1:
                for b in range(2):
                    act.wait_ge(stored[b], 16 * copies_before(NT, b))

        @block.tensor
        def _(pe):
            def step(i, n, b, more):
                pe.wait_ge(g_in[n], 4 * i - 4 * n + 16)
                if not early(i):
                    pe.wait_ge(chain, 3 * i - 5)
                for h in range(2):
                    last = pe.matmul(pY[b][:, :], s["last"][:, group_of(i), h, :], gin[:, n, h, :], start=(h == 0), stop=(h == 1))
                last.then_inc(y_made, 1)
            in_tiles(pe, step)

        @block.gpsimd
        def _(pool):
            pool.wait_ge(wts, 16)

            def step(i, n, b, more):
                if not early(i):
                    pool.wait_ge(chain, 3 * i - 4)
                pool.tensor_tensor(zb[:, b, :], tile_of(s, 0, i), bias[:, :], ALU.mult).then_inc(biased, 1)
            in_tiles(pool, step)

        @block.vector
        def _(dve):
            def step(i, n, b, more):
                dve.wait_ge(y_made, i + 1)
                dve.tensor_tensor(ynorm[:, b, :], s["norm"][:, group_of(i), 0, :], pY[b][:, :], ALU.mult).then_inc(chain, 1)
                dve.wait_ge(chain, 3 * i + 1)
                dve.wait_ge(biased, i + 1)
                dve.tensor_tensor(ynorm[:, b, :], ynorm[:, b, :], zb[:, b, :], ALU.add).then_inc(chain, 1)
                dve.wait_ge(chain, 3 * i + 2)
                if order == 1 and not early(i):
                    dve.wait_ge(stored[b], 16 * copies_before(i, b))
                dve.tensor_tensor(out[:, b, :] if order == 1 else tile_of(s, 0, i), ynorm[:, b, :], tile_of(s, 1 + order, i),
                                  ALU.mult).then_inc(chain, 1)
            in_tiles(dve, step)


def merge(nc, io):
    with ExitStack() as ctx:
        def sb(name, shape, dt=F32):
            return ctx.enter_context(nc.sbuf_tensor("mg_" + name, shape, dt))

        def ps(name, shape):
            return ctx.enter_context(nc.psum_tensor("mg_" + name, shape, F32))

        sem = semaphores(nc, ctx, "mg_")
        w = sb("w", [P, KD, D])
        wr = sb("wr", [P, KD, E_N])
        ogain = sb("ogain", [P, KD])
        mgain = sb("mgain", [P, D])
        eye = sb("eye", [P, P])
        eps, mhalf = sb("eps", [P, 2]), sb("mhalf", [P, 2])
        y = sb("y", [P, 2, D])
        x = sb("x", [P, 2, D])
        junk_y, junk_x = sb("junk_y", [P, D]), sb("junk_x", [P, D])
        my, mye, ry = sb("my", [P, 2, 2]), sb("mye", [P, 2, 2]), sb("ry", [P, 2, 2])
        mx, mxe, rx = sb("mx", [P, 2]), sb("mxe", [P, 2]), sb("rx", [P, 2])
        yn = sb("yn", [P, 2, D])
        yT = [sb(f"yT{b}", [P, KD, P]) for b in range(2)]
        x2 = sb("x2", [P, 2, D])
        xn = sb("xn", [P, 2, D])
        xT = sb("xT", [P, KD, P])
        lg = sb("lg", [E_N, 2, P])
        pY, pX = ps("pY", [P, KD, P]), ps("pX", [P, KD, P])
        pU, pL = ps("pU", [P, D]), ps("pL", [E_N, P])

        wts, scaled, consts = sem("wts"), sem("scaled"), sem("consts")
        t_in = [sem(f"t_in{b}") for b in range(2)]
        squared, eps_y, root_y, y_normed = sem("squared"), sem("eps_y"), sem("root_y"), sem("y_normed")
        y_turned, yT_ready, produced, added = sem("y_turned"), sem("yT_ready"), sem("produced"), sem("added")
        x_squared, eps_x, root_x, x_normed = sem("x_squared"), sem("eps_x"), sem("root_x"), sem("x_normed")
        x_turned, xT_ready, routed, lg_ready = sem("x_turned"), sem("xT_ready"), sem("routed"), sem("lg_ready")
        x2_out = [sem(f"x2_out{b}") for b in range(2)]
        xn_out = [sem(f"xn_out{b}") for b in range(2)]
        lg_out = [sem(f"lg_out{b}") for b in range(2)]
        WTS = 16 * 4
        w_in = [sem(f"w_in{k}") for k in range(KD)]
        block = ctx.enter_context(nc.Block())

        def over_tiles(eng, step):
            step(0, 0)
            step(1, 1)
            with eng.Fori(1, NTP // 2 - 1) as i:
                step(2 * i, 0)
                step(2 * i + 1, 1)
            for t in range(NTP - 2, NT):
                step(t, t % 2)

        def x_rows(t, names):
            name = names[0] if not isinstance(t, int) or t < NTP else names[1]
            return io[name][0, rows(t if name == names[0] else t - NTP), :]

        def load(eng, t, b):
            eng.dma_start(y[:, b, 0:DH], io["YH"][rows(t), :]).then_inc(t_in[b], 16)
            eng.dma_start(y[:, b, DH:], io["YA"][rows(t), :]).then_inc(t_in[b], 16)
            eng.dma_start(x[:, b, :], x_rows(t, ("x_prompt", "x_sample"))).then_inc(t_in[b], 16)

        @block.sync
        def _(sp):
            sp.dma_start(eye[:, :], io["tab_eye"]).then_inc(wts, 16)
            sp.dma_start(ogain[:, :], io["out_norm"]).then_inc(wts, 16)
            sp.dma_start(mgain[:, :], io["mlp_norm"].to_broadcast([P, D])).then_inc(wts, 16)
            sp.dma_start(wr[:, :, :], io["w_router"][0].rearrange("(k p) e -> p k e", p=P)).then_inc(wts, 16)
            for k in range(KD):
                sp.dma_start(w[:, k, :], io["w_out"][0, k * P:(k + 1) * P, :]).then_inc(w_in[k], 16)

        @block.gpsimd
        def _(pool):
            pool.memset(eps[:, :], EPS).then_inc(consts, 1)
            pool.memset(mhalf[:, :], -0.5).then_inc(consts, 1)
            pool.wait_ge(consts, 2)

            def of_y(t, b):
                pool.wait_ge(squared, 2 * t + 2)
                if not early(t):
                    pool.wait_ge(y_normed, 2 * t - 2)
                pool.tensor_tensor(mye[:, b, :], my[:, b, :], eps[:, :], ALU.add).then_inc(eps_y, 1)
                pool.wait_ge(eps_y, t + 1)
                pool.tensor_tensor(ry[:, b, :], mye[:, b, :], mhalf[:, :], ALU.pow).then_inc(root_y, 1)

            def step(t, b):
                if not (isinstance(t, int) and t == NT - 1):
                    of_y(t + 1, 1 - b)
                pool.wait_ge(x_squared, t + 1)
                if not early(t):
                    pool.wait_ge(x_normed, t - 1)
                pool.tensor_tensor(mxe[:, b:b + 1], mx[:, b:b + 1], eps[:, 0:1], ALU.add).then_inc(eps_x, 1)
                pool.wait_ge(eps_x, t + 1)
                pool.tensor_tensor(rx[:, b:b + 1], mxe[:, b:b + 1], mhalf[:, 0:1], ALU.pow).then_inc(root_x, 1)
            of_y(0, 0)
            over_tiles(pool, step)

        @block.scalar
        def _(act):
            load(act, 0, 0)
            load(act, 1, 1)

            def square_y(t, b):
                act.wait_ge(t_in[b], 24 * t - 24 * b + 48)
                act.wait_ge(squared, 2 * t)
                if not early(t):
                    act.wait_ge(root_y, t - 1)
                for h in range(2):
                    act.activation(junk_y[:, h * DH:(h + 1) * DH], y[:, b, h * DH:(h + 1) * DH], ACT.Square,
                                   scale=DH ** -0.5, accum_out=my[:, b, h:h + 1]).then_inc(squared, 1)

            def copy_yT(t, b):
                act.wait_ge(y_turned, t + 1)
                if not early(t):
                    act.wait_ge(produced, t - 1)
                for h in range(2):
                    act.activation(yT[b][:, 4 * h:4 * h + 4, :], pY[:, 4 * h:4 * h + 4, :], ACT.Copy).then_inc(yT_ready, 1)

            def copy_xT(t, b):
                act.wait_ge(x_turned, t + 1)
                if not (isinstance(t, int) and t == 0):
                    act.wait_ge(routed, t)
                for h in range(2):
                    act.activation(xT[:, 4 * h:4 * h + 4, :], pX[:, 4 * h:4 * h + 4, :], ACT.Copy).then_inc(xT_ready, 1)

            def copy_logits(t, b):
                act.wait_ge(routed, t + 1)
                act.wait_ge(lg_out[b], 8 * t - 8 * b)
                act.activation(lg[:, b, :], pL[:, :], ACT.Copy).then_inc(lg_ready, 1)
                act.wait_ge(lg_ready, t + 1)
                act.dma_start(io["LG"][:, rows(t)], lg[:, b, :]).then_inc(lg_out[b], 16)
                act.dma_start(io["XN"][rows(t), :], xn[:, b, :]).then_inc(xn_out[b], 16)

            def step(t, b):
                if not (isinstance(t, int) and t == NT - 1):
                    square_y(t + 1, 1 - b)
                if not (isinstance(t, int) and t == 0):
                    copy_xT(t - 1, 1 - b)
                if not (isinstance(t, int) and t == NT - 1):
                    copy_yT(t + 1, 1 - b)
                if not (isinstance(t, int) and t == 0):
                    copy_logits(t - 1, 1 - b)
                act.wait_ge(added, 2 * t + 2)
                act.wait_ge(x_squared, t)
                if not early(t):
                    act.wait_ge(root_x, t - 1)
                act.activation(junk_x[:, :], x2[:, b, :], ACT.Square, scale=D ** -0.5,
                               accum_out=mx[:, b:b + 1]).then_inc(x_squared, 1)
                act.dma_start(x_rows(t, ("y_prompt", "y_sample")), x2[:, b, :]).then_inc(x2_out[b], 16)
                if not (isinstance(t, int) and t + 2 >= NT):
                    load(act, t + 2, b)

            square_y(0, 0)
            copy_yT(0, 0)
            over_tiles(act, step)
            copy_xT(NT - 1, 1)
            copy_logits(NT - 1, 1)
            for b in range(2):
                for out in (x2_out, xn_out, lg_out):
                    act.wait_ge(out[b], 16 * NT // 2)

        @block.tensor
        def _(pe):
            pe.wait_ge(wts, WTS)

            def turn_y(t, b):
                pe.wait_ge(y_normed, 2 * t + 2)
                if not (isinstance(t, int) and t == 0):
                    pe.wait_ge(yT_ready, 2 * t)
                for k in range(KD):
                    last = pe.transpose(pY[:, k, :], yn[:, b, k * P:(k + 1) * P], eye[:, :])
                last.then_inc(y_turned, 1)

            def turn_x(t, b):
                pe.wait_ge(x_normed, t + 1)
                if not (isinstance(t, int) and t == 0):
                    pe.wait_ge(xT_ready, 2 * t)
                for k in range(KD):
                    last = pe.transpose(pX[:, k, :], xn[:, b, k * P:(k + 1) * P], eye[:, :])
                last.then_inc(x_turned, 1)

            def route(t, b):
                pe.wait_ge(xT_ready, 2 * t + 2)
                if not (isinstance(t, int) and t == 0):
                    pe.wait_ge(lg_ready, t)
                for k in range(KD):
                    last = pe.matmul(pL[:, :], wr[:, k, :], xT[:, k, :], start=(k == 0), stop=(k == KD - 1))
                last.then_inc(routed, 1)

            def step(t, b):
                pe.wait_ge(yT_ready, 2 * t + 2)
                if not (isinstance(t, int) and t == 0):
                    pe.wait_ge(added, 2 * t)
                for h in range(2):
                    for k in range(KD):
                        if isinstance(t, int) and t == 0 and h == 0:
                            pe.wait_ge(scaled, k + 1)
                        last = pe.matmul(pU[:, h * 512:(h + 1) * 512], yT[b][:, k, :], w[:, k, h * 512:(h + 1) * 512],
                                         start=(k == 0), stop=(k == KD - 1))
                last.then_inc(produced, 1)
                if not (isinstance(t, int) and t == 0):
                    turn_x(t - 1, 1 - b)
                if not (isinstance(t, int) and t == NT - 1):
                    turn_y(t + 1, 1 - b)
                if not (isinstance(t, int) and t == 0):
                    route(t - 1, 1 - b)
            turn_y(0, 0)
            over_tiles(pe, step)
            turn_x(NT - 1, 1)
            route(NT - 1, 1)

        @block.vector
        def _(dve):
            def norm_y(t, b):
                dve.wait_ge(root_y, t + 1)
                if not early(t):
                    dve.wait_ge(y_turned, t - 1)
                for h in range(2):
                    dve.tensor_scalar(yn[:, b, h * DH:(h + 1) * DH], y[:, b, h * DH:(h + 1) * DH], ry[:, b, h:h + 1],
                                      None, ALU.mult).then_inc(y_normed, 1)

            def step(t, b):
                if not (isinstance(t, int) and t == NT - 1):
                    norm_y(t + 1, 1 - b)
                dve.wait_ge(produced, t + 1)
                dve.wait_ge(x2_out[b], 8 * t - 8 * b)
                for h in range(2):
                    dve.tensor_tensor(x2[:, b, h * 512:(h + 1) * 512], x[:, b, h * 512:(h + 1) * 512],
                                      pU[:, h * 512:(h + 1) * 512], ALU.add).then_inc(added, 1)
                dve.wait_ge(root_x, t + 1)
                if not early(t):
                    dve.wait_ge(x_turned, t - 1)
                    dve.wait_ge(xn_out[b], 8 * t - 8 * b)
                dve.scalar_tensor_tensor(xn[:, b, :], x2[:, b, :], rx[:, b:b + 1], mgain[:, :], ALU.mult, ALU.mult
                                         ).then_inc(x_normed, 1)
            norm_y(0, 0)
            dve.wait_ge(wts, WTS)
            for k in range(KD):
                dve.wait_ge(w_in[k], 16)
                dve.tensor_scalar(w[:, k, :], w[:, k, :], ogain[:, k:k + 1], None, ALU.mult).then_inc(scaled, 1)
            over_tiles(dve, step)


SLOT_TILES = ((0, 0, P), (0, P, P), (1, 0, CAPS[1]))
NTOK = sum(n for _, _, n in SLOT_TILES)


def moe(nc, io):
    with ExitStack() as ctx:
        def sb(name, dt=F32):
            return ctx.enter_context(nc.sbuf_tensor("mo_" + name, [P, len(SLOT_TILES), E_N], dt))

        chosen = {"gather": sb("gather", I32), "scatter": sb("scatter", I32), "gate": sb("gate")}

        sem = semaphores(nc, ctx, "mo_")
        weights = {name: [ctx.enter_context(nc.sbuf_tensor(f"mo_{name}{b}", shape, F32)) for b in range(2)]
                   for name, shape in (("gate", [P, KD, FE]), ("up", [P, KD, FE]), ("down", [P, FE // P, D]))}
        weights["gu_in"] = [sem(f"gu_in{b}") for b in range(2)]
        weights["d_in"] = [sem(f"d_in{b}") for b in range(2)]
        choose(nc, io, chosen, weights)
        experts(nc, io, chosen, weights)


def load_gate_up(eng, io, weights, e, b):
    for name in ("gate", "up"):
        eng.dma_start(weights[name][b][:, :, :], io["w_" + name][0, e, :, :].rearrange("(k p) f -> p k f", p=P)
                      ).then_inc(weights["gu_in"][b], 16)


def load_down(eng, io, weights, e, b):
    eng.dma_start(weights["down"][b][:, :, :], io["w_down"][0, e, :, :].rearrange("(k p) f -> p k f", p=P)
                  ).then_inc(weights["d_in"][b], 16)


def choose(nc, io, chosen, weights):
    assert CAPS[0] == 2 * P
    NC, NJ = len(SLOT_TILES), NT // 2
    HALF = tuple(n // 2 for n in GROUPS)
    tile_pairs = [(j, j + NTP // 2) for j in range(NTP // 2)] + [(NTP, NTP + 1)]
    assert len(tile_pairs) == NJ
    with ExitStack() as ctx:
        def sb(name, shape, dt=F32):
            return ctx.enter_context(nc.sbuf_tensor("ch_" + name, shape, dt))

        def ps(name, shape):
            return ctx.enter_context(nc.psum_tensor("ch_" + name, shape, F32))

        sem = semaphores(nc, ctx, "ch_")
        eye = sb("eye", [P, P])
        lg = sb("lg", [E_N, T])
        ex = sb("ex", [P, NJ, 2, E_N])
        top, tot, inv = sb("top", [P, NJ, 2]), sb("tot", [P, NJ, 2]), sb("inv", [P, NJ, 2])
        aff = sb("aff", [2 * E_N, NJ * P])
        idx = sb("idx", [2 * E_N, NTOK], U32)
        lists = sb("lists", [2 * E_N, 4, NTOK])
        cols = sb("cols", [P, 4, NC, 2, E_N])
        better, apart = sb("better", [P, NC, E_N]), sb("apart", [P, NC, E_N])
        token = sb("token", [P, NC, E_N])
        pT = ps("pT", [P, NJ, 2, E_N])
        pA = ps("pA", [2 * E_N, 3 * 512])
        pC = ps("pC", [P, 4, NC, 2 * E_N])
        loaded, turned, chain, exps, back = sem("loaded"), sem("turned"), sem("chain"), sem("exps"), sem("back")
        aff_ready, listed, columns, cols_ready = sem("aff_ready"), sem("listed"), sem("columns"), sem("cols_ready")
        eights, merged, blank = sem("eights"), sem("merged"), sem("blank")
        block = ctx.enter_context(nc.Block())

        @block.sync
        def _(sp):
            sp.dma_start(eye[:, :], io["tab_eye"]).then_inc(loaded, 16)
            sp.dma_start(lg[:, :], io["LG"]).then_inc(loaded, 16)
            for b in range(2):
                load_gate_up(sp, io, weights, b, b)
                load_down(sp, io, weights, b, b)

        @block.gpsimd
        def _(pool):
            pool.memset(cols[:, :, :, :, :], 0.0).then_inc(blank, 1)

        @block.tensor
        def _(pe):
            pe.wait_ge(loaded, 32)
            for j, pair in enumerate(tile_pairs):
                for half, t in enumerate(pair):
                    last = pe.transpose(pT[:, j, half, :], lg[:, t * P:(t + 1) * P], eye[0:E_N, 0:E_N])
            last.then_inc(turned, 1)
            pe.wait_ge(chain, 5)
            for j in reversed(range(NJ)):
                last = pe.transpose(pA[:, j * P:(j + 1) * P], ex[:, j, :, :].rearrange("p h e -> p (h e)"), eye[:, :])
            last.then_inc(back, 1)
            pe.wait_ge(listed, 3)
            s0 = 0
            for c, (g, a, n) in enumerate(SLOT_TILES):
                for m in range(4):
                    last = pe.transpose(pC[0:n, m, c, :], lists[:, m, s0:s0 + n], eye[0:2 * E_N, 0:2 * E_N])
                s0 += n
            last.then_inc(columns, 1)

        @block.scalar
        def _(act):
            act.wait_ge(chain, 2)
            act.activation(ex[:, :, :, :], ex[:, :, :, :], ACT.Exp).then_inc(exps, 1)
            act.wait_ge(back, 1)
            act.activation(aff[:, HALF[0]:], pA[:, HALF[0]:NJ * P], ACT.Copy).then_inc(aff_ready, 1)
            act.activation(aff[:, 0:HALF[0]], pA[:, 0:HALF[0]], ACT.Copy).then_inc(aff_ready, 1)
            act.wait_ge(columns, 1)
            act.wait_ge(blank, 1)
            for c, (g, a, n) in enumerate(SLOT_TILES):
                act.activation(cols[0:n, :, c, :, :], pC[0:n, :, c, :].rearrange("p m (h e) -> p m h e", h=2), ACT.Copy
                               ).then_inc(cols_ready, 1)

        @block.vector
        def _(dve):
            def step(ins, sem, n):
                ins.then_inc(sem, 1)
                dve.wait_ge(sem, n)

            over_experts = lambda x: x.unsqueeze(3).to_broadcast([P, NJ, 2, E_N])
            dve.wait_ge(turned, 1)
            step(dve.tensor_reduce(top[:, :, :], pT[:, :, :, :], AX.X, ALU.max), chain, 1)
            step(dve.tensor_tensor(ex[:, :, :, :], pT[:, :, :, :], over_experts(top[:, :, :]), ALU.subtract), chain, 2)
            dve.wait_ge(exps, 1)
            step(dve.tensor_reduce(tot[:, :, :], ex[:, :, :, :], AX.X, ALU.add), chain, 3)
            step(dve.reciprocal(inv[:, :, :], tot[:, :, :]), chain, 4)
            step(dve.tensor_tensor(ex[:, :, :, :], ex[:, :, :, :], over_experts(inv[:, :, :]), ALU.mult), chain, 5)
            count = 0
            for g, order in ((1, 1), (0, 2)):
                dve.wait_ge(aff_ready, order)
                rest = aff[:, sum(HALF[:g]):sum(HALF[:g + 1])]
                s0 = sum(CAPS[:g])
                for r in range(CAPS[g] // 8):
                    eight = slice(s0 + 8 * r, s0 + 8 * r + 8)
                    v8, i8 = lists[:, 1, eight], idx[:, eight]
                    step(dve.max(v8, rest), eights, count + 1)
                    step(dve.max_index(i8, v8, rest), eights, count + 2)
                    step(dve.match_replace(rest, v8, rest, -1.0), eights, count + 3)
                    count += 3
            step(dve.tensor_copy(lists[:, 0, :], idx[:, :]), listed, 1)
            for m in range(2):
                for g in range(2):
                    s0, n = sum(CAPS[:g]), CAPS[g]
                    ins = dve.tensor_copy(lists[:, 2 + m, s0:s0 + n], lists[:, m, s0:s0 + n][:, ::-1])
                ins.then_inc(listed, 1)
            dve.wait_ge(cols_ready, NC)
            first, second = cols[:, 0:2, :, 0, :], cols[:, 2:4, :, 1, :]
            step(dve.tensor_tensor(better[:, :, :], first[:, 1], second[:, 1], ALU.is_ge), merged, 1)
            step(dve.tensor_tensor(chosen["gate"][:, :, :], first[:, 1], second[:, 1], ALU.max), merged, 2)
            for c, (g, a, n) in enumerate(SLOT_TILES):
                step(dve.tensor_scalar(token[:, c, :], second[:, 0, c], float(HALF[g]), None, ALU.add), merged, 3 + c)
            step(dve.tensor_tensor(apart[:, :, :], first[:, 0], token[:, :, :], ALU.subtract), merged, NC + 3)
            step(dve.tensor_tensor(apart[:, :, :], apart[:, :, :], better[:, :, :], ALU.mult), merged, NC + 4)
            step(dve.tensor_tensor(token[:, :, :], token[:, :, :], apart[:, :, :], ALU.add), merged, NC + 5)
            step(dve.tensor_copy(chosen["scatter"][:, :, :], token[:, :, :]), merged, NC + 6)
            for c, (g, a, n) in enumerate(SLOT_TILES):
                step(dve.tensor_scalar(chosen["gather"][:, c, :], token[:, c, :], float(sum(GROUPS[:g])), None, ALU.add
                                       ), merged, NC + 7 + c)


def experts(nc, io, chosen, weights):
    NC = len(SLOT_TILES)
    FT = FE // P
    starts = [sum(n for _, _, n in SLOT_TILES[:c]) for c in range(NC)]
    with ExitStack() as ctx:
        def sb(name, shape, dt=F32):
            return ctx.enter_context(nc.sbuf_tensor("ex_" + name, shape, dt))

        def ps(name, shape):
            return ctx.enter_context(nc.psum_tensor("ex_" + name, shape, F32))

        sem = semaphores(nc, ctx, "ex_")
        eye = sb("eye", [P, P])
        wg, wu, wd = weights["gate"], weights["up"], weights["down"]
        now_g = [sb(f"now_g{b}", [P, NC], I32) for b in range(2)]
        now_s = [sb(f"now_s{b}", [P, NC], I32) for b in range(2)]
        now_w = [sb(f"now_w{b}", [P, NC]) for b in range(2)]
        xs = [[sb(f"xs{b}{c}", [P, D]) for c in range(NC)] for b in range(2)]
        xT = sb("xT", [P, KD, NTOK])
        si = sb("si", [P, 2, NTOK])
        hT = sb("hT", [P, FT, NTOK])
        ys = [[sb(f"ys{b}{c}", [P, D]) for c in range(NC)] for b in range(2)]
        pT = ps("pT", [P, 2, 512])
        pG = [ps(f"pG{r}", [P, 512]) for r in range(2)]
        pU = [ps(f"pU{r}", [P, 512]) for r in range(2)]
        pY = ps("pY", [P, D])

        mark = sb("mark", [P, 2])
        wts, ticks = sem("wts"), sem("ticks")
        gu_in, d_in = weights["gu_in"], weights["d_in"]
        placed = sem("placed")
        gathered = [sem(f"gathered{b}") for b in range(2)]
        x_turned, xT_ready, gate_made, up_made = sem("x_turned"), sem("xT_ready"), sem("gate_made"), sem("up_made")
        silued, h_ready, y_made, y_ready = sem("silued"), sem("h_ready"), sem("y_made"), sem("y_ready")
        scattered = sem("scattered")
        block = ctx.enter_context(nc.Block())

        def over_experts(eng, step):
            step(0, 0, True)
            step(1, 1, True)
            with eng.Fori(1, E_N // 2 - 1) as i:
                step(2 * i, 0, True)
                step(2 * i + 1, 1, True)
            step(E_N - 2, 0, True)
            step(E_N - 1, 1, False)

        @block.sync
        def _(sp):
            sp.dma_start(eye[:, :], io["tab_eye"]).then_inc(wts, 16)

            def step(e, b):
                sp.wait_ge(up_made, FT * e + FT)
                load_gate_up(sp, io, weights, e + 2, b)
                sp.wait_ge(y_made, 2 * NC * e + 2 * NC)
                load_down(sp, io, weights, e + 2, b)
            with sp.Fori(0, E_N // 2 - 1) as i:
                step(2 * i, 0)
                step(2 * i + 1, 1)

        @block.gpsimd
        def _(pool):
            pool.memset(mark[:, :], 0.0).then_inc(ticks, 1)
            pool.wait_ge(ticks, 1)

            def tick(n):
                pool.wait_ge(ticks, n + 1)
                pool.tensor_tensor(mark[:, 1:2], mark[:, 0:1], mark[:, 0:1], ALU.add).then_inc(ticks, 1)

            def gather(e, b):
                pool.wait_ge(placed, 3 * e + 3)
                if not early(e):
                    pool.wait_ge(x_turned, KD * (e - 1))
                tick((NC + 1) * e - NC if not isinstance(e, int) or e else 0)
                for c, (g, _, n) in enumerate(SLOT_TILES):
                    pool.indirect_dma_start(out=xs[b][c][0:n, :], out_offset=None, in_=io["XN"],
                                            in_offset=bass.IndirectOffsetOnAxis(ap=now_g[b][0:n, c:c + 1], axis=0)
                                            ).then_inc(gathered[b], 16)

            def step(e, b, more):
                if more:
                    gather(e + 1, 1 - b)
                if not (isinstance(e, int) and e == 0):
                    pool.wait_ge(scattered, 16 * NC * e)
                for c, (g, _, n) in enumerate(SLOT_TILES):
                    pool.wait_ge(y_ready, 2 * NC * e + 2 * c + 2)
                    tick((NC + 1) * e + 1 + more + c)
                    out = io[("y_prompt", "y_sample")[g]][0]
                    pool.indirect_dma_start(out=out, out_offset=bass.IndirectOffsetOnAxis(ap=now_s[b][0:n, c:c + 1], axis=0),
                                            in_=ys[b][c][0:n, :], in_offset=None, compute_op=ALU.add).then_inc(scattered, 16)
            gather(0, 0)
            over_experts(pool, step)
            pool.wait_ge(scattered, 16 * NC * E_N)

        @block.scalar
        def _(act):
            def copies(e, b):
                for k in range(KD):
                    act.wait_ge(x_turned, KD * e + k + 1)
                    if k == 0 and not (isinstance(e, int) and e == 0):
                        act.wait_ge(up_made, FT * e)
                    act.activation(xT[:, k, :], pT[:, k % 2, 0:NTOK], ACT.Copy).then_inc(xT_ready, 1)

            def step(e, b, more):
                for f in range(FT):
                    act.wait_ge(gate_made, FT * e + f + 1)
                    if not (isinstance(e, int) and e == 0 and f < 2):
                        act.wait_ge(h_ready, FT * e + f - 1)
                    act.activation(si[:, f % 2, :], pG[f % 2][:, 0:NTOK], ACT.Silu).then_inc(silued, 1)
                if more:
                    copies(e + 1, 1 - b)
            copies(0, 0)
            over_experts(act, step)

        @block.tensor
        def _(pe):
            def turn(e, b):
                pe.wait_ge(gathered[b], 24 * e - 24 * b + 48)
                for k in range(KD):
                    if not (isinstance(e, int) and e == 0 and k < 2):
                        pe.wait_ge(xT_ready, KD * e + k - 1)
                    for c, (_, _, n) in enumerate(SLOT_TILES):
                        last = pe.transpose(pT[:, k % 2, starts[c]:starts[c] + n], xs[b][c][0:n, k * P:(k + 1) * P],
                                            eye[0:n, 0:n])
                    last.then_inc(x_turned, 1)

            def step(e, b, more):
                pe.wait_ge(gu_in[b], 16 * e - 16 * b + 32)
                pe.wait_ge(xT_ready, KD * e + KD)
                for f in range(FT):
                    for out, w, done, free in ((pG, wg, gate_made, silued), (pU, wu, up_made, h_ready)):
                        if not (isinstance(e, int) and e == 0 and f < 2):
                            pe.wait_ge(free, FT * e + f - 1)
                        for k in range(KD):
                            last = pe.matmul(out[f % 2][:, 0:NTOK], w[b][:, k, f * P:(f + 1) * P], xT[:, k, :],
                                             start=(k == 0), stop=(k == KD - 1))
                        last.then_inc(done, 1)
                if more:
                    turn(e + 1, 1 - b)
                pe.wait_ge(d_in[b], 8 * e - 8 * b + 16)
                pe.wait_ge(h_ready, FT * e + FT)
                for c, (_, _, n) in enumerate(SLOT_TILES):
                    for h in range(2):
                        if not (isinstance(e, int) and e == 0 and c == 0):
                            pe.wait_ge(y_ready, 2 * NC * e + 2 * c + h - 1)
                        for f in range(FT):
                            last = pe.matmul(pY[0:n, h * 512:(h + 1) * 512], hT[:, f, starts[c]:starts[c] + n],
                                             wd[b][:, f, h * 512:(h + 1) * 512], start=(f == 0), stop=(f == FT - 1))
                        last.then_inc(y_made, 1)
            pe.wait_ge(wts, 16)
            turn(0, 0)
            over_experts(pe, step)

        @block.vector
        def _(dve):
            def place(e, b):
                if not early(e):
                    dve.wait_ge(scattered, 16 * NC * (e - 1))
                for dst, name in ((now_g, "gather"), (now_s, "scatter"), (now_w, "gate")):
                    for_c = dst[b][:, :]
                    if name == "gate":
                        dve.tensor_copy(dst[b][:, 0:2], chosen[name][:, 0:2, bass.ds(e, 1)].rearrange("p c e -> p (c e)"))
                        dve.tensor_copy(dst[b][0:CAPS[1], 2:3], chosen[name][0:CAPS[1], 2, bass.ds(e, 1)]).then_inc(placed, 1)
                    else:
                        dve.tensor_copy(for_c, chosen[name][:, :, bass.ds(e, 1)].rearrange("p c e -> p (c e)")).then_inc(placed, 1)

            def step(e, b, more):
                if more:
                    place(e + 1, 1 - b)
                for f in range(FT):
                    dve.wait_ge(silued, FT * e + f + 1)
                    dve.wait_ge(up_made, FT * e + f + 1)
                    if f == 0 and not (isinstance(e, int) and e == 0):
                        dve.wait_ge(y_made, 2 * NC * e)
                    dve.tensor_tensor(hT[:, f, :], si[:, f % 2, :], pU[f % 2][:, 0:NTOK], ALU.mult).then_inc(h_ready, 1)
                if not early(e):
                    dve.wait_ge(scattered, 16 * NC * (e - 1))
                for c, (_, _, n) in enumerate(SLOT_TILES):
                    if c == 0:
                        dve.wait_ge(placed, 3 * e + 3)
                    for h in range(2):
                        half = slice(h * 512, (h + 1) * 512)
                        dve.wait_ge(y_made, 2 * NC * e + 2 * c + h + 1)
                        dve.tensor_scalar(ys[b][c][0:n, half], pY[0:n, half], now_w[b][0:n, c:c + 1], None, ALU.mult
                                          ).then_inc(y_ready, 1)
            place(0, 0)
            over_experts(dve, step)


INPUTS = {
    "x_prompt": (1, GROUPS[0], D), "x_sample": (1, GROUPS[1], D), "attn_norm": (1, D), "w_in": (1, D, CH + CM),
    "conv_w": (1, 3, CH), "conv_b": (1, CH), "filt_w1": (1, FEAT, FH), "filt_b1": (1, FH), "filt_w2": (1, FH, FH),
    "filt_b2": (1, FH), "filt_w3": (1, FH, 4 * DH), "filt_freq": (1, FH), "filt_decay": (1, 2, 2, DH),
    "hyena_bias": (1, 2, DH), "q_a_norm": (1, QL), "w_uq": (1, QL, NH * QH), "kv_a_norm": (1, KVL),
    "w_ukv": (1, KVL, NH * (ND + VH)), "q_norm": (1, QH), "k_norm": (1, QH), "out_norm": (1, D), "w_out": (1, D, D),
    "mlp_norm": (1, D), "w_router": (1, D, E_N), "w_gate": (1, E_N, D, FE), "w_up": (1, E_N, D, FE),
    "w_down": (1, E_N, FE, D),
}
COLUMNS = {"attn_norm": P, "q_a_norm": P, "kv_a_norm": P, "out_norm": P, "filt_b1": FH, "filt_b2": FH, "filt_freq": FH}


def lay_out(name, a):
    a = np.ascontiguousarray(a)
    return np.ascontiguousarray(a.reshape(-1, COLUMNS[name]).T) if name in COLUMNS else a


def laid_shape(name):
    n = INPUTS[name][-1]
    return (COLUMNS[name], n // COLUMNS[name]) if name in COLUMNS else INPUTS[name]


SCRATCH = {
    "H": (FH, T),
    "Z": (T, CH),
    "C": (T, CM),
    "QK": (2 * NH, QH, T),
    "V": (T, NH, VH),
    "S": (P, 1),
    "YA": (T, DH), "YH": (T, DH),
    "F": (2 * T, 3 * DH),
    "G": (2 * T, DH),
    "XN": (T, D),
    "LG": (E_N, T),
}
PHASES = ["project", "latent", "attend", "hyena", "merge", "moe"]


def build(nc, io, phases=PHASES):
    makers = {"project": project, "latent": latent, "attend": attend, "hyena": hyena,
              "merge": merge, "moe": moe}
    TAKEN.clear()
    for name in phases:
        makers[name](nc, io)
        if name == "attend":
            clear_semaphores(nc)


def kernel(**inputs):
    import concourse.bacc as bacc
    from concourse.bass_utils import run_bass_kernel_spmd

    nc = bacc.Bacc("TRN2", target_bir_lowering=False, num_devices=1)
    arrays = {"in_" + name: lay_out(name, inputs[name]) for name in INPUTS}
    io = {name: nc.dram_tensor("in_" + name, laid_shape(name), F32, kind="ExternalInput").ap() for name in INPUTS}
    for name, a in tables().items():
        arrays[name] = a
        io[name] = nc.dram_tensor(name, a.shape, F32, kind="ExternalInput").ap()
    for name, shape in SCRATCH.items():
        io[name] = nc.dram_tensor("s_" + name, shape, F32, kind="Internal").ap()
    for name, L in (("y_prompt", GROUPS[0]), ("y_sample", GROUPS[1])):
        io[name] = nc.dram_tensor(name, (1, L, D), F32, kind="ExternalOutput").ap()
    build(nc, io)
    r = run_bass_kernel_spmd(nc, [arrays], core_ids=[0])
    return r.results[0]["y_prompt"], r.results[0]["y_sample"]
```
